# Optimizing a Trainium2 kernel written in Bass

```python
import math
import jax, jax.numpy as jnp
from jax import lax
import numpy as np
import math, functools

D_MODEL = 1024
BATCH = 1
SEQ = 256
DEPTH = 2

HEAD_DIM = 64
D_MIX = D_MODEL
RWKV_HEADS = (3 * D_MIX) // (8 * HEAD_DIM)
D_RWKV = RWKV_HEADS * HEAD_DIM
ATTN_HEADS = (3 * D_MIX) // (8 * HEAD_DIM)
D_ATTN = ATTN_HEADS * HEAD_DIM
D_CONV = D_MIX - D_RWKV - D_ATTN
DECAY_LORA = 32
ICLR_LORA = 32
GATE_LORA = 64
CONV_WIDTH = 31
DILATED_PATTERNS = ((128, 1), (512, 4), (2048, 16))
ATTN_BLOCK = 128
D_FF = 2816
NORM_EPS = 1e-6
RWKV_GN_EPS = 64e-5
CONV_LN_EPS = 1e-5
D_SHIFT = 3 * D_RWKV + DECAY_LORA + ICLR_LORA + GATE_LORA
D_IN = D_SHIFT + 3 * D_ATTN + 2 * D_CONV


def _alibi_slopes(n):
    def pow2(m):
        start = 2.0 ** (-8.0 / m)
        return [start ** (i + 1) for i in range(m)]
    if math.log2(n).is_integer():
        return pow2(n)
    c = 2 ** int(math.floor(math.log2(n)))
    return pow2(c) + pow2(2 * c)[0::2][: n - c]

def _rms_norm(x, g):
    xf = x.astype(jnp.float32)
    y = xf * lax.rsqrt(jnp.mean(xf * xf, axis=-1, keepdims=True) + NORM_EPS)
    return y.astype(x.dtype) * g

def _head_rms(t, g):
    return t * lax.rsqrt(jnp.mean(t * t, axis=-1, keepdims=True) + NORM_EPS) * g.astype(jnp.float32)

def _swiglu(x, w_gate, w_up, w_down):
    return (jax.nn.silu(x @ w_gate) * (x @ w_up)) @ w_down

def _token_shift(p, mu):
    prev = jnp.pad(p, ((0, 0), (1, 0), (0, 0)))[:, :-1]
    return p + (prev - p) * mu.astype(p.dtype)

def _rwkv7_scan(r, w, k, v, kk, a):
    B, S, H, N = r.shape
    xs = tuple(jnp.moveaxis(t, 1, 0) for t in (r, w, k, v, -kk, kk * a))

    def step(state, inp):
        r_t, w_t, k_t, v_t, a_t, b_t = inp
        sa = jnp.einsum('bhij,bhj->bhi', state, a_t)
        state = (state * w_t[:, :, None, :]
                 + sa[..., None] * b_t[:, :, None, :]
                 + v_t[..., None] * k_t[:, :, None, :])
        y_t = jnp.einsum('bhij,bhj->bhi', state, r_t)
        return state, y_t

    state0 = jnp.zeros((B, H, N, N), jnp.float32)
    _, y = lax.scan(step, state0, xs)
    return jnp.moveaxis(y, 0, 1)

def _rwkv7_mixer(p, w0, w2, a0, a2, g2, k_k, k_a, r_k, ln_w, ln_b):
    B, S, _ = p.shape
    o = 0
    r = p[..., o:o + D_RWKV]; o += D_RWKV
    k = p[..., o:o + D_RWKV]; o += D_RWKV
    v = p[..., o:o + D_RWKV]; o += D_RWKV
    xw = p[..., o:o + DECAY_LORA]; o += DECAY_LORA
    xa = p[..., o:o + ICLR_LORA]; o += ICLR_LORA
    xg = p[..., o:o + GATE_LORA]
    f32 = jnp.float32
    w_log = -jax.nn.softplus(-(w0.astype(f32) + jnp.tanh(xw) @ w2.astype(f32))) - 0.5
    decay = jnp.exp(-jnp.exp(w_log))
    a = jax.nn.sigmoid(a0.astype(f32) + xa @ a2.astype(f32))
    g = jax.nn.sigmoid(xg) @ g2.astype(f32)
    heads = lambda t: t.reshape(B, S, RWKV_HEADS, HEAD_DIM)
    kk = heads(k * k_k.astype(f32))
    kk = kk * lax.rsqrt(jnp.sum(kk * kk, axis=-1, keepdims=True) + 1e-12)
    k = k * (1.0 + (a - 1.0) * k_a.astype(f32))
    rh, kh, vh = heads(r), heads(k), heads(v)
    y = _rwkv7_scan(rh, heads(decay), kh, vh, kk, heads(a))
    mu = jnp.mean(y, axis=-1, keepdims=True)
    var = jnp.mean(jnp.square(y - mu), axis=-1, keepdims=True)
    y = ((y - mu) * lax.rsqrt(var + RWKV_GN_EPS)).reshape(B, S, D_RWKV)
    y = y * ln_w.astype(f32) + ln_b.astype(f32)
    bonus = jnp.sum(rh * kh * r_k.astype(f32), axis=-1, keepdims=True) * vh
    return (y + bonus.reshape(B, S, D_RWKV)) * g

def _dilated_attention(q, k, v, slopes, window, dilation):
    B, S, H, N = q.shape
    n_keys = window // dilation
    L = S // dilation
    nb = -(-L // ATTN_BLOCK)
    Lp = nb * ATTN_BLOCK

    def blocks(t):
        t = t.reshape(B, L, dilation, H, N)
        t = jnp.pad(t, ((0, 0), (0, Lp - L), (0, 0), (0, 0), (0, 0)))
        return t.reshape(B, nb, ATTN_BLOCK, dilation, H, N)

    def band(t):
        prev = jnp.pad(t, ((0, 0), (1, 0), (0, 0), (0, 0), (0, 0), (0, 0)))[:, :-1]
        return jnp.concatenate([prev, t], axis=2)

    qb = blocks(q)
    kb = band(blocks(k))
    vb = band(blocks(v))
    s = jnp.einsum('bnqchd,bnkchd->bnqchk', qb, kb)
    qi = jnp.arange(ATTN_BLOCK)
    ki = jnp.arange(2 * ATTN_BLOCK)
    dist = qi[:, None] + ATTN_BLOCK - ki[None, :]
    key_idx = jnp.arange(nb)[:, None] * ATTN_BLOCK + ki[None, :] - ATTN_BLOCK
    valid = ((dist >= 0) & (dist <= n_keys))[None] & (key_idx >= 0)[:, None, :]
    bias = -slopes[:, None] * (dist * dilation).astype(jnp.float32)[:, None, None, :]
    s = jnp.where(valid[None, :, :, None, None, :], s + bias, -jnp.inf)
    lse = jax.nn.logsumexp(s, axis=-1)
    p = jnp.exp(s - lse[..., None])
    o = jnp.einsum('bnqchk,bnkchd->bnqchd', p, vb)
    o = o.reshape(B, Lp, dilation, H, N)[:, :L].reshape(B, S, H, N)
    lse = lse.reshape(B, Lp, dilation, H)[:, :L].reshape(B, S, H)
    return o, lse

def _attention_mixer(qkv, q_norm, k_norm):
    B, S, _ = qkv.shape
    q = qkv[..., :D_ATTN].reshape(B, S, ATTN_HEADS, HEAD_DIM)
    k = qkv[..., D_ATTN:2 * D_ATTN].reshape(B, S, ATTN_HEADS, HEAD_DIM)
    v = qkv[..., 2 * D_ATTN:].reshape(B, S, ATTN_HEADS, HEAD_DIM)
    q = _head_rms(q, q_norm) * (HEAD_DIM ** -0.5)
    k = _head_rms(k, k_norm)
    slopes = jnp.asarray(_alibi_slopes(ATTN_HEADS), jnp.float32)
    res = [_dilated_attention(q, k, v, slopes, w, d) for (w, d) in DILATED_PATTERNS]
    outs = jnp.stack([r_[0] for r_ in res], axis=0)
    lses = jnp.stack([r_[1] for r_ in res], axis=0)
    alpha = jax.nn.softmax(lses, axis=0)
    out = jnp.sum(alpha[..., None] * outs, axis=0)
    return out.reshape(B, S, D_ATTN)

def _conv_mixer(u, dw_w, dw_b, ln_w, ln_b):
    f32 = jnp.float32
    z = u[..., :D_CONV] * jax.nn.sigmoid(u[..., D_CONV:])
    z = lax.conv_general_dilated(z, dw_w.astype(f32)[:, None, :], window_strides=(1,),
                                 padding=[(CONV_WIDTH - 1, 0)],
                                 dimension_numbers=('NWC', 'WIO', 'NWC'),
                                 feature_group_count=D_CONV) + dw_b.astype(f32)
    mu = jnp.mean(z, axis=-1, keepdims=True)
    var = jnp.mean(jnp.square(z - mu), axis=-1, keepdims=True)
    z = (z - mu) * lax.rsqrt(var + CONV_LN_EPS) * ln_w.astype(f32) + ln_b.astype(f32)
    return jax.nn.silu(z)

def first_inputs(seed: int = 0) -> dict:
    key = jax.random.key(seed)
    ks = iter(jax.random.split(key, 40))
    f32 = jnp.float32
    L = DEPTH

    def normal(shape, scale):
        return jax.random.normal(next(ks), shape, f32) * scale

    def gain(shape):
        return 1.0 + 0.05 * jax.random.normal(next(ks), shape, f32)

    def unif(shape, lo, hi):
        return jax.random.uniform(next(ks), shape, f32, lo, hi)

    return {
        'x': normal((BATCH, SEQ, D_MODEL), 1.0),
        'norm_ffn1': gain((L, D_MODEL)),
        'ffn1_w_gate': normal((L, D_MODEL, D_FF), D_MODEL ** -0.5),
        'ffn1_w_up': normal((L, D_MODEL, D_FF), D_MODEL ** -0.5),
        'ffn1_w_down': normal((L, D_FF, D_MODEL), D_FF ** -0.5),
        'norm_mix': gain((L, D_MODEL)),
        'w_in': normal((L, D_MODEL, D_IN), D_MODEL ** -0.5),
        'shift_mu': unif((L, D_SHIFT), 0.0, 1.0),
        'rwkv_w0': unif((L, D_RWKV), -6.0, 1.0),
        'rwkv_w2': normal((L, DECAY_LORA, D_RWKV), 0.1),
        'rwkv_a0': normal((L, D_RWKV), 0.5),
        'rwkv_a2': normal((L, ICLR_LORA, D_RWKV), 0.1),
        'rwkv_g2': normal((L, GATE_LORA, D_RWKV), GATE_LORA ** -0.5),
        'rwkv_k_k': 0.85 + normal((L, D_RWKV), 0.05),
        'rwkv_k_a': gain((L, D_RWKV)),
        'rwkv_r_k': 0.5 + normal((L, RWKV_HEADS, HEAD_DIM), 0.1),
        'rwkv_ln_w': gain((L, D_RWKV)),
        'rwkv_ln_b': normal((L, D_RWKV), 0.02),
        'attn_q_norm': gain((L, HEAD_DIM)),
        'attn_k_norm': gain((L, HEAD_DIM)),
        'conv_dw_w': normal((L, CONV_WIDTH, D_CONV), CONV_WIDTH ** -0.5),
        'conv_dw_b': normal((L, D_CONV), 0.02),
        'conv_ln_w': gain((L, D_CONV)),
        'conv_ln_b': normal((L, D_CONV), 0.02),
        'w_out': normal((L, D_MIX, D_MODEL), D_MIX ** -0.5),
        'norm_ffn2': gain((L, D_MODEL)),
        'ffn2_w_gate': normal((L, D_MODEL, D_FF), D_MODEL ** -0.5),
        'ffn2_w_up': normal((L, D_MODEL, D_FF), D_MODEL ** -0.5),
        'ffn2_w_down': normal((L, D_FF, D_MODEL), D_FF ** -0.5),
    }

def first_block(x, norm_ffn1, ffn1_w_gate, ffn1_w_up, ffn1_w_down, norm_mix, w_in, shift_mu,
              rwkv_w0, rwkv_w2, rwkv_a0, rwkv_a2, rwkv_g2, rwkv_k_k, rwkv_k_a, rwkv_r_k,
              rwkv_ln_w, rwkv_ln_b, attn_q_norm, attn_k_norm, conv_dw_w, conv_dw_b,
              conv_ln_w, conv_ln_b, w_out, norm_ffn2, ffn2_w_gate, ffn2_w_up, ffn2_w_down):
    for l in range(DEPTH):
        x = x + 0.5 * _swiglu(_rms_norm(x, norm_ffn1[l]), ffn1_w_gate[l], ffn1_w_up[l], ffn1_w_down[l])
        h = _rms_norm(x, norm_mix[l])
        proj = (h @ w_in[l]).astype(jnp.float32)
        p_rwkv = _token_shift(proj[..., :D_SHIFT], shift_mu[l])
        y_rwkv = _rwkv7_mixer(p_rwkv, rwkv_w0[l], rwkv_w2[l], rwkv_a0[l], rwkv_a2[l], rwkv_g2[l],
                              rwkv_k_k[l], rwkv_k_a[l], rwkv_r_k[l], rwkv_ln_w[l], rwkv_ln_b[l])
        y_attn = _attention_mixer(proj[..., D_SHIFT:D_SHIFT + 3 * D_ATTN], attn_q_norm[l], attn_k_norm[l])
        y_conv = _conv_mixer(proj[..., D_SHIFT + 3 * D_ATTN:], conv_dw_w[l], conv_dw_b[l],
                             conv_ln_w[l], conv_ln_b[l])
        mix = jnp.concatenate([y_rwkv, y_attn, y_conv], axis=-1).astype(x.dtype)
        x = x + mix @ w_out[l]
        x = x + 0.5 * _swiglu(_rms_norm(x, norm_ffn2[l]), ffn2_w_gate[l], ffn2_w_up[l], ffn2_w_down[l])
    return x


DEPTH_2 = 1

D_MIX_2 = D_MODEL
ATTN_WIDTH = D_MIX_2 // 2
CONV_WIDTH_2 = D_MIX_2 // 4
POOL_WIDTH = D_MIX_2 - ATTN_WIDTH - CONV_WIDTH_2
N_ATTN_HEADS = ATTN_WIDTH // HEAD_DIM
POOL_WINDOWS = (2, 4, 8, 16)
N_POOL_GROUPS = len(POOL_WINDOWS)
POOL_GROUP = POOL_WIDTH // N_POOL_GROUPS
CONV_K = 3
MOBA_BLOCK = 256
MOBA_TOP_K = 3
NUM_BUCKETS = 32
MAX_DISTANCE = 1024
D_FF_2 = ((8 * D_MODEL // 3 + 255) // 256) * 256
IN_COLS = 3 * ATTN_WIDTH + 3 * CONV_WIDTH_2 + POOL_WIDTH
DEEPNORM_ALPHA = (2.0 * DEPTH_2) ** 0.25
DEEPNORM_BETA = (8.0 * DEPTH_2) ** -0.25
LN_EPS = 1e-5
NEG_INF = -1e30


def layer_norm(x, g, b):
    xf = x.astype(jnp.float32)
    mu = xf.mean(-1, keepdims=True)
    var = jnp.square(xf - mu).mean(-1, keepdims=True)
    return ((xf - mu) * lax.rsqrt(var + LN_EPS)).astype(x.dtype) * g + b

def causal_dwconv(x, w):
    S = x.shape[1]
    xp = jnp.pad(x, ((0, 0), (CONV_K - 1, 0), (0, 0)))
    return sum(xp[:, j:j + S] * w[j] for j in range(CONV_K))

def t5_bucket(dist):
    n = jnp.maximum(dist, 0)
    max_exact = NUM_BUCKETS // 2
    nf = jnp.maximum(n, 1).astype(jnp.float32)
    large = max_exact + (jnp.log(nf / max_exact) / math.log(MAX_DISTANCE / max_exact)
                         * (NUM_BUCKETS - max_exact)).astype(jnp.int32)
    large = jnp.minimum(large, NUM_BUCKETS - 1)
    return jnp.where(n < max_exact, n, large)

def _moba_query_block(i, n_sel, args):
    qh, selh, kh, vh, tab = args
    L = MOBA_BLOCK
    scale = HEAD_DIM ** -0.5
    r = jnp.arange(L)
    rel = r[:, None] - r[None, :]
    own_logits = (jnp.einsum('qd,ld->ql', qh, kh[i]).astype(jnp.float32) * scale
                  + tab[t5_bucket(rel)].astype(jnp.float32))
    own_logits = jnp.where(rel >= 0, own_logits, NEG_INF)
    if n_sel == 0:
        p = jax.nn.softmax(own_logits, axis=-1).astype(vh.dtype)
        return jnp.einsum('ql,ld->qd', p, vh[i])
    k_sel = kh[selh]
    v_sel = vh[selh]
    dist = (i - selh)[:, :, None] * L + rel[:, None, :]
    sel_logits = (jnp.einsum('qd,qnld->qnl', qh, k_sel).astype(jnp.float32) * scale
                  + tab[t5_bucket(dist)].astype(jnp.float32))
    logits = jnp.concatenate([sel_logits.reshape(L, n_sel * L), own_logits], axis=-1)
    p = jax.nn.softmax(logits, axis=-1).astype(vh.dtype)
    p_sel = p[:, :n_sel * L].reshape(L, n_sel, L)
    p_own = p[:, n_sel * L:]
    return jnp.einsum('qnl,qnld->qd', p_sel, v_sel) + jnp.einsum('ql,ld->qd', p_own, vh[i])

def moba_attention(q, k, v, rel_bias):
    B, H, S, Dh = q.shape
    L = MOBA_BLOCK
    nb = -(-S // L)
    pad = nb * L - S
    if pad:
        cfg = ((0, 0), (0, 0), (0, pad), (0, 0))
        q, k, v = jnp.pad(q, cfg), jnp.pad(k, cfg), jnp.pad(v, cfg)
    qb = q.reshape(B, H, nb, L, Dh)
    kb = k.reshape(B, H, nb, L, Dh)
    vb = v.reshape(B, H, nb, L, Dh)
    k_mean = kb.astype(jnp.float32).mean(axis=3).astype(k.dtype)
    k_flat = kb.reshape(B * H, nb, L, Dh)
    v_flat = vb.reshape(B * H, nb, L, Dh)
    tab = jnp.broadcast_to(rel_bias[None], (B,) + rel_bias.shape).reshape(B * H, NUM_BUCKETS)
    outs = []
    for i in range(nb):
        q_i = qb[:, :, i]
        n_sel = min(MOBA_TOP_K, i)
        if n_sel:
            gate = jnp.einsum('bhqd,bhnd->bhqn', q_i, k_mean[:, :, :i]).astype(jnp.float32)
            _, sel = lax.top_k(gate, n_sel)
            sel = sel.reshape(B * H, L, n_sel)
        else:
            sel = jnp.zeros((B * H, L, 0), jnp.int32)
        step = functools.partial(_moba_query_block, i, n_sel)
        outs.append(lax.map(step, (q_i.reshape(B * H, L, Dh), sel, k_flat, v_flat, tab)))
    out = jnp.concatenate(outs, axis=1).reshape(B, H, nb * L, Dh)
    return out[:, :, :S]

def pool_mixer(p, w_pool, pool_scale):
    B, S, _ = p.shape
    pg = p.reshape(B, S, N_POOL_GROUPS, POOL_GROUP)
    pf = pg.astype(jnp.float32)
    c = jnp.cumsum(pf, axis=1)
    pos = jnp.arange(1, S + 1, dtype=jnp.float32)
    means = []
    for g, w in enumerate(POOL_WINDOWS):
        cg = c[:, :, g]
        lag = jnp.pad(cg, ((0, 0), (w, 0), (0, 0)))[:, :S]
        means.append((cg - lag) / jnp.minimum(pos, float(w))[None, :, None])
    pooled = (jnp.stack(means, axis=2) - pf).astype(p.dtype)
    y = jnp.einsum('bsgc,gcd->bsgd', pooled, w_pool)
    return y.reshape(B, S, POOL_WIDTH) * pool_scale

def to_heads(t):
    B, S, _ = t.shape
    return t.reshape(B, S, -1, HEAD_DIM).transpose(0, 2, 1, 3)

def hybrid_layer(x, w_in, conv_w, w_pool, pool_scale, w_out, ln1_g, ln1_b,
                 w_up, ffn_conv_w, ffn_conv_b, w_down, ln2_g, ln2_b, rel_bias):
    B, S, _ = x.shape
    h = x @ w_in
    sizes = [ATTN_WIDTH, ATTN_WIDTH, ATTN_WIDTH, CONV_WIDTH_2, CONV_WIDTH_2, CONV_WIDTH_2]
    q, k, v, cb, cc, cx, pin = jnp.split(h, list(np.cumsum(sizes)), axis=-1)
    attn = moba_attention(to_heads(q), to_heads(k), to_heads(v), rel_bias)
    attn = attn.transpose(0, 2, 1, 3).reshape(B, S, ATTN_WIDTH)
    conv = cb * causal_dwconv(cc * cx, conv_w)
    pool = pool_mixer(pin, w_pool, pool_scale)
    mix = jnp.concatenate([attn, conv, pool], axis=-1) @ w_out
    x = layer_norm(DEEPNORM_ALPHA * x + mix, ln1_g, ln1_b)
    up = causal_dwconv(x @ w_up, ffn_conv_w) + ffn_conv_b
    u, g = jnp.split(up, 2, axis=-1)
    ff = (u * jax.nn.silu(g)) @ w_down
    return layer_norm(DEEPNORM_ALPHA * x + ff, ln2_g, ln2_b)

def second_inputs(seed: int = 0) -> dict:
    key = jax.random.key(seed)
    ks = jax.random.split(key, 16)
    nrm = jax.random.normal
    return {
        'x': nrm(ks[0], (BATCH, SEQ, D_MODEL), jnp.float32),
        'w_in': nrm(ks[1], (DEPTH_2, D_MODEL, IN_COLS), jnp.float32) * D_MODEL ** -0.5,
        'conv_w': nrm(ks[2], (DEPTH_2, CONV_K, CONV_WIDTH_2), jnp.float32) * CONV_K ** -0.5,
        'w_pool': nrm(ks[3], (DEPTH_2, N_POOL_GROUPS, POOL_GROUP, POOL_GROUP), jnp.float32) * POOL_GROUP ** -0.5,
        'pool_scale': 1.0 + 0.02 * nrm(ks[4], (DEPTH_2, POOL_WIDTH), jnp.float32),
        'w_out': nrm(ks[5], (DEPTH_2, D_MIX_2, D_MODEL), jnp.float32) * (D_MIX_2 ** -0.5 * DEEPNORM_BETA),
        'ln1_g': 1.0 + 0.02 * nrm(ks[6], (DEPTH_2, D_MODEL), jnp.float32),
        'ln1_b': 0.02 * nrm(ks[7], (DEPTH_2, D_MODEL), jnp.float32),
        'w_up': nrm(ks[8], (DEPTH_2, D_MODEL, 2 * D_FF_2), jnp.float32) * D_MODEL ** -0.5,
        'ffn_conv_w': nrm(ks[9], (DEPTH_2, CONV_K, 2 * D_FF_2), jnp.float32) * CONV_K ** -0.5,
        'ffn_conv_b': 0.02 * nrm(ks[10], (DEPTH_2, 2 * D_FF_2), jnp.float32),
        'w_down': nrm(ks[11], (DEPTH_2, D_FF_2, D_MODEL), jnp.float32) * (D_FF_2 ** -0.5 * DEEPNORM_BETA),
        'ln2_g': 1.0 + 0.02 * nrm(ks[12], (DEPTH_2, D_MODEL), jnp.float32),
        'ln2_b': 0.02 * nrm(ks[13], (DEPTH_2, D_MODEL), jnp.float32),
        'rel_bias': 0.5 * nrm(ks[14], (N_ATTN_HEADS, NUM_BUCKETS), jnp.float32),
    }

def second_block(x, w_in, conv_w, w_pool, pool_scale, w_out, ln1_g, ln1_b,
              w_up, ffn_conv_w, ffn_conv_b, w_down, ln2_g, ln2_b, rel_bias):
    for l in range(DEPTH_2):
        x = hybrid_layer(x, w_in[l], conv_w[l], w_pool[l], pool_scale[l], w_out[l],
                         ln1_g[l], ln1_b[l], w_up[l], ffn_conv_w[l], ffn_conv_b[l],
                         w_down[l], ln2_g[l], ln2_b[l], rel_bias)
    return x


_first_inputs = second_inputs


def second_inputs(seed=0):
    import zlib

    import numpy as np

    out = dict(_first_inputs(seed))
    spreads = {}
    factors = {'pool_scale': 8.0, 'ln1_b': 2.784, 'ffn_conv_b': 7.017, 'ln2_g': 2.89, 'ln2_b': 2.747}
    for name, (base, spread) in spreads.items():
        noise = np.random.default_rng([zlib.crc32(name.encode()), seed]).standard_normal(out[name].shape)
        drawn = base * np.exp(spread * noise) if base else spread * noise
        out[name] = __import__('jax').numpy.asarray(drawn.astype(out[name].dtype))
    for name, factor in factors.items():
        out[name] = (out[name] * factor).astype(out[name].dtype)
    return out


_narrow_inputs = second_inputs


def second_inputs(seed=0):

    out = dict(_narrow_inputs(seed))
    wider = {'pool_scale': 3.68, 'ln2_g': 3.24, 'ln2_b': 3.25, 'rel_bias': 4.28}
    for name, times in wider.items():
        mean = out[name].mean()
        out[name] = (mean + times * (out[name] - mean)).astype(out[name].dtype)
    return out


def setup_inputs(seed=0):
    out = dict(first_inputs(seed))
    for name, value in second_inputs(seed + 1).items():
        if name != "x":
            out[name + "_2"] = value
    return out


def reference(
    x, norm_ffn1, ffn1_w_gate, ffn1_w_up, ffn1_w_down, norm_mix, w_in, shift_mu, rwkv_w0,
    rwkv_w2, rwkv_a0, rwkv_a2, rwkv_g2, rwkv_k_k, rwkv_k_a, rwkv_r_k, rwkv_ln_w, rwkv_ln_b,
    attn_q_norm, attn_k_norm, conv_dw_w, conv_dw_b, conv_ln_w, conv_ln_b, w_out, norm_ffn2,
    ffn2_w_gate, ffn2_w_up, ffn2_w_down, w_in_2, conv_w_2, w_pool_2, pool_scale_2, w_out_2,
    ln1_g_2, ln1_b_2, w_up_2, ffn_conv_w_2, ffn_conv_b_2, w_down_2, ln2_g_2, ln2_b_2,
    rel_bias_2,
):
    x = first_block(
        x, norm_ffn1, ffn1_w_gate, ffn1_w_up, ffn1_w_down, norm_mix, w_in, shift_mu, rwkv_w0,
        rwkv_w2, rwkv_a0, rwkv_a2, rwkv_g2, rwkv_k_k, rwkv_k_a, rwkv_r_k, rwkv_ln_w, rwkv_ln_b,
        attn_q_norm, attn_k_norm, conv_dw_w, conv_dw_b, conv_ln_w, conv_ln_b, w_out, norm_ffn2,
        ffn2_w_gate, ffn2_w_up, ffn2_w_down,
    )
    return second_block(
        x, w_in_2, conv_w_2, w_pool_2, pool_scale_2, w_out_2, ln1_g_2, ln1_b_2, w_up_2,
        ffn_conv_w_2, ffn_conv_b_2, w_down_2, ln2_g_2, ln2_b_2, rel_bias_2,
    )


_drawn_inputs = setup_inputs


def setup_inputs(seed=0):
    import zlib

    import numpy as np

    out = dict(_drawn_inputs(seed))
    spreads = {}
    factors = {'rwkv_w2': 4.036,
     'rwkv_k_k': 3.358,
     'rwkv_ln_b': 7.518,
     'attn_q_norm': 5.203,
     'attn_k_norm': 5.025,
     'conv_dw_b': 3.351,
     'conv_ln_b': 7.426,
     'ln1_g_2': 2.835}
    for name, (base, spread) in spreads.items():
        noise = np.random.default_rng([zlib.crc32(name.encode()), seed]).standard_normal(out[name].shape)
        drawn = base * np.exp(spread * noise) if base else spread * noise
        out[name] = __import__('jax').numpy.asarray(drawn.astype(out[name].dtype))
    for name, factor in factors.items():
        out[name] = (out[name] * factor).astype(out[name].dtype)
    return out
```

```python
from contextlib import ExitStack

import numpy as np

import concourse.bass as bass
from concourse import mybir

F32 = mybir.dt.float32
ALU = mybir.AluOpType
ACT = mybir.ActivationFunctionType
AX = mybir.AxisListType.X

P = 128
SEQ, D, DEPTH = 256, 1024, 2
NT = SEQ // P
KC = D // P
DFF = 2816
DIN = 2944
NCH = DIN // P
DIN2 = 2560
CONV_W = 31
CHUNK = 64
NH1, NH2 = 6, 8
NORM_EPS, GN_EPS, LN_EPS = 1e-6, 64e-5, 1e-5
ALPHA = 2.0 ** 0.25
NEG = -1e30
WORK = 22900
GROUPS = DFF // 256
LOOPS = (GROUPS - 3) // 2
SLOTS = ["gate0", "up0", "down0", "gate1", "up1", "down1"]
assert GROUPS == 11 and NCH == 23 and DEPTH == 2

R, K, V, LORA, AQ, AK, AV, CU, CG = 0, 3, 6, 9, 10, 13, 16, 19, 21
Q2, K2, V2, CB2, CC2, CX2, PI2 = 0, 4, 8, 12, 14, 16, 18


def param_rows():
    rows, at = {}, 0
    for name, n in (("norm_ffn1", 8), ("norm_mix", 8), ("norm_ffn2", 8), ("shift_mu", 10), ("rwkv_w0", 3),
                    ("rwkv_a0", 3), ("rwkv_k_k", 3), ("rwkv_k_a", 3), ("rwkv_r_k", 3), ("rwkv_ln_w", 3),
                    ("rwkv_ln_b", 3), ("conv_dw_w", 2 * CONV_W), ("conv_dw_b", 2), ("conv_ln_w", 2),
                    ("conv_ln_b", 2), ("attn_q_norm", 1), ("attn_k_norm", 1)):
        rows[name] = at
        at += n
    return rows, at


ROWS, NROWS = param_rows()
B_TAP2, B_BIAS, B_CONV, B_POOL, B_ROWS = 0, 44, 88, 94, 96


def constants():
    s = np.arange(P)[:, None]
    t = np.arange(P)[None, :]
    same = lambda n: (s // n == t // n)
    f = lambda m: m.astype(np.float32)
    strict, incl = f((s < t) & same(CHUNK)), f((s <= t) & same(CHUNK))
    parts = {
        "ident": np.eye(P, dtype=np.float32),
        "pair": f(same(64)),
        "mask4": np.concatenate([strict, incl, strict, incl], 1),
        "blk16": f(same(16)),
        "blk32": f(same(32) & ~same(16)),
        "blk64": f(same(64) & ~same(32)),
        "ones": np.ones((P, P), np.float32),
        "scan": np.broadcast_to(f(np.arange(SEQ) % CHUNK != 0), (P, SEQ)),
    }
    dist = (P + s) - np.arange(2 * P)[None, :]
    count = sum(((dist >= 0) & (dist % dil == 0) & (dist <= win)).astype(int)
                for win, dil in ((128, 1), (512, 4), (2048, 16)))
    logc = np.where(count > 0, np.log(np.maximum(count, 1)), NEG)
    slopes = [2.0 ** (-2.0 * (i + 1)) for i in range(4)] + [2.0 ** (-1.0 * (i + 1)) for i in range(8)][0::2][:2]
    parts["bias1"] = np.concatenate([np.where(count > 0, -m * dist + logc, NEG) for m in slopes], 1)
    pos = np.arange(1, SEQ + 1)
    parts["poolw"] = np.concatenate(
        [np.concatenate([np.broadcast_to(1.0 / np.minimum(pos, w), (64, SEQ)) for w in pair], 0)
         for pair in ((2, 4), (8, 16))], 1)
    at, cols = 0, {}
    for name, a in parts.items():
        cols[name] = (at, at + a.shape[1])
        at += a.shape[1]
    packed = np.ascontiguousarray(np.concatenate([np.asarray(a, np.float32) for a in parts.values()], 1))
    d = 255 - np.arange(384)
    n = np.maximum(d, 0)
    nf = np.maximum(n, 1).astype(np.float32)
    large = 16 + (np.log(nf / np.float32(16)) / np.float32(np.log(1024 / 16)) * np.float32(16)).astype(np.int32)
    bucket = np.where(n < 16, n, np.minimum(large, 31))
    hot = np.zeros((33, 384), np.float32)
    hot[bucket, np.arange(384)] = (d >= 0)
    hot[32] = np.where(d < 0, NEG, 0.0)
    return packed, cols, hot


def chain_plan():
    steps = [
        [("copy", "D2", "DT", "D"), ("copy", "D2T", "D", "DT")],
        [("add", "INV", "D2", "INV"), ("copy", "D", "D2T", "D2"), ("copy", "DT", "D2", "D2T")],
        [("add", "INV", "D", "INV"), ("copy", "D2", "DT", "D")],
        [("add", "INV", "D2", "INV"), ("add", "D", "AT", None)],
        [("copy", "D2T", "INV", None), ("copy", "DT", "D", "INV")],
        [("add", "INV", "D2T", "DT"), ("add", "D2", "AT", None)],
        [("copy", "D2T", "INV", None), ("copy", "DT", "D2", "INV")],
        [("add", "INV", "D2T", "DT")],
    ]
    plan, n = [], {"copy": 0, "add": 0}
    last = {}
    for step, products in enumerate(steps):
        for b in range(3):
            written = []
            for kind, dst, lhs, rhs in products:
                needs = [last.get((x, b)) for x in (lhs, rhs) if x]
                plan.append((step, b, kind, n[kind], dst, lhs, rhs, [x for x in needs if x], last.get((dst, b))))
                written.append(((dst, b), (kind, n[kind])))
                n[kind] += 1
            last.update(written)
    return plan


CHAIN = chain_plan()
COPIES, ADDS = (sum(c[2] == k for c in CHAIN) for k in ("copy", "add"))


def build(nc, a, out):
    packed_cols = constants()[1]
    ctx = ExitStack()
    with ctx:
        def sb(name, shape):
            return ctx.enter_context(nc.sbuf_tensor(name, shape, F32))

        loaded = {n: ctx.enter_context(nc.semaphore(f"loaded_{n}")) for n in SLOTS}
        used = {n: ctx.enter_context(nc.semaphore(f"used_{n}")) for n in SLOTS}
        arrived = ctx.enter_context(nc.semaphore("arrived"))
        cleared = ctx.enter_context(nc.semaphore("cleared"))
        consts_in = ctx.enter_context(nc.semaphore("consts_in"))
        x_in = ctx.enter_context(nc.semaphore("x_in"))
        rows_in = ctx.enter_context(nc.semaphore("rows_in"))
        second_in = ctx.enter_context(nc.semaphore("second_in"))
        setup_done = ctx.enter_context(nc.semaphore("setup_done"))
        spread_out = ctx.enter_context(nc.semaphore("spread_out"))
        bias_in = ctx.enter_context(nc.semaphore("bias_in"))
        over = ctx.enter_context(nc.semaphore("over"))
        resumed = ctx.enter_context(nc.semaphore("resumed"))
        slot_free = ctx.enter_context(nc.semaphore("slot_free"))
        stored = ctx.enter_context(nc.semaphore("stored"))

        names = """rows_picked params_psum params_ready squares_done rms_root normed transposed_a transposed_d
            h_ready_a h_ready_d silu_done ff_ready x_updated x_rounds  proj_ready dve_link
            act_link pool_link shifted lora_acts lora_mm decay_sig iclr_sig gate_copied cum_ready exps_done
            kk_sq kk_sum kk_root rw_ready bonus_sq bonus_mm bonus_ready tok_mm tok_copied_a tok_copied_d
            mats_mm mats_ready a_mm d_ready dt_ready inv_seed copy_mm add_mm copy_done add_done
            pav_mm pav_done mat_mm mat_done sa_mm sa_done st_mm st_done cend_ready y_mm y_copied
            gn_mean gn_centered gn_sq gn_var gn_root mixr_ready
            qk_sq qk_sum qk_root qk_ready score_mm biased maxed exp_done p_ready pt_mm pt_done av_mm mixa_ready
            conv_sig conv_z conv_acc cl_mean cl_sq cl_var cl_root cl_ready mixc_ready
            biasrow_mm spread_ready pool_ready pool_mm taps_act taps_picked lag_done taps_done stats_ready""".split()
        S = {n: ctx.enter_context(nc.semaphore(n)) for n in names}
        layer_sems = range(S[names[0]].num, S[names[-1]].num + 1)
        assert [S[n].num for n in names] == list(layer_sems)

        slot = {n: sb(f"w_{n}", [P, 2048]) for n in SLOTS}
        x = sb("x", [P, NT, D])
        hT = sb("hT", [P, KC, SEQ])
        proj = sb("proj", [P, NCH, SEQ + 1])
        mix = sb("mix", [P, KC, SEQ])
        cst = sb("cst", [P, list(packed_cols.values())[-1][1]])
        rows = sb("rows", [P, DEPTH, P])
        row_now = sb("row_now", [P, P])
        par = sb("par", [P, P])
        lora_all = sb("lora_all", [P, DEPTH, 384])
        lora_w = sb("lora_w", [P, 384])
        small = sb("small", [P, 96])
        hot = sb("hot", [33, 384])
        work = sb("work", [P, WORK])
        psum = [ctx.enter_context(nc.psum_tensor(f"bank{i}", [P, 512], F32)) for i in range(8)]

        def area(at, *shape):
            n = int(np.prod(shape))
            v = work[:, at:at + n]
            if len(shape) == 2:
                v = v.rearrange("p (a b) -> p a b", a=shape[0])
            if len(shape) == 3:
                v = v.rearrange("p (a b c) -> p a b c", a=shape[0], b=shape[1])
            if len(shape) == 4:
                v = v.rearrange("p (a b c d) -> p a b c d", a=shape[0], b=shape[1], c=shape[2])
            return v, at + n

        def const(name, parts=slice(0, P)):
            lo, hi = packed_cols[name]
            return cst[parts, lo:hi]

        ident, pairs, ones = const("ident"), const("pair"), const("ones")
        hN, _ = area(0, NT, D)
        silu, o = area(0, 2, 512)
        ffT, o = area(o, 2, 512)
        taps, o = area(o, 2, 2, 512)
        sh, o = area(0, 10, SEQ)
        ar, o = area(o, 3, NT, 2, P)
        bh, o = area(o, 3, SEQ)
        kh, o = area(o, 3, SEQ)
        ec, o = area(o, 3, SEQ)
        gate, o = area(o, 3, SEQ)
        bonus, o = area(o, 3, SEQ)
        tok, o = area(o, 4, NT, 384)
        avtok, o = area(o, NT, 512)
        o_mats = o
        mats, o = area(o, 12, 4, P)
        o_chain = o
        chain = {"D": hT[:, 0:6, :].rearrange("p a b -> p (a b)").rearrange("p (a b) -> p a b", a=12),
                 "DT": area(0, 12, P)[0]}
        for n in ("D2", "D2T", "INV"):
            chain[n], o = area(o, 12, P)
        assert o <= WORK, o
        o = o_mats
        ld, o = area(o, 3, SEQ)
        cum, o = area(o, 3, SEQ)
        ecx, o = area(o, 3, SEQ)
        en, o = area(o, 3, SEQ)
        iclr, o = area(o, 3, SEQ)
        kk, o = area(o, 3, SEQ)
        kmod, o = area(o, 3, SEQ)
        tmp, o = area(o, 3, SEQ)
        lact, o = area(o, SEQ)
        qsq, o = area(o, 6, SEQ)
        logit, o = area(o, 2, 384)
        probT, o = area(o, 2, 384)
        assert o <= WORK, o
        o = o_chain
        pav, o = area(o, NT, 384)
        mat_, o = area(o, NT, 384)
        satok, o = area(o, NT, 384)
        assert o <= o_chain + 2 * 12 * P
        state, o = area(0, 3, 3, P)
        cend, o = area(o, 3, 3, P)
        ysb = hT[:, 0:3, :]
        ysq, o = area(o_mats, 3, SEQ)
        yroot, o = area(o, 3, SEQ)
        par2, o = area(4096, 4, 44)
        par2c, o = area(o, 8)
        bias2, o = area(o, NH2, 2 * P)
        ln_gb, o = area(o, 2, D)
        spread, o = area(o, NH2, 384)
        rows2, o = area(o, 2, P)
        tab, o = area(o, 64)
        avtok2, o = area(o, NT, 512)
        logit2, o = area(o, 2, 384)
        probT2, o = area(o, 2, 384)
        cz, o = area(o, 2, SEQ)
        pl, o = area(o, 3, 2, SEQ)
        wpool, o = area(o, 2, P)
        tap_now, o = area(o, 2, 4, 2, 2)
        assert o <= WORK, o
        rstd = small[:, 0:8]
        eps = {n: small[:, 8 + i:9 + i] for i, n in enumerate(("norm", "gn", "ln", "kk"))}
        amax, anmax, asum, arec = (small[:, 12 + 16 * i:28 + 16 * i].rearrange("p (h t) -> p h t", t=NT)
                                   for i in range(4))
        lnstat = small[:, 76:88].rearrange("p (a b) -> p a b", a=2)
        lnvar = small[:, 88:92].rearrange("p (a b) -> p a b", a=2)

        block = ctx.enter_context(nc.Block())
        scratch = nc.dram_tensor("bias_scratch", [P, NH2, 384], F32)

        def col(name, i=0):
            c = ROWS[name] + i
            return par[:, c:c + 1]

        class Chain:

            def __init__(self, eng, sem):
                self.eng, self.sem, self.n = eng, sem, 0

            def __call__(self, ins):
                self.n += 1
                ins.then_inc(self.sem, 1)
                self.eng.wait_ge(self.sem, self.n)

        class Uses:

            def __init__(self, layer, per_layer):
                self.base = lambda n: layer * per_layer[n]
                self.n = dict.fromkeys(SLOTS, 0)

            def now(self, name, more=0):
                return self.base(name) + (more + self.n[name] + 1)

            def ffn(self):
                for n in SLOTS:
                    self.n[n] += 6 if n.endswith("0") else 5

            def each(self, names, times=1):
                for n in names:
                    self.n[n] += times

        PER_LAYER = {n: 2 * (6 if n.endswith("0") else 5) + 2 for n in SLOTS}
        for i in range(4):
            PER_LAYER[SLOTS[i]] += 1

        def fill(sp, uses, name, src, more=0):
            n = uses.now(name, more)
            sp.wait_ge(used[name], n)
            sp.sem_inc(slot_free, 1)
            width = src.shape[2]
            dst = slot[name][:, :].rearrange("p (c n) -> p c n", n=width)
            sp.dma_start(dst, src).then_inc(loaded[name], 16)

        def columns(w, l, start, width=256):
            return w[bass.ds(l, 1), :, bass.ds(start, width)].rearrange("a (c p) n -> p (a c) n", p=P)

        def krows(w, l, start):
            return w[bass.ds(l, 1), bass.ds(start, 256), :].rearrange("a (c p) n -> p (a c) n", p=P)

        def sp_ffn(sp, uses, l, wg, g0, wu, u0, wd):
            def gu(g, par_, more=0):
                fill(sp, uses, f"gate{par_}", columns(wg, l, g * 256 + g0), more)
                fill(sp, uses, f"up{par_}", columns(wu, l, g * 256 + u0), more)

            def dn(g, par_, more=0):
                fill(sp, uses, f"down{par_}", krows(wd, l, g * 256), more)

            gu(0, 0)
            gu(1, 1)
            dn(0, 0)
            with sp.Fori(0, LOOPS) as it:
                gu(it * 2 + 2, 0, it + 1)
                dn(it * 2 + 1, 1, it)
                gu(it * 2 + 3, 1, it + 1)
                dn(it * 2 + 2, 0, it + 1)
            gu(10, 0, LOOPS + 1)
            dn(9, 1, LOOPS)
            dn(10, 0, LOOPS + 1)
            uses.ffn()

        def sp_proj(sp, uses, l, w, per, starts):
            with sp.Fori(0, 2) as it:
                for j in range(per):
                    fill(sp, uses, SLOTS[j], columns(w, l, starts(it, j) * P), it)
            uses.each(SLOTS[:per], 2)

        def sp_out(sp, uses, l, w):
            for j in range(4):
                fill(sp, uses, SLOTS[j], krows(w, l, j * 256))
                uses.n[SLOTS[j]] += 1

        def start1(it, j):
            return it * 12 + 2 * j if j < 5 else it * 11 + 10

        def start2(it, j):
            return it * 10 + 2 * j

        def over_groups(eng, body):
            body(0, 0, 0)
            body(1, 1, 0)
            with eng.Fori(0, LOOPS) as it:
                body(it * 2 + 2, 0, it + 1)
                body(it * 2 + 3, 1, it + 1)
            body(10, 0, LOOPS + 1)

        def pe_ffn(pe, uses, f):
            b = f * GROUPS

            def gu(g, par_, more=0):
                if not isinstance(g, int) or g >= 2:
                    pe.wait_ge(S["ff_ready"], g + (b - 1))
                for name, bank in (("gate", psum[par_]), ("up", psum[2 + par_])):
                    sl = f"{name}{par_}"
                    pe.wait_ge(loaded[sl], uses.now(sl, more) * 16)
                    w = slot[sl][:, :].rearrange("p (c n) -> p c n", n=256)
                    for j in range(2):
                        for c in range(KC):
                            mm = pe.matmul(bank[:, j * SEQ:(j + 1) * SEQ], w[:, c, j * P:(j + 1) * P], hT[:, c, :],
                                           start=(c == 0), stop=(c == KC - 1))
                    mm.then_inc(used[sl], 1)

            def down(g, par_, more=0, first=False, last=False):
                sl = f"down{par_}"
                pe.wait_ge(S["ff_ready"], g + (b + 1))
                pe.wait_ge(loaded[sl], uses.now(sl, more) * 16)
                w = slot[sl][:, :].rearrange("p (c n) -> p c n", n=D)
                for j in range(2):
                    for t in range(NT):
                        for h in range(2):
                            mm = pe.matmul(psum[4 + 2 * t + h][:, :], ffT[:, par_, j * SEQ + t * P:j * SEQ + (t + 1) * P],
                                           w[:, j, h * 512:(h + 1) * 512], start=first and j == 0,
                                           stop=last and j == 1, skip_group_check=True)
                mm.then_inc(used[sl], 1)

            gu(0, 0)
            gu(1, 1)
            down(0, 0, first=True)
            with pe.Fori(0, LOOPS) as it:
                gu(it * 2 + 2, 0, it + 1)
                down(it * 2 + 1, 1, it)
                gu(it * 2 + 3, 1, it + 1)
                down(it * 2 + 2, 0, it + 1)
            gu(10, 0, LOOPS + 1)
            down(9, 1, LOOPS)
            down(10, 0, LOOPS + 1, last=True)
            uses.ffn()

        def later(g):
            return not isinstance(g, int) or g >= 2

        def products_done(eng, uses, name, more=0):
            eng.wait_ge(used[name], uses.now(name, more) + 1)

        def act_ffn(act, uses, f):
            b = f * GROUPS

            def group(g, par_, more):
                products_done(act, uses, f"up{par_}", more)
                if later(g):
                    act.wait_ge(S["ff_ready"], g + (b - 1))
                act.activation(silu[:, par_, :], psum[par_][:, :], ACT.Silu).then_inc(S["silu_done"], 1)

            over_groups(act, group)
            uses.ffn()

        def dve_ffn(dve, uses, f):
            b = f * GROUPS

            def group(g, par_, more):
                dve.wait_ge(S["silu_done"], g + (b + 1))
                if later(g):
                    products_done(dve, uses, f"down{par_}", more - 1)
                dve.tensor_tensor(ffT[:, par_, :], silu[:, par_, :], psum[2 + par_][:, :],
                                  ALU.mult).then_inc(S["ff_ready"], 1)

            over_groups(dve, group)
            products_done(dve, uses, "down0", LOOPS + 1)
            uses.ffn()

        def dve_residual(dve, scale):
            for t in range(NT):
                for h in range(2):
                    xs = x[:, t, h * 512:(h + 1) * 512]
                    ins = dve.scalar_tensor_tensor(xs, psum[4 + 2 * t + h][:, :], scale, xs, ALU.mult, ALU.add)
            ins.then_inc(S["x_updated"], 1)

        def act_norm(act, n):
            if n == 0:
                act.wait_ge(x_in, 16)
            else:
                act.wait_ge(S["x_updated"], n)
            for t in range(NT):
                act.activation(hN[:, t, :], x[:, t, :], ACT.Square,
                               accum_out=rstd[:, t:t + 1]).then_inc(S["squares_done"], 1)
            act.wait_ge(S["squares_done"], 2 * n + 2)
            act.activation(rstd[:, 2:4], rstd[:, 0:2], ACT.Sqrt, bias=eps["norm"], scale=1.0 / D)\
               .then_inc(S["rms_root"], 1)

        def dve_norm(dve, n, link):
            dve.wait_ge(S["rms_root"], n + 1)
            link(dve.reciprocal(rstd[:, 4:6], rstd[:, 2:4]))
            for t in range(NT):
                dve.tensor_scalar(hN[:, t, :], x[:, t, :], rstd[:, 4 + t:5 + t], None, ALU.mult)\
                   .then_inc(S["normed"], 1)

        def pe_turn(pe, n, src, ready, count=None):
            for t in range(NT):
                if ready is not None:
                    pe.wait_ge(ready, NT * (n if count is None else count) + t + 1)
                for c in range(KC):
                    at = (c % 2) * SEQ + t * P
                    mm = pe.transpose(psum[c // 2][:, at:at + P], src[:, t, c * P:(c + 1) * P], ident)
            mm.then_inc(S["transposed_a"], 1)

        def evac_turn(eng, n, gain, scalar):
            eng.wait_ge(S["transposed_a"], n + 1)
            for c in range(KC):
                src = psum[c // 2][:, (c % 2) * SEQ:(c % 2 + 1) * SEQ]
                g = col(gain, c) if gain else 1.0
                if scalar and c < KC // 2:
                    eng.activation(hT[:, c, :], src, ACT.Copy, scale=g).then_inc(S["h_ready_a"], 1)
                if not scalar and c >= KC // 2:
                    eng.tensor_scalar(hT[:, c, :], src, g, None, ALU.mult).then_inc(S["h_ready_d"], 1)

        def pe_h_ready(pe, n):
            pe.wait_ge(S["h_ready_a"], 4 * n + 4)
            pe.wait_ge(S["h_ready_d"], 4 * n + 4)

        def pe_proj(pe, uses, per):
            with pe.Fori(0, 2) as it:
                for j in range(per):
                    if j >= 4:
                        pe.wait_ge(S["proj_ready"], it * per + (j - 3))
                    sl = SLOTS[j]
                    pe.wait_ge(loaded[sl], uses.now(sl, it) * 16)
                    w = slot[sl][:, :].rearrange("p (c n) -> p c n", n=256)
                    for i in range(2):
                        for c in range(KC):
                            mm = pe.matmul(psum[j][:, i * SEQ:(i + 1) * SEQ], w[:, c, i * P:(i + 1) * P], hT[:, c, :],
                                           start=(c == 0), stop=(c == KC - 1))
                    mm.then_inc(used[sl], 1)
                pe.wait_ge(S["proj_ready"], it * per + (per - 1 if per < 6 else 4))
            uses.each(SLOTS[:per], 2)

        def dve_proj(dve, uses, per, starts):
            with dve.Fori(0, 2) as it:
                for j in range(per):
                    products_done(dve, uses, SLOTS[j], it)
                    if j == 5:
                        dve.wait_ge(S["proj_ready"], it * per + 5)
                    dve.tensor_scalar(proj[:, bass.ds(starts(it, j), 2), 1:SEQ + 1],
                                      psum[j][:, :].rearrange("p (a b) -> p a b", a=2), 1.0, None,
                                      ALU.mult).then_inc(S["proj_ready"], 1)
            uses.each(SLOTS[:per], 2)

        def pe_out(pe, uses):
            for k in range(4):
                sl = SLOTS[k]
                pe.wait_ge(loaded[sl], uses.now(sl) * 16)
                w = slot[sl][:, :].rearrange("p (c n) -> p c n", n=D)
                for j in range(2):
                    c = 2 * k + j
                    for t in range(NT):
                        for h in range(2):
                            mm = pe.matmul(psum[4 + 2 * t + h][:, :], mix[:, c, t * P:(t + 1) * P],
                                           w[:, j, h * 512:(h + 1) * 512], start=(c == 0), stop=(c == KC - 1),
                                           skip_group_check=True)
                mm.then_inc(used[sl], 1)
                uses.n[sl] += 1

        def half(h):
            return slice(64 * (h % 2), 64 * (h % 2) + 64)

        def pe_attention(pe, nh, qc, kc, vtok, logit_, probT_):
            def score(h):
                bank, r = psum[h % 4], half(h)
                if h >= 4:
                    pe.wait_ge(S["biased"], h - 3)
                q, k = proj[r, qc + h // 2, 1:], proj[r, kc + h // 2, 1:]
                pe.matmul(bank[:, 0:P], q[:, 0:P], k[:, 0:P], start=True, stop=True)
                pe.matmul(bank[:, P:3 * P], q[:, P:], k, start=True, stop=True).then_inc(S["score_mm"], 1)

            def turn(h):
                pe.wait_ge(S["p_ready"], h + 1)
                if h >= 2:
                    pe.wait_ge(S["pt_done"], h - 1)
                for i in range(3):
                    mm = pe.transpose(psum[4 + h % 2][:, i * P:(i + 1) * P], logit_[:, h % 2, i * P:(i + 1) * P],
                                      ident)
                mm.then_inc(S["pt_mm"], 1)

            def value(h):
                pe.wait_ge(S["pt_done"], h + 1)
                if h % 2 == 0 and h >= 4:
                    pe.wait_ge(S["mixa_ready"], h // 2 - 1)
                bank = psum[6 + (h // 2) % 2]
                v = [vtok[:, t, h * 64:(h + 1) * 64] for t in range(NT)]
                pt = [probT_[:, h % 2, i * P:(i + 1) * P] for i in range(3)]
                pe.matmul(bank[half(h), 0:P], v[0], pt[0], start=True, stop=True)
                pe.matmul(bank[half(h), P:2 * P], v[0], pt[1], start=True, stop=False)
                pe.matmul(bank[half(h), P:2 * P], v[1], pt[2], start=False, stop=True).then_inc(S["av_mm"], 1)

            score(0)
            score(1)
            for h in range(nh):
                if h + 2 < nh:
                    score(h + 2)
                turn(h)
                if h:
                    value(h - 1)
            value(nh - 1)

        def dve_attention(dve, nh, bias, logit_, link):
            def logits(h):
                dve.wait_ge(S["score_mm"], h + 1)
                if h >= 2:
                    dve.wait_ge(S["pt_mm"], h - 1)
                bank, bh_ = psum[h % 4], bias(h)
                dve.scalar_tensor_tensor(logit_[:, h % 2, 0:P], bank[:, 0:P], 0.125, bh_[:, P:2 * P],
                                         ALU.mult, ALU.add)
                dve.scalar_tensor_tensor(logit_[:, h % 2, P:3 * P], bank[:, P:3 * P], 0.125, bh_,
                                         ALU.mult, ALU.add).then_inc(S["biased"], 1)
                dve.wait_ge(S["biased"], h + 1)
                dve.tensor_reduce(amax[:, h, 0:1], logit_[:, h % 2, 0:P], AX, ALU.max)
                link(dve.tensor_reduce(amax[:, h, 1:2], logit_[:, h % 2, P:3 * P], AX, ALU.max))
                dve.tensor_scalar(anmax[:, h, :], amax[:, h, :], -1.0, None, ALU.mult).then_inc(S["maxed"], 1)

            def normalise(h):
                dve.wait_ge(S["exp_done"], 2 * h + 2)
                link(dve.reciprocal(arec[:, h, :], asum[:, h, :]))
                for t, (lo, hi) in enumerate(((0, P), (P, 3 * P))):
                    ins = dve.tensor_scalar(logit_[:, h % 2, lo:hi], logit_[:, h % 2, lo:hi], arec[:, h, t:t + 1],
                                            None, ALU.mult)
                ins.then_inc(S["p_ready"], 1)

            logits(0)
            for h in range(nh):
                if h + 1 < nh:
                    logits(h + 1)
                normalise(h)

        def act_attention(act, nh, logit_, probT_, to):
            def exps(h):
                act.wait_ge(S["maxed"], h + 1)
                for t, (lo, hi) in enumerate(((0, P), (P, 3 * P))):
                    act.activation(logit_[:, h % 2, lo:hi], logit_[:, h % 2, lo:hi], ACT.Exp, bias=anmax[:, h, t:t + 1],
                                   accum_out=asum[:, h, t:t + 1]).then_inc(S["exp_done"], 1)

            def copy(h):
                act.wait_ge(S["pt_mm"], h + 1)
                if h >= 2:
                    act.wait_ge(S["av_mm"], h - 1)
                act.activation(probT_[:, h % 2, :], psum[4 + h % 2][:, 0:384], ACT.Copy).then_inc(S["pt_done"], 1)

            def out_(pair):
                act.wait_ge(S["av_mm"], 2 * pair + 2)
                act.activation(mix[:, to + pair, :], psum[6 + pair % 2][:, 0:SEQ], ACT.Copy)\
                   .then_inc(S["mixa_ready"], 1)

            exps(0)
            for h in range(nh):
                if h + 1 < nh:
                    exps(h + 1)
                copy(h)
                if h % 2 == 0 and h >= 2:
                    out_(h // 2 - 1)
            out_(nh // 2 - 1)

        def prob(t, h):
            return t * NH1 + h

        def bank_pair(c):
            return c // 2, slice((c % 2) * SEQ, (c % 2 + 1) * SEQ)

        def three(first):
            return [(psum[first][:, :].rearrange("p (a b) -> p a b", a=2), slice(0, 2)),
                    (psum[first + 1][:, 0:SEQ].rearrange("p (a b) -> p a b", a=1), slice(2, 3))]

        def ones_product(pe, first, src, mat=pairs):
            flat = src.rearrange("p a b -> p (a b)")
            pe.matmul(psum[first][:, :], mat, flat[:, 0:512], start=True, stop=True)
            return pe.matmul(psum[first + 1][:, 0:SEQ], mat, flat[:, 512:768], start=True, stop=True)

        TOK = [(w, t) for w in range(5) for t in range(NT)]
        TOK_BANK = [5, 6, 7, 0, 1, 2, 5, 6, 7, 0]

        def pe_mixer(pe, uses):
            pe.wait_ge(S["proj_ready"], 12)
            pe.wait_ge(S["lora_acts"], 2)
            for lo, hi, first, src in ((0, 32, 0, lact), (32, 64, 2, None), (64, 128, 4, lact)):
                for c in range(3):
                    b, cols_ = bank_pair(c)
                    rhs = src[lo:hi, :] if src is not None else sh[lo:hi, LORA, :]
                    mm = pe.matmul(psum[first + b][:, cols_], lora_w[lo:hi, c * P:(c + 1) * P], rhs,
                                   start=True, stop=True)
                mm.then_inc(S["lora_mm"], 1)
            pe.wait_ge(S["kk_sq"], 1)
            ones_product(pe, 6, tmp).then_inc(S["kk_sum"], 1)
            pe.wait_ge(S["qk_sq"], 1)
            pe.wait_ge(S["decay_sig"], 3)
            pe.wait_ge(S["iclr_sig"], 3)
            flat = qsq.rearrange("p a b -> p (a b)")
            for i in range(3):
                mm = pe.matmul(psum[i][:, :], pairs, flat[:, i * 512:(i + 1) * 512], start=True, stop=True)
            mm.then_inc(S["qk_sum"], 1)
            pe.wait_ge(S["bonus_sq"], 1)
            pe.wait_ge(S["gate_copied"], 2)
            ones_product(pe, 3, tmp).then_inc(S["bonus_mm"], 1)
            pe.wait_ge(S["rw_ready"], 1)
            pe.wait_ge(S["qk_root"], 1)
            for n, (w, t) in enumerate(TOK):
                if n >= 6:
                    pe.wait_ge(S["tok_copied_a" if n % 2 == 0 else "tok_copied_d"], (n - 6) // 2 + 1)
                for c in range(3):
                    if w == 0:
                        src = ar[:, c, t, 0, :]
                    elif w == 4:
                        src = proj[:, AV + c, 1 + t * P:1 + (t + 1) * P]
                    else:
                        src = (None, bh[:, c], kh[:, c], sh[:, V + c])[w][:, t * P:(t + 1) * P]
                    mm = pe.transpose(psum[TOK_BANK[n]][:, c * P:(c + 1) * P], src, ident)
                mm.then_inc(S["tok_mm"], 1)
            pe.wait_ge(S["qk_ready"], 1)
            pe.wait_ge(S["tok_copied_a"], 5)
            pe.wait_ge(S["tok_copied_d"], 5)
            pe.wait_ge(S["bonus_ready"], 1)
            pe_attention(pe, NH1, AQ, AK, avtok, logit, probT)
            pe.wait_ge(S["mixa_ready"], 3)
            for t in range(NT):
                for h in range(NH1):
                    p, r, c = prob(t, h), half(h), h // 2
                    if p >= 4:
                        pe.wait_ge(S["mats_ready"], p - 3)
                    rhs = ar[r, c, t].rearrange("p a b -> p (a b)")
                    pe.matmul(psum[p % 4][:, 0:256], bh[r, c, t * P:(t + 1) * P], rhs, start=True, stop=True)
                    pe.matmul(psum[p % 4][:, 256:512], kh[r, c, t * P:(t + 1) * P], rhs, start=True,
                              stop=True).then_inc(S["mats_mm"], 1)
                    if p % 4 == 3:
                        b = p // 4
                        pe.wait_ge(S["mats_ready"], p + 1)
                        for i in range(4):
                            mm = pe.transpose(psum[4 + b][:, i * P:(i + 1) * P], mats[:, 4 * b + i, 0, :], ident)
                        mm.then_inc(S["a_mm"], 1)
            for step, b, kind, n, dst, lhs, rhs, needs, _ in CHAIN:
                if step == 0:
                    pe.wait_ge(S["d_ready"], b + 1)
                    pe.wait_ge(S["dt_ready"], b + 1)
                    pe.wait_ge(S["mats_ready"], 12)
                if step == 1 and kind == "add":
                    pe.wait_ge(S["inv_seed"], 1)
                for k_, m in needs:
                    pe.wait_ge(S["copy_done" if k_ == "copy" else "add_done"], m + 1)
                if n >= 4:
                    pe.wait_ge(S["copy_done" if kind == "copy" else "add_done"], n - 3)
                bank = psum[(0 if kind == "copy" else 4) + n % 4]
                for i in range(4):
                    at, q = slice(i * P, (i + 1) * P), 4 * b + i
                    if rhs is None:
                        src = mats[:, q, 0, :] if lhs == "AT" else chain[lhs][:, q, :]
                        mm = pe.transpose(bank[:, at], src, ident)
                    else:
                        mm = pe.matmul(bank[:, at], chain[lhs][:, q, :], chain[rhs][:, q, :], start=True, stop=True)
                mm.then_inc(S["copy_mm" if kind == "copy" else "add_mm"], 1)
            inv = chain["INV"]
            pe.wait_ge(S["copy_done"], COPIES)
            for t in range(NT):
                for h in range(NH1):
                    mm = pe.matmul(psum[t][:, h * 64:(h + 1) * 64], mats[:, prob(t, h), 2, :],
                                   tok[:, 3, t, h * 64:(h + 1) * 64], start=True, stop=True)
                mm.then_inc(S["pav_mm"], 1)
            pe.wait_ge(S["add_done"], ADDS)
            for t in range(NT):
                for h in range(NH1):
                    mm = pe.matmul(psum[2 + t][half(h), (h // 2) * P:(h // 2 + 1) * P],
                                   tok[:, 0, t, h * 64:(h + 1) * 64], inv[:, prob(t, h), :], start=True, stop=True)
                mm.then_inc(S["mat_mm"], 1)
            pe.wait_ge(S["conv_acc"], 1)
            for c in range(2):
                mm = pe.matmul(psum[7][:, 0:SEQ], ones, mix[:, 6 + c, :], start=(c == 0), stop=(c == 1))
            mm.then_inc(S["cl_mean"], 1)
            pe.wait_ge(S["cl_sq"], 1)
            for c in range(2):
                mm = pe.matmul(psum[7][:, SEQ:2 * SEQ], ones, proj[:, CG + c, 1:], start=(c == 0), stop=(c == 1))
            mm.then_inc(S["cl_var"], 1)
            pe.wait_ge(S["cl_root"], 1)
            for ch in range(4):
                t, rows_ = ch // 2, slice(64 * (ch % 2), 64 * (ch % 2) + 64)
                if ch % 2 == 0:
                    pe.wait_ge(S["pav_done"], t + 1)
                    for h in range(NH1):
                        mm = pe.matmul(psum[4 + t][:, h * 64:(h + 1) * 64], inv[:, prob(t, h), :],
                                       pav[:, t, h * 64:(h + 1) * 64], start=(h == 0), stop=True,
                                       skip_group_check=True)
                if ch > 0:
                    pe.wait_ge(S["mat_done"], t + 1)
                    pe.wait_ge(S["st_done"], ch)
                    for pr in range(3):
                        at = slice(pr * P, (pr + 1) * P)
                        mm = pe.matmul(psum[4 + t][rows_, at], mat_[:, t, pr * P + 64 * (ch % 2):pr * P + 64 * (ch % 2) + 64],
                                       state[:, ch - 1, pr, :], start=False, stop=True, skip_group_check=True)
                mm.then_inc(S["sa_mm"], 1)
                if ch == 3:
                    break
                bank = psum[6 + ch % 2]
                for pr in range(3):
                    at = slice(pr * P, (pr + 1) * P)
                    pe.matmul(bank[:, at], tok[rows_, 2, t, at], tok[rows_, 3, t, at], start=(pr == 0), stop=False,
                              skip_group_check=True)
                pe.wait_ge(S["sa_done"], ch + 1)
                for pr in range(3):
                    at = slice(pr * P, (pr + 1) * P)
                    mm = pe.matmul(bank[:, at], tok[rows_, 1, t, at], satok[rows_, t, at], start=False, stop=True,
                                   skip_group_check=True)
                mm.then_inc(S["st_mm"], 1)
            pe.wait_ge(S["sa_done"], 4)
            for c in range(3):
                for t in range(NT):
                    at = slice(t * P, (t + 1) * P)
                    for h in (2 * c, 2 * c + 1):
                        v = slice(h * 64, (h + 1) * 64)
                        pe.matmul(psum[c][half(h), at], satok[:, t, v], mats[:, prob(t, h), 1, :], start=True,
                                  stop=False, skip_group_check=True)
                        pe.matmul(psum[c][half(h), at], tok[:, 3, t, v], mats[:, prob(t, h), 3, :], start=False,
                                  stop=True, skip_group_check=True)
                    for ch in (2 * t, 2 * t + 1):
                        if ch > 0:
                            k = 64 * (ch % 2)
                            mm = pe.matmul(psum[c][:, t * P + k:t * P + k + 64], state[:, ch - 1, c, :],
                                           ar[:, c, t, 1, k:k + 64], start=False, stop=True, skip_group_check=True)
                mm.then_inc(S["y_mm"], 1)
            pe.wait_ge(S["y_copied"], 3)
            ones_product(pe, 3, ysb).then_inc(S["gn_mean"], 1)
            pe.wait_ge(S["gn_sq"], 1)
            ones_product(pe, 5, ysq).then_inc(S["gn_var"], 1)
            pe.wait_ge(S["mixr_ready"], 1)
            pe.wait_ge(S["mixc_ready"], 2)
            pe_out(pe, uses)

        def act_mixer(act, link):
            act.wait_ge(S["proj_ready"], 12)
            act.activation(qsq, proj[:, AQ:AQ + 6, 1:], ACT.Square).then_inc(S["qk_sq"], 1)
            act.activation(proj[:, CG:CG + 2, 1:], proj[:, CG:CG + 2, 1:], ACT.Sigmoid).then_inc(S["conv_sig"], 1)
            act.wait_ge(S["shifted"], 10)
            act.activation(lact[0:32, :], sh[0:32, LORA, :], ACT.Tanh).then_inc(S["lora_acts"], 1)
            act.activation(lact[64:128, :], sh[64:128, LORA, :], ACT.Sigmoid).then_inc(S["lora_acts"], 1)
            act.wait_ge(S["lora_mm"], 2)
            for c in range(3):
                b, cols_ = bank_pair(c)
                act.activation(ld[:, c, :], psum[b][:, cols_], ACT.Sigmoid, bias=col("rwkv_w0", c))\
                   .then_inc(S["decay_sig"], 1)
                act.activation(iclr[:, c, :], psum[2 + b][:, cols_], ACT.Sigmoid, bias=col("rwkv_a0", c))\
                   .then_inc(S["iclr_sig"], 1)
            act.wait_ge(S["lora_mm"], 3)
            for v, at in three(4):
                act.activation(gate[:, at, :], v, ACT.Copy).then_inc(S["gate_copied"], 1)
            act.wait_ge(S["kk_sum"], 1)
            for i, (v, at) in enumerate(three(6)):
                ins = act.activation(tmp[:, at, :], v, ACT.Sqrt, bias=eps["kk"])
            ins.then_inc(S["kk_root"], 1)
            act.wait_ge(S["qk_sum"], 1)
            for i in range(3):
                ins = act.activation(qsq[:, 2 * i:2 * i + 2, :], psum[i][:, :].rearrange("p (a b) -> p a b", a=2),
                                     ACT.Sqrt, bias=eps["norm"], scale=1.0 / 64)
            ins.then_inc(S["qk_root"], 1)
            act.wait_ge(S["cum_ready"], 2)
            act.activation(ec, cum, ACT.Exp).then_inc(S["exps_done"], 1)
            act.activation(en, cum, ACT.Exp, scale=-1.0).then_inc(S["exps_done"], 1)
            act.activation(ecx, ld, ACT.Exp).then_inc(S["exps_done"], 1)
            for n in range(0, 10, 2):
                w, t = TOK[n]
                act.wait_ge(S["tok_mm"], n + 1)
                dst = tok[:, w, t, :] if w < 4 else avtok[:, t, 0:384]
                act.activation(dst, psum[TOK_BANK[n]][:, 0:384], ACT.Copy).then_inc(S["tok_copied_a"], 1)
            act_attention(act, NH1, logit, probT, 3)
            for step, b, kind, n, dst, *_ in CHAIN:
                if kind == "copy":
                    act.wait_ge(S["copy_mm"], n + 1)
                    act.activation(chain[dst][:, 4 * b:4 * b + 4, :],
                                   psum[n % 4][:, :].rearrange("p (a b) -> p a b", a=4), ACT.Copy)\
                       .then_inc(S["copy_done"], 1)
            for t in range(NT):
                act.wait_ge(S["pav_mm"], t + 1)
                act.activation(pav[:, t, :], psum[t][:, 0:384], ACT.Copy).then_inc(S["pav_done"], 1)
            for t in range(NT):
                act.wait_ge(S["mat_mm"], t + 1)
                act.activation(mat_[:, t, :], psum[2 + t][:, 0:384], ACT.Copy).then_inc(S["mat_done"], 1)
            act.wait_ge(S["cl_var"], 1)
            act.activation(proj[:, CG, 1:], psum[7][:, SEQ:], ACT.Sqrt, bias=eps["ln"], scale=1.0 / 256)\
               .then_inc(S["cl_root"], 1)
            for ch in range(4):
                t, rows_ = ch // 2, slice(64 * (ch % 2), 64 * (ch % 2) + 64)
                act.wait_ge(S["sa_mm"], ch + 1)
                act.activation(satok[rows_, t, :], psum[4 + t][rows_, 0:384], ACT.Copy).then_inc(S["sa_done"], 1)
            act.wait_ge(S["cl_ready"], 1)
            for c in range(2):
                act.activation(mix[:, 6 + c, :], mix[:, 6 + c, :], ACT.Silu, bias=col("conv_ln_b", c),
                               scale=col("conv_ln_w", c)).then_inc(S["mixc_ready"], 1)
            for c in range(3):
                act.wait_ge(S["y_mm"], c + 1)
                act.activation(ysb[:, c, :], psum[c][:, 0:SEQ], ACT.Copy).then_inc(S["y_copied"], 1)
            act.wait_ge(S["gn_var"], 1)
            for v, at in three(5):
                ins = act.activation(yroot[:, at, :], v, ACT.Sqrt, bias=eps["gn"], scale=1.0 / 64)
            ins.then_inc(S["gn_root"], 1)

        def dve_mixer(dve, uses, link):
            mult, add, sub = ALU.mult, ALU.add, ALU.subtract
            dve.wait_ge(S["proj_ready"], 12)
            link(dve.tensor_tensor(sh, proj[:, 0:10, 0:SEQ], proj[:, 0:10, 1:], sub))
            for c in (9, 3, 4, 5, 0, 1, 2, 6, 7, 8):
                dve.scalar_tensor_tensor(sh[:, c, :], sh[:, c, :], col("shift_mu", c), proj[:, c, 1:], mult, add)\
                   .then_inc(S["shifted"], 1)
            dve.wait_ge(S["shifted"], 10)
            for c in range(3):
                ins = dve.tensor_scalar(kk[:, c, :], sh[:, K + c, :], col("rwkv_k_k", c), None, mult)
            link(ins)
            dve.tensor_tensor(tmp, kk, kk, mult).then_inc(S["kk_sq"], 1)
            dve.wait_ge(S["decay_sig"], 3)
            link(dve.tensor_scalar(ld, ld, -float(np.exp(-0.5)), None, mult))
            for c in range(3):
                ins = dve.tensor_tensor_scan(cum[:, c, :], const("scan"), ld[:, c, :], 0.0, mult, add)
            ins.then_inc(S["cum_ready"], 1)
            dve.wait_ge(S["cum_ready"], 1)
            dve.tensor_tensor(ld, cum, ld, sub).then_inc(S["cum_ready"], 1)
            dve.wait_ge(S["iclr_sig"], 3)
            for c in range(3):
                ins = dve.tensor_scalar(kmod[:, c, :], iclr[:, c, :], 1.0, col("rwkv_k_a", c), sub, mult)
            link(ins)
            link(dve.scalar_tensor_tensor(kmod, kmod, 1.0, sh[:, K:K + 3, :], add, mult))
            dve.wait_ge(S["kk_root"], 1)
            link(dve.reciprocal(tmp, tmp))
            link(dve.tensor_tensor(kk, kk, tmp, mult))
            link(dve.tensor_tensor(iclr, kk, iclr, mult))
            for c in range(3):
                ins = dve.scalar_tensor_tensor(tmp[:, c, :], sh[:, R + c, :], col("rwkv_r_k", c), kmod[:, c, :],
                                               mult, mult)
            ins.then_inc(S["bonus_sq"], 1)
            dve.wait_ge(S["exps_done"], 3)
            v4 = lambda a_: a_.rearrange("p c (t k) -> p c t k", t=NT)
            dve.scalar_tensor_tensor(ar[:, :, :, 0, :], v4(kk), -1.0, v4(ecx), mult, mult)
            dve.tensor_tensor(ar[:, :, :, 1, :], v4(sh[:, R:R + 3, :]), v4(ec), mult)
            dve.tensor_tensor(bh, iclr, en, mult)
            dve.tensor_tensor(kh, kmod, en, mult).then_inc(S["rw_ready"], 1)
            dve.wait_ge(S["qk_root"], 1)
            link(dve.reciprocal(qsq, qsq))
            for c in range(6):
                ins = dve.scalar_tensor_tensor(proj[:, AQ + c, 1:], proj[:, AQ + c, 1:],
                                               col("attn_q_norm" if c < 3 else "attn_k_norm"), qsq[:, c, :],
                                               mult, mult)
            ins.then_inc(S["qk_ready"], 1)
            dve.wait_ge(S["bonus_mm"], 1)
            for v, at in three(3):
                ins = dve.tensor_tensor(bonus[:, at, :], v, sh[:, V + at.start:V + at.stop, :], mult)
            ins.then_inc(S["bonus_ready"], 1)
            for n in range(1, 10, 2):
                w, t = TOK[n]
                dve.wait_ge(S["tok_mm"], n + 1)
                dst = tok[:, w, t, :] if w < 4 else avtok[:, t, 0:384]
                dve.tensor_copy(dst, psum[TOK_BANK[n]][:, 0:384]).then_inc(S["tok_copied_d"], 1)
            bias1 = const("bias1")
            dve_attention(dve, NH1, lambda h: bias1[:, h * 256:(h + 1) * 256], logit, link)
            m4 = const("mask4")
            blk = const("blk16").unsqueeze(1).broadcast_to([P, 4, P])
            for p in range(12):
                dve.wait_ge(S["mats_mm"], p + 1)
                dve.tensor_tensor(mats[:, p].rearrange("p a b -> p (a b)"), psum[p % 4][:, :], m4, mult)\
                   .then_inc(S["mats_ready"], 1)
                if p % 4 == 3:
                    b = p // 4
                    dve.wait_ge(S["a_mm"], b + 1)
                    dve.wait_ge(S["mats_ready"], p + 1)
                    dve.tensor_tensor(chain["D"][:, 4 * b:4 * b + 4, :],
                                      psum[4 + b][:, :].rearrange("p (a b) -> p a b", a=4), blk, mult)\
                       .then_inc(S["d_ready"], 1)
                    dve.tensor_tensor(chain["DT"][:, 4 * b:4 * b + 4, :], mats[:, 4 * b:4 * b + 4, 0, :], blk, mult)\
                       .then_inc(S["dt_ready"], 1)
            dve.wait_ge(S["dt_ready"], 3)
            dve.tensor_tensor(chain["INV"], chain["DT"], ident.unsqueeze(1).broadcast_to([P, 12, P]), add)\
               .then_inc(S["inv_seed"], 1)
            for step, b, kind, n, dst, _, _, _, before in CHAIN:
                if kind == "add":
                    dve.wait_ge(S["add_mm"], n + 1)
                    src = psum[4 + n % 4][:, :].rearrange("p (a b) -> p a b", a=4)
                    to = chain[dst][:, 4 * b:4 * b + 4, :]
                    if dst == "INV":
                        if before is None:
                            dve.wait_ge(S["inv_seed"], 1)
                        else:
                            dve.wait_ge(S["add_done"], before[1] + 1)
                        ins = dve.tensor_tensor(to, src, to, add)
                    else:
                        if before[0] == "copy":
                            dve.wait_ge(S["copy_done"], before[1] + 1)
                        blk = const("blk32" if dst == "D" else "blk64").unsqueeze(1).broadcast_to([P, 4, P])
                        ins = dve.tensor_tensor(to, src, blk, mult)
                    ins.then_inc(S["add_done"], 1)
            dve.wait_ge(S["cl_mean"], 1)
            for c in range(2):
                ins = dve.scalar_tensor_tensor(mix[:, 6 + c, :], psum[7][:, 0:SEQ], -1.0 / 256, mix[:, 6 + c, :],
                                               mult, add)
            link(ins)
            dve.tensor_tensor(proj[:, CG:CG + 2, 1:], mix[:, 6:8, :], mix[:, 6:8, :], mult).then_inc(S["cl_sq"], 1)
            dve.wait_ge(S["cl_root"], 1)
            link(dve.reciprocal(proj[:, CG + 1, 1:], proj[:, CG, 1:]))
            for c in range(2):
                ins = dve.tensor_tensor(mix[:, 6 + c, :], mix[:, 6 + c, :], proj[:, CG + 1, 1:], mult)
            ins.then_inc(S["cl_ready"], 1)
            for ch in range(3):
                dve.wait_ge(S["st_mm"], ch + 1)
                src = psum[6 + ch % 2][:, 0:384].rearrange("p (a b) -> p a b", a=3)
                if ch == 0:
                    dve.wait_ge(S["cend_ready"], 3)
                    dve.tensor_tensor(state[:, 0], src, cend[:, 0], mult).then_inc(S["st_done"], 1)
                else:
                    link(dve.tensor_tensor(state[:, ch], src, state[:, ch - 1], add))
                    dve.tensor_tensor(state[:, ch], state[:, ch], cend[:, ch], mult).then_inc(S["st_done"], 1)
                dve.wait_ge(S["st_done"], ch + 1)
            dve.wait_ge(S["gn_mean"], 1)
            for v, at in three(3):
                ins = dve.scalar_tensor_tensor(ysb[:, at, :], v, -1.0 / 64, ysb[:, at, :], mult, add)
            link(ins)
            dve.tensor_tensor(ysq, ysb, ysb, mult).then_inc(S["gn_sq"], 1)
            dve.wait_ge(S["gn_root"], 1)
            link(dve.reciprocal(yroot, yroot))
            link(dve.tensor_tensor(ysb, ysb, yroot, mult))
            for c in range(3):
                ins = dve.tensor_scalar(ysb[:, c, :], ysb[:, c, :], col("rwkv_ln_w", c), col("rwkv_ln_b", c),
                                        mult, add)
            link(ins)
            link(dve.tensor_tensor(ysb, ysb, bonus, add))
            dve.tensor_tensor(mix[:, 0:3, :], ysb, gate, mult).then_inc(S["mixr_ready"], 1)
            uses.each(SLOTS[:3])
            products_done(dve, uses, SLOTS[3])
            uses.each(SLOTS[3:4])

        def pool_mixer(pool, link):
            mult, add = ALU.mult, ALU.add
            z = proj[:, CU:CU + 2, 1:]
            pool.wait_ge(S["conv_sig"], 1)
            link(pool.tensor_tensor(z, z, proj[:, CG:CG + 2, 1:], mult))
            for c in range(2):
                ins = pool.tensor_scalar(mix[:, 6 + c, :], z[:, c, :], col("conv_dw_w", 2 * (CONV_W - 1) + c),
                                         col("conv_dw_b", c), mult, add)
            link(ins)
            part = proj[:, CG:CG + 2, 1:]
            for lag in range(1, CONV_W):
                for c in range(2):
                    ins = pool.tensor_scalar(part[:, c, lag:], z[:, c, 0:SEQ - lag],
                                             col("conv_dw_w", 2 * (CONV_W - 1 - lag) + c), None, mult)
                link(ins)
                ins = pool.tensor_tensor(mix[:, 6:8, lag:], mix[:, 6:8, lag:], part[:, :, lag:], add)
                if lag < CONV_W - 1:
                    link(ins)
            ins.then_inc(S["conv_acc"], 1)
            pool.wait_ge(S["add_done"], ADDS)
            pool.wait_ge(S["exps_done"], 1)
            for ch in range(3):
                end = ec[:, :, (ch + 1) * CHUNK - 1:(ch + 1) * CHUNK].broadcast_to([P, 3, P])
                pool.tensor_tensor(cend[:, ch], end, pairs.unsqueeze(1).broadcast_to([P, 3, P]), mult)\
                    .then_inc(S["cend_ready"], 1)

        def dve_pick_rows(dve, l):
            dve.wait_ge(rows_in, 16 * N_ROW_DMAS)
            one = lambda a_: a_.rearrange("p a b -> p (a b)")
            dve.tensor_scalar(row_now[0:NROWS, :], one(rows[0:NROWS, bass.ds(l, 1), :]), 1.0, None, ALU.mult)\
               .then_inc(S["rows_picked"], 1)
            dve.tensor_scalar(lora_w[:, :], one(lora_all[:, bass.ds(l, 1), :]), 1.0, None, ALU.mult)\
               .then_inc(S["rows_picked"], 1)
            dve.wait_ge(S["params_psum"], 1)
            dve.tensor_copy(par[:, 0:NROWS], psum[7][:, 0:NROWS]).then_inc(S["params_ready"], 1)
            dve.wait_ge(S["params_ready"], 1)

        ROW_SOURCES = [(ROWS[n], a[n].rearrange("l (r p) -> r l p", p=P)) for n in
                       ("norm_ffn1", "norm_mix", "norm_ffn2", "shift_mu", "rwkv_w0", "rwkv_a0", "rwkv_k_k",
                        "rwkv_k_a", "rwkv_ln_w", "rwkv_ln_b", "conv_dw_b", "conv_ln_w", "conv_ln_b")]
        ROW_SOURCES += [(ROWS["rwkv_r_k"], a["rwkv_r_k"].rearrange("l (r h) p -> r l (h p)", h=2)),
                        (ROWS["conv_dw_w"], None)]
        LORAS = (("rwkv_w2", 0, 32), ("rwkv_a2", 32, 64), ("rwkv_g2", 64, 128))
        N_ROW_DMAS = len(ROW_SOURCES) - 1 + DEPTH + 4 + len(LORAS)

        def load_rows(eng):
            n = 0
            for at, src in ROW_SOURCES:
                if src is None:
                    for l in range(DEPTH):
                        eng.dma_start(rows[at:at + 2 * CONV_W, l, :],
                                      a["conv_dw_w"][l].rearrange("j (c p) -> (j c) p", p=P)).then_inc(rows_in, 16)
                        n += 1
                else:
                    eng.dma_start(rows[at:at + src.shape[0], :, :], src).then_inc(rows_in, 16)
                    n += 1
            for name in ("attn_q_norm", "attn_k_norm"):
                for half_ in range(2):
                    eng.dma_start(rows[ROWS[name]:ROWS[name] + 1, :, half_ * 64:half_ * 64 + 64],
                                  a[name].rearrange("(o l) k -> o l k", o=1)).then_inc(rows_in, 16)
                    n += 1
            for name, lo, hi in LORAS:
                eng.dma_start(lora_all[lo:hi, :, :], a[name].rearrange("l k n -> k l n")).then_inc(rows_in, 16)
                n += 1
            assert n == N_ROW_DMAS

        def layer_over(eng, l):
            eng.drain().then_inc(arrived, 1)
            eng.wait_ge(cleared, l + 1)
            eng.sem_inc(resumed, 1)

        N_SECOND = 5 + 1 + 4
        SECOND = DEPTH

        def act_second_loads(act):
            w3, b1_, cw, ps = a["ffn_conv_w_2"], a["ffn_conv_b_2"], a["conv_w_2"], a["pool_scale_2"]
            act.wait_ge(S["pool_link"], 2)
            for dst, src in ((rows2[0:88, 0, :], w3[0, 0:2].rearrange("j (c p) -> (j c) p", p=P)),
                             (rows2[0:44, 1, :], w3[0, 2].rearrange("(c p) -> c p", p=P)),
                             (rows2[44:88, 1, :], b1_[0].rearrange("(c p) -> c p", p=P)),
                             (rows2[88:94, 1, :], cw[0].rearrange("j (c p) -> (j c) p", p=P)),
                             (rows2[94:96, 1, :], ps[0].rearrange("(c p) -> c p", p=P)),
                             (tab[0:NH2, 32:64], a["rel_bias_2"])):
                act.dma_start(dst, src).then_inc(second_in, 16)
            for g in range(4):
                lo = 64 * (g % 2)
                act.dma_start(wpool[lo:lo + 64, g // 2, lo:lo + 64], a["w_pool_2"][0, g]).then_inc(second_in, 16)

        def load_ln(eng, g, b):
            for i, n in enumerate((g, b)):
                eng.dma_start(ln_gb[:, i, :], a[n].broadcast_to([P, D])).then_inc(x_in, 16)

        def pe_second(pe, uses):
            pe_turn(pe, 0, x, None)
            pe.wait_ge(second_in, 16 * N_SECOND)
            pe.transpose(psum[4][:, 0:88], rows2[0:88, 0, :], ident[0:88, 0:88])
            pe.transpose(psum[4][:, 128:128 + B_ROWS], rows2[0:B_ROWS, 1, :], ident[0:B_ROWS, 0:B_ROWS])
            pe.transpose(psum[4][0:32, 256:256 + NH2], tab[0:NH2, 32:64], ident[0:NH2, 0:NH2])\
              .then_inc(S["params_psum"], 1)
            pe.wait_ge(S["params_ready"], 1)
            for h in range(NH2):
                if h >= 2:
                    pe.wait_ge(S["spread_ready"], h - 1)
                pe.matmul(psum[5 + h % 2][:, 0:384], tab[0:33, h:h + 1].broadcast_to([33, P]), hot[:, :],
                          start=True, stop=True).then_inc(S["biasrow_mm"], 1)
            pe_h_ready(pe, 0)
            pe.wait_ge(S["params_ready"], 1)
            pe_proj(pe, uses, 5)
            pe.wait_ge(S["proj_ready"], 10)
            pe.wait_ge(S["spread_ready"], NH2)
            for t in range(NT):
                for c in range(4):
                    mm = pe.transpose(psum[6 + t][:, c * P:(c + 1) * P], proj[:, V2 + c, 1 + t * P:1 + (t + 1) * P],
                                      ident)
                mm.then_inc(S["tok_mm"], 1)
            pe.wait_ge(S["tok_copied_a"], 2)
            pe_attention(pe, NH2, Q2, K2, avtok2, logit2, probT2)
            pe.wait_ge(S["pool_ready"], 1)
            pe.wait_ge(S["mixa_ready"], 4)
            for c in range(2):
                mm = pe.matmul(psum[c][:, 0:SEQ], wpool[:, c, :], pl[:, 0, c, :], start=True, stop=True)
            mm.then_inc(S["pool_mm"], 1)
            pe.wait_ge(S["mixr_ready"], 1)
            pe.wait_ge(S["mixc_ready"], 1)
            pe_out(pe, uses)
            pe_turn(pe, 1, x, S["normed"], count=0)
            pe_h_ready(pe, 1)
            pe_ffn(pe, uses, 0)

        def act_second(act, uses):
            act_second_loads(act)
            load_ln(act, "ln1_g_2", "ln1_b_2")
            evac_turn(act, 0, None, True)
            for h in range(NH2):
                act.wait_ge(S["biasrow_mm"], h + 1)
                act.activation(spread[:, h, :], psum[5 + h % 2][:, 0:384], ACT.Copy).then_inc(S["spread_ready"], 1)
            act.wait_ge(S["spread_ready"], NH2)
            act.dma_start(scratch.ap(), spread).then_inc(spread_out, 16)
            act.wait_ge(spread_out, 16)
            pitch = NH2 * 384
            act.dma_start(bias2, bass.AP(scratch, P - 1, [[pitch - 1, P], [384, NH2], [1, 2 * P]]))\
               .then_inc(bias_in, 16)
            for t in range(NT):
                act.wait_ge(S["tok_mm"], t + 1)
                act.activation(avtok2[:, t, :], psum[6 + t][:, :], ACT.Copy).then_inc(S["tok_copied_a"], 1)
            act_attention(act, NH2, logit2, probT2, 0)
            act.wait_ge(S["pool_mm"], 1)
            for c in range(2):
                ins = act.activation(mix[:, 6 + c, :], psum[c][:, 0:SEQ], ACT.Copy, scale=par2c[:, 6 + c:7 + c])
            ins.then_inc(S["mixr_ready"], 1)
            act_ln(act, 0)
            act.wait_ge(S["normed"], NT)
            load_ln(act, "ln2_g_2", "ln2_b_2")
            evac_turn(act, 1, None, True)
            uses.each(SLOTS[:5], 2)
            uses.each(SLOTS[:4])

            def group(g, par_, more):
                products_done(act, uses, f"up{par_}", more)
                act.wait_ge(S["taps_picked"], g + 1)
                if later(g):
                    act.wait_ge(S["ff_ready"], g - 1)
                for q, bank in enumerate((psum[2 + par_], psum[par_])):
                    for j in range(2):
                        at = slice(j * SEQ, (j + 1) * SEQ)
                        ins = act.activation(taps[:, par_, q, at], bank[:, at], ACT.Identity,
                                             bias=tap_now[:, par_, 3, q, j:j + 1],
                                             scale=tap_now[:, par_, 2, q, j:j + 1])
                ins.then_inc(S["taps_act"], 1)
                act.wait_ge(S["taps_done"], g + 1)
                act.activation(silu[:, par_, :], taps[:, par_, 1, :], ACT.Silu).then_inc(S["silu_done"], 1)

            over_groups(act, group)
            uses.ffn()
            act_ln(act, 1)
            act.wait_ge(S["normed"], 2 * NT)
            act.dma_start(out[0].rearrange("(t p) n -> p t n", p=P), x[:, :, :]).then_inc(stored, 16)
            act.wait_ge(stored, 16)

        def act_ln(act, n):
            for t in range(NT):
                act.wait_ge(S["stats_ready"], NT * n + t + 1)
                act.activation(rstd[:, t:t + 1], lnvar[:, t, 1:2], ACT.Sqrt, bias=eps["ln"])\
                   .then_inc(S["rms_root"], 1)

        def dve_ln(dve, n, link):
            for t in range(NT):
                for h in range(2):
                    xs = x[:, t, h * 512:(h + 1) * 512]
                    ins = dve.scalar_tensor_tensor(xs, xs, ALPHA, psum[4 + 2 * t + h][:, :], ALU.mult, ALU.add)
                link(ins)
                for h in range(2):
                    ins = dve.bn_stats(lnstat[:, h, :], x[:, t, h * 512:(h + 1) * 512])
                link(ins)
                dve.bn_aggr(lnvar[:, t, :], lnstat).then_inc(S["stats_ready"], 1)
                dve.wait_ge(S["stats_ready"], NT * n + t + 1)
            dve.wait_ge(x_in, 16 * (1 + 2 * n + 2))
            for t in range(NT):
                dve.wait_ge(S["rms_root"], NT * n + t + 1)
                link(dve.reciprocal(rstd[:, 4 + t:5 + t], rstd[:, t:t + 1]))
                link(dve.tensor_scalar(x[:, t, :], x[:, t, :], lnvar[:, t, 0:1], rstd[:, 4 + t:5 + t],
                                       ALU.subtract, ALU.mult))
                link(dve.tensor_tensor(x[:, t, :], x[:, t, :], ln_gb[:, 0, :], ALU.mult))
                dve.tensor_tensor(x[:, t, :], x[:, t, :], ln_gb[:, 1, :], ALU.add).then_inc(S["normed"], 1)

        def dve_second(dve, uses, link):
            evac_turn(dve, 0, None, False)
            dve.wait_ge(S["params_psum"], 1)
            dve.tensor_copy(par2[:, 0:2, :].rearrange("p a b -> p (a b)"), psum[4][:, 0:88])
            dve.tensor_copy(par2[:, 2:4, :].rearrange("p a b -> p (a b)"), psum[4][:, 128:216])
            dve.tensor_copy(tab[0:32, 0:NH2], psum[4][0:32, 256:256 + NH2])
            dve.tensor_copy(par2c, psum[4][:, 216:224]).then_inc(S["params_ready"], 1)
            dve_proj(dve, uses, 5, start2)
            dve.wait_ge(bias_in, 16)
            dve_attention(dve, NH2, lambda h: bias2[:, h, :], logit2, link)
            uses.each(SLOTS[:3])
            products_done(dve, uses, SLOTS[3])
            uses.each(SLOTS[3:4])
            dve_ln(dve, 0, link)
            evac_turn(dve, 1, None, False)
            view = par2.rearrange("p k (q u) -> p k q u", q=2)

            def group(g, par_, more):
                if later(g):
                    dve.wait_ge(S["taps_act"], g - 1)
                dve.tensor_scalar(tap_now[:, par_], view[:, :, :, bass.ds(g * 2, 2)], 1.0, None,
                                  ALU.mult).then_inc(S["taps_picked"], 1)
                dve.wait_ge(S["taps_picked"], g + 1)
                dve.wait_ge(S["taps_act"], g + 1)
                for lag in (1, 2):
                    for q, bank in enumerate((psum[2 + par_], psum[par_])):
                        for j in range(2):
                            to = taps[:, par_, q, j * SEQ + lag:(j + 1) * SEQ]
                            ins = dve.scalar_tensor_tensor(to, bank[:, j * SEQ:(j + 1) * SEQ - lag],
                                                           tap_now[:, par_, 2 - lag, q, j:j + 1], to,
                                                           ALU.mult, ALU.add)
                    ins.then_inc(S["lag_done" if lag == 1 else "taps_done"], 1)
                    if lag == 1:
                        dve.wait_ge(S["lag_done"], g + 1)
                dve.wait_ge(S["silu_done"], g + 1)
                if later(g):
                    products_done(dve, uses, f"down{par_}", more - 1)
                dve.tensor_tensor(ffT[:, par_, :], silu[:, par_, :], taps[:, par_, 0, :],
                                  ALU.mult).then_inc(S["ff_ready"], 1)

            over_groups(dve, group)
            products_done(dve, uses, "down0", LOOPS + 1)
            uses.ffn()
            dve_ln(dve, 1, link)

        def pool_second(pool, link):
            mult, add = ALU.mult, ALU.add
            link(pool.memset(wpool, 0.0))
            link(pool.memset(tab[32:33, 0:NH2], 1.0))
            pool.wait_ge(S["proj_ready"], 10)
            pool.wait_ge(S["params_ready"], 1)
            link(pool.tensor_tensor(cz, proj[:, CC2:CC2 + 2, 1:], proj[:, CX2:CX2 + 2, 1:], mult))
            for c in range(2):
                ins = pool.tensor_scalar(mix[:, 4 + c, :], cz[:, c, :], par2c[:, 4 + c:5 + c], None, mult)
            link(ins)
            part = proj[:, CC2:CC2 + 2, 1:]
            for lag in (1, 2):
                for c in range(2):
                    i = 2 * (2 - lag) + c
                    ins = pool.tensor_scalar(part[:, c, lag:], cz[:, c, 0:SEQ - lag], par2c[:, i:i + 1], None, mult)
                link(ins)
                link(pool.tensor_tensor(mix[:, 4:6, lag:], mix[:, 4:6, lag:], part[:, :, lag:], add))
            pool.tensor_tensor(mix[:, 4:6, :], mix[:, 4:6, :], proj[:, CB2:CB2 + 2, 1:], mult)\
                .then_inc(S["mixc_ready"], 1)
            p_ = proj[:, PI2:PI2 + 2, 1:]
            u, v = pl[:, 0], pl[:, 1]
            link(pool.tensor_copy(u, p_))
            link(pool.tensor_tensor(u[:, :, 1:], u[:, :, 1:], p_[:, :, 0:SEQ - 1], add))
            link(pool.tensor_copy(v, u))
            link(pool.tensor_tensor(v[64:P, 0, 2:], v[64:P, 0, 2:], u[64:P, 0, 0:SEQ - 2], add))
            link(pool.tensor_tensor(v[:, 1, 2:], v[:, 1, 2:], u[:, 1, 0:SEQ - 2], add))
            link(pool.tensor_copy(u, v))
            link(pool.tensor_tensor(u[:, 1, 4:], u[:, 1, 4:], v[:, 1, 0:SEQ - 4], add))
            link(pool.tensor_copy(v, u))
            link(pool.tensor_tensor(v[64:P, 1, 8:], v[64:P, 1, 8:], u[64:P, 1, 0:SEQ - 8], add))
            link(pool.tensor_tensor(v, v, const("poolw").rearrange("p (a b) -> p a b", a=2), mult))
            pool.tensor_tensor(u, v, p_, ALU.subtract).then_inc(S["pool_ready"], 1)

        @block.sync
        def _(sp):
            with sp.Fori(0, DEPTH) as l:
                uses = Uses(l, PER_LAYER)
                sp_ffn(sp, uses, l, a["ffn1_w_gate"], 0, a["ffn1_w_up"], 0, a["ffn1_w_down"])
                sp_proj(sp, uses, l, a["w_in"], 6, start1)
                sp_out(sp, uses, l, a["w_out"])
                sp_ffn(sp, uses, l, a["ffn2_w_gate"], 0, a["ffn2_w_up"], 0, a["ffn2_w_down"])
            uses = Uses(SECOND, PER_LAYER)
            sp_proj(sp, uses, 0, a["w_in_2"], 5, start2)
            sp_out(sp, uses, 0, a["w_out_2"])
            sp_ffn(sp, uses, 0, a["w_up_2"], DFF, a["w_up_2"], 0, a["w_down_2"])

        @block.gpsimd
        def _(pool):
            for n, v in (("norm", NORM_EPS), ("gn", GN_EPS), ("ln", LN_EPS), ("kk", 1e-12)):
                pool.memset(eps[n], v)
            pool.memset(proj[:, :, 0:1], 0.0).then_inc(setup_done, 1)
            with pool.Fori(0, DEPTH) as l:
                pool.wait_ge(S["params_ready"], 1)
                pool_mixer(pool, Chain(pool, S["pool_link"]))
                pool.drain()
                pool.wait_ge(arrived, l * 3 + 3)
                pool.sem_inc(over, 1)
                pool.sem_clear(layer_sems)
                pool.sem_inc(cleared, 1)
            pool_second(pool, Chain(pool, S["pool_link"]))

        @block.scalar
        def _(act):
            act.dma_start(x[:, :, :], a["x"][0].rearrange("(t p) n -> p t n", p=P)).then_inc(x_in, 16)
            act.dma_start(cst[:, :], a["consts"]).then_inc(consts_in, 16)
            act.dma_start(hot[:, :], a["hot"]).then_inc(consts_in, 16)
            load_rows(act)
            act.wait_ge(setup_done, 1)
            with act.Fori(0, DEPTH) as l:
                uses = Uses(l, PER_LAYER)
                act_norm(act, 0)
                act.wait_ge(S["params_ready"], 1)
                evac_turn(act, 0, "norm_ffn1", True)
                act_ffn(act, uses, 0)
                act_norm(act, 1)
                evac_turn(act, 1, "norm_mix", True)
                act_mixer(act, Chain(act, S["act_link"]))
                uses.each(SLOTS, 2)
                uses.each(SLOTS[:4])
                act_norm(act, 2)
                evac_turn(act, 2, "norm_ffn2", True)
                act_ffn(act, uses, 1)
                layer_over(act, l)
            act_second(act, Uses(SECOND, PER_LAYER))

        @block.vector
        def _(dve):
            dve.wait_ge(consts_in, 32)
            dve.wait_ge(setup_done, 1)
            with dve.Fori(0, DEPTH) as l:
                uses = Uses(l, PER_LAYER)
                link = Chain(dve, S["dve_link"])
                dve_pick_rows(dve, l)
                dve_norm(dve, 0, link)
                evac_turn(dve, 0, "norm_ffn1", False)
                dve_ffn(dve, uses, 0)
                dve_residual(dve, 0.5)
                dve_norm(dve, 1, link)
                evac_turn(dve, 1, "norm_mix", False)
                dve_proj(dve, uses, 6, start1)
                dve_mixer(dve, uses, link)
                dve_residual(dve, 1.0)
                dve_norm(dve, 2, link)
                evac_turn(dve, 2, "norm_ffn2", False)
                dve_ffn(dve, uses, 1)
                dve_residual(dve, 0.5)
                layer_over(dve, l)
            dve_second(dve, Uses(SECOND, PER_LAYER), Chain(dve, S["dve_link"]))

        @block.tensor
        def _(pe):
            for n in SLOTS:
                pe.sem_inc(used[n], 1)
            pe.wait_ge(consts_in, 32)
            with pe.Fori(0, DEPTH) as l:
                uses = Uses(l, PER_LAYER)
                pe.wait_ge(S["rows_picked"], 1)
                pe.transpose(psum[7][:, 0:NROWS], row_now[0:NROWS, :], ident[0:NROWS, 0:NROWS])\
                  .then_inc(S["params_psum"], 1)
                pe_turn(pe, 0, hN, S["normed"])
                pe_h_ready(pe, 0)
                pe_ffn(pe, uses, 0)
                pe_turn(pe, 1, hN, S["normed"])
                pe_h_ready(pe, 1)
                pe_proj(pe, uses, 6)
                pe_mixer(pe, uses)
                pe_turn(pe, 2, hN, S["normed"])
                pe_h_ready(pe, 2)
                pe_ffn(pe, uses, 1)
                layer_over(pe, l)
            pe_second(pe, Uses(SECOND, PER_LAYER))


INS = ["x", "norm_ffn1", "ffn1_w_gate", "ffn1_w_up", "ffn1_w_down", "norm_mix", "w_in", "shift_mu", "rwkv_w0",
       "rwkv_w2", "rwkv_a0", "rwkv_a2", "rwkv_g2", "rwkv_k_k", "rwkv_k_a", "rwkv_r_k", "rwkv_ln_w", "rwkv_ln_b",
       "attn_q_norm", "attn_k_norm", "conv_dw_w", "conv_dw_b", "conv_ln_w", "conv_ln_b", "w_out", "norm_ffn2",
       "ffn2_w_gate", "ffn2_w_up", "ffn2_w_down", "w_in_2", "conv_w_2", "w_pool_2", "pool_scale_2", "w_out_2",
       "ln1_g_2", "ln1_b_2", "w_up_2", "ffn_conv_w_2", "ffn_conv_b_2", "w_down_2", "ln2_g_2", "ln2_b_2",
       "rel_bias_2"]


def kernel(**inputs):
    import concourse.bacc as bacc
    from concourse.bass_utils import run_bass_kernel_spmd

    nc = bacc.Bacc("TRN2", target_bir_lowering=False, num_devices=1)
    packed, _, hot = constants()
    arrays = {f"in_{n}_dram": np.ascontiguousarray(inputs[n]) for n in INS}
    arrays["in_consts_dram"] = packed
    arrays["in_hot_dram"] = hot
    args = {n: nc.dram_tensor(f"in_{n}_dram", arrays[f"in_{n}_dram"].shape, F32, kind="ExternalInput").ap()
            for n in INS + ["consts", "hot"]}
    out = nc.dram_tensor("out_0_dram", (1, SEQ, D), F32, kind="ExternalOutput").ap()
    build(nc, args, out)
    r = run_bass_kernel_spmd(nc, [arrays], core_ids=[0])
    return r.results[0]["out_0_dram"]
```

```python
from contextlib import ExitStack

import numpy as np

import concourse.bass as bass
from concourse import mybir

F32 = mybir.dt.float32
F32R = mybir.dt.float32r
ALU = mybir.AluOpType
ACT = mybir.ActivationFunctionType
AX = mybir.AxisListType.X

P = 128
SEQ, D, DEPTH = 256, 1024, 2
NT = SEQ // P
KC = D // P
DFF = 2816
DIN = 2944
NCH = DIN // P
DIN2 = 2560
CONV_W = 31
CHUNK = 64
NH1, NH2 = 6, 8
NORM_EPS, GN_EPS, LN_EPS = 1e-6, 64e-5, 1e-5
ALPHA = 2.0 ** 0.25
NEG = -1e30
WORK = 20992
GROUPS = DFF // 256
LOOPS = (GROUPS - 3) // 2
SLOTS = ["gate0", "up0", "down0", "gate1", "up1", "down1"]
KINDS = ["gate", "up", "down"]
assert GROUPS == 11 and NCH == 23 and DEPTH == 2

R, K, V, LORA, AQ, AK, AV, CU, CG = 0, 3, 6, 9, 10, 13, 16, 19, 21
Q2, K2, V2, CB2, CC2, CX2, PI2 = 0, 4, 8, 12, 14, 16, 18


def param_rows():
    rows, at = {}, 0
    for name, n in (("norm_ffn1", 8), ("norm_mix", 8), ("norm_ffn2", 8), ("shift_mu", 10), ("rwkv_w0", 3),
                    ("rwkv_a0", 3), ("rwkv_k_k", 3), ("rwkv_k_a", 3), ("rwkv_r_k", 3), ("rwkv_ln_w", 3),
                    ("rwkv_ln_b", 3), ("conv_dw_w", 2 * CONV_W), ("conv_dw_b", 2), ("conv_ln_w", 2),
                    ("conv_ln_b", 2), ("attn_q_norm", 1), ("attn_k_norm", 1)):
        rows[name] = at
        at += n
    return rows, at


ROWS, NROWS = param_rows()
B_TAP2, B_BIAS, B_CONV, B_POOL, B_ROWS = 0, 44, 88, 94, 96


def constants():
    s = np.arange(P)[:, None]
    t = np.arange(P)[None, :]
    same = lambda n: (s // n == t // n)
    f = lambda m: m.astype(np.float32)
    strict, incl = f((s < t) & same(CHUNK)), f((s <= t) & same(CHUNK))
    parts = {
        "ident": np.eye(P, dtype=np.float32),
        "pair": f(same(64)),
        "mask4": np.concatenate([strict, incl, strict, incl], 1),
        "blk16": f(same(16)),
        "blk32": f(same(32) & ~same(16)),
        "blk64": f(same(64) & ~same(32)),
        "ones": np.ones((P, P), np.float32),
        "scan": np.broadcast_to(f(np.arange(SEQ) % CHUNK != 0), (P, SEQ)),
    }
    dist = (P + s) - np.arange(2 * P)[None, :]
    count = sum(((dist >= 0) & (dist % dil == 0) & (dist <= win)).astype(int)
                for win, dil in ((128, 1), (512, 4), (2048, 16)))
    logc = np.where(count > 0, np.log(np.maximum(count, 1)), NEG)
    slopes = [2.0 ** (-2.0 * (i + 1)) for i in range(4)] + [2.0 ** (-1.0 * (i + 1)) for i in range(8)][0::2][:2]
    parts["bias1"] = np.concatenate([np.where(count > 0, -m * dist + logc, NEG) for m in slopes], 1)
    pos = np.arange(1, SEQ + 1)
    parts["poolw"] = np.concatenate(
        [np.concatenate([np.broadcast_to(1.0 / np.minimum(pos, w), (64, SEQ)) for w in pair], 0)
         for pair in ((2, 4), (8, 16))], 1)
    at, cols = 0, {}
    for name, a in parts.items():
        cols[name] = (at, at + a.shape[1])
        at += a.shape[1]
    packed = np.ascontiguousarray(np.concatenate([np.asarray(a, np.float32) for a in parts.values()], 1))
    d = 255 - np.arange(384)
    n = np.maximum(d, 0)
    nf = np.maximum(n, 1).astype(np.float32)
    large = 16 + (np.log(nf / np.float32(16)) / np.float32(np.log(1024 / 16)) * np.float32(16)).astype(np.int32)
    bucket = np.where(n < 16, n, np.minimum(large, 31))
    hot = np.zeros((33, 384), np.float32)
    hot[bucket, np.arange(384)] = (d >= 0)
    hot[32] = np.where(d < 0, NEG, 0.0)
    return packed, cols, hot


def chain_plan():
    steps = [
        [("copy", "D2", "DT", "D"), ("copy", "D2T", "D", "DT")],
        [("add", "INV", "D2", "INV"), ("copy", "D", "D2T", "D2"), ("copy", "DT", "D2", "D2T")],
        [("add", "INV", "D", "INV"), ("copy", "D2", "DT", "D")],
        [("add", "INV", "D2", "INV"), ("add", "D", "AT", None)],
        [("copy", "D2T", "INV", None), ("copy", "DT", "D", "INV")],
        [("add", "INV", "D2T", "DT"), ("add", "D2", "AT", None)],
        [("copy", "D2T", "INV", None), ("copy", "DT", "D2", "INV")],
        [("add", "INV", "D2T", "DT")],
    ]
    plan, n = [], {"copy": 0, "add": 0}
    last = {}
    for step, products in enumerate(steps):
        for b in range(3):
            written = []
            for kind, dst, lhs, rhs in products:
                needs = [last.get((x, b)) for x in (lhs, rhs) if x]
                plan.append((step, b, kind, n[kind], dst, lhs, rhs, [x for x in needs if x], last.get((dst, b))))
                written.append(((dst, b), (kind, n[kind])))
                n[kind] += 1
            last.update(written)
    return plan


CHAIN = chain_plan()
COPIES, ADDS = (sum(c[2] == k for c in CHAIN) for k in ("copy", "add"))


def build(nc, a, out):
    packed_cols = constants()[1]
    ctx = ExitStack()
    with ctx:
        def sb(name, shape):
            return ctx.enter_context(nc.sbuf_tensor(name, shape, F32))

        loaded = {n: ctx.enter_context(nc.semaphore(f"loaded_{n}")) for n in SLOTS}
        high = {n: ctx.enter_context(nc.semaphore(f"high_{n}")) for n in SLOTS}
        split = {n: ctx.enter_context(nc.semaphore(f"split_{n}")) for n in SLOTS}
        used = {n: ctx.enter_context(nc.semaphore(f"used_{n}")) for n in KINDS}
        arrived = ctx.enter_context(nc.semaphore("arrived"))
        cleared = ctx.enter_context(nc.semaphore("cleared"))
        consts_in = ctx.enter_context(nc.semaphore("consts_in"))
        x_in = ctx.enter_context(nc.semaphore("x_in"))
        rows_in = ctx.enter_context(nc.semaphore("rows_in"))
        second_in = ctx.enter_context(nc.semaphore("second_in"))
        setup_done = ctx.enter_context(nc.semaphore("setup_done"))
        spread_out = ctx.enter_context(nc.semaphore("spread_out"))
        bias_in = ctx.enter_context(nc.semaphore("bias_in"))
        over = ctx.enter_context(nc.semaphore("over"))
        resumed = ctx.enter_context(nc.semaphore("resumed"))
        slot_free = ctx.enter_context(nc.semaphore("slot_free"))
        stored = ctx.enter_context(nc.semaphore("stored"))

        names = """rows_picked params_psum params_ready squares_done rms_root normed turned
            h_high h_low prod_done ff_high mix_high mix_low silu_done ff_ready x_updated x_rounds  proj_ready dve_link
            act_link pool_link shifted lora_acts lora_mm decay_sig iclr_sig gate_copied cum_ready exps_done
            kk_sq kk_sum kk_root rw_ready bonus_sq bonus_mm bonus_ready tok_mm tok_copied_a tok_copied_d
            mats_mm mats_ready a_mm d_ready dt_ready inv_seed copy_mm add_mm copy_done add_done
            pav_mm pav_done mat_mm mat_done sa_mm sa_done st_mm st_done cend_ready y_mm y_copied
            gn_mean gn_centered gn_sq gn_var gn_root mixr_ready
            qk_sq qk_sum qk_root qk_ready score_mm biased maxed exp_done p_ready pt_mm pt_done av_mm mixa_ready
            conv_sig conv_z conv_acc cl_mean cl_sq cl_var cl_root cl_ready mixc_ready
            biasrow_mm spread_ready pool_ready pool_mm taps_act taps_picked lag_done taps_done stats_ready""".split()
        S = {n: ctx.enter_context(nc.semaphore(n)) for n in names}
        layer_sems = range(S[names[0]].num, S[names[-1]].num + 1)
        assert [S[n].num for n in names] == list(layer_sems)

        slot = {n: sb(f"w_{n}", [P, 2048]) for n in SLOTS}
        x = sb("x", [P, NT, D])
        proj = sb("proj", [P, NCH, SEQ + 1])
        mix = sb("mix", [P, KC, SEQ])
        cst = sb("cst", [P, list(packed_cols.values())[-1][1]])
        rows = sb("rows", [P, DEPTH, P])
        row_now = sb("row_now", [P, P])
        par = sb("par", [P, P])
        lora_all = sb("lora_all", [P, DEPTH, 384])
        lora_w = sb("lora_w", [P, 384])
        small = sb("small", [P, 96])
        hot = sb("hot", [33, 384])
        work_at = (nc.sbuf_base + 31) // 32 * 32
        work = sb("work", [P, WORK])
        pair_at = (nc.sbuf_base + 31) // 32 * 32
        hT = [ctx.enter_context(nc.sbuf_tensor(f"hT_{n}", [P, KC, SEQ], F32R)) for n in ("hi", "lo")]
        spare = nc.alloc_sbuf_tensor_at("spare", [P, 2 * KC * SEQ], F32, offset=pair_at)

        def over_work(name, at, *shape):
            return nc.alloc_sbuf_tensor_at(name, [P, *shape], F32R, offset=work_at + 4 * at)

        staged = {n: [over_work(f"{n}_{part}", 4096 * i + 2048 * j, 2048) for j, part in enumerate(("hi", "lo"))]
                  for i, n in enumerate(KINDS)}
        ffT = [over_work(f"ff_{part}", 12288 + 1024 * j, 2, 512) for j, part in enumerate(("hi", "lo"))]
        psum = [ctx.enter_context(nc.psum_tensor(f"bank{i}", [P, 512], F32)) for i in range(8)]

        def area(at, *shape):
            n = int(np.prod(shape))
            v = work[:, at:at + n]
            if len(shape) == 2:
                v = v.rearrange("p (a b) -> p a b", a=shape[0])
            if len(shape) == 3:
                v = v.rearrange("p (a b c) -> p a b c", a=shape[0], b=shape[1])
            if len(shape) == 4:
                v = v.rearrange("p (a b c d) -> p a b c d", a=shape[0], b=shape[1], c=shape[2])
            return v, at + n

        def const(name, parts=slice(0, P)):
            lo, hi = packed_cols[name]
            return cst[parts, lo:hi]

        ident, pairs, ones = const("ident"), const("pair"), const("ones")
        o_ffn = 14336
        silu, o = area(o_ffn, 2, 512)
        prod, o = area(o, 512)
        taps, o = area(o, 2, 2, 512)
        hN, _ = area(o_ffn, NT, D)
        sh, o = area(0, 10, SEQ)
        ar, o = area(o, 3, NT, 2, P)
        bh, o = area(o, 3, SEQ)
        kh, o = area(o, 3, SEQ)
        ec, o = area(o, 3, SEQ)
        tok, o = area(o, 4, NT, 384)
        avtok, o = area(o, NT, 384)
        o_mats = o
        mats, o = area(o, 12, 4, P)
        o_chain = o
        chain = {}
        for n in ("D2", "D2T"):
            chain[n], o = area(o, 12, P)
        gate, o = area(o, 3, SEQ)
        bonus, o = area(o, 3, SEQ)
        assert o <= WORK, o
        blocks = lambda at: spare[:, at:at + 12 * P].rearrange("p (a b) -> p a b", a=12)
        chain |= {"D": blocks(0), "DT": blocks(12 * P), "INV": area(0, 12, P)[0]}
        o = o_mats
        ld, o = area(o, 3, SEQ)
        cum, o = area(o, 3, SEQ)
        ecx, o = area(o, 3, SEQ)
        en, o = area(o, 3, SEQ)
        iclr, o = area(o, 3, SEQ)
        kk, o = area(o, 3, SEQ)
        kmod, o = area(o, 3, SEQ)
        tmp, o = area(o, 3, SEQ)
        lact, o = area(o, SEQ)
        assert o <= o_chain + 2 * 12 * P, o
        qsq = mix[:, 0:6, :]
        logit, o = area(o_mats, 2, 384)
        probT, o = area(o, 2, 384)
        o = o_chain
        pav, o = area(o, NT, 384)
        mat_, o = area(o, NT, 384)
        satok, o = area(o, NT, 384)
        ysb, o = area(o, 3, SEQ)
        assert o <= o_chain + 2 * 12 * P
        nine = lambda at: spare[:, at:at + 9 * P].rearrange("p (a b c) -> p a b c", a=3, b=3)
        state = nine(0)
        cend = nine(9 * P)
        ysq, o = area(12288, 3, SEQ)
        yroot, o = area(o, 3, SEQ)
        par2, o = area(o_ffn + 3584, 4, 44)
        par2c, o = area(o, 8)
        tap_now, o = area(o, 2, 4, 2, 2)
        ln_gb, o = area(o, 2, D)
        assert o <= WORK, o
        bias2, o = area(12288, NH2, 2 * P)
        spread, _ = area(o, NH2, 384)
        rows2, o = area(o_ffn + 3072, 2, P)
        tab, o = area(o, 64)
        assert o <= o_ffn + 3584
        wpool, o = area(20184, 2, P)
        assert o <= WORK
        avtok2, o = area(7680, NT, 512)
        logit2, o = area(o, 2, 384)
        probT2, o = area(o, 2, 384)
        cz, o = area(o, 2, SEQ)
        pl, o = area(o, 3, 2, SEQ)
        assert o <= 12288
        rstd = small[:, 0:8]
        eps = {n: small[:, 8 + i:9 + i] for i, n in enumerate(("norm", "gn", "ln", "kk"))}
        amax, anmax, asum, arec = (small[:, 12 + 16 * i:28 + 16 * i].rearrange("p (h t) -> p h t", t=NT)
                                   for i in range(4))
        lnstat = small[:, 76:88].rearrange("p (a b) -> p a b", a=2)
        lnvar = small[:, 88:92].rearrange("p (a b) -> p a b", a=2)

        block = ctx.enter_context(nc.Block())
        scratch = nc.dram_tensor("bias_scratch", [P, NH2, 384], F32)

        def col(name, i=0):
            c = ROWS[name] + i
            return par[:, c:c + 1]

        class Chain:

            def __init__(self, eng, sem):
                self.eng, self.sem, self.n = eng, sem, 0

            def __call__(self, ins):
                self.n += 1
                ins.then_inc(self.sem, 1)
                self.eng.wait_ge(self.sem, self.n)

        class Uses:

            def __init__(self, layer, per_layer):
                self.base = lambda n: layer * per_layer[n]
                self.n = dict.fromkeys(SLOTS + KINDS, 0)

            def now(self, name, more=0):
                return self.base(name) + (more + self.n[name] + 1)

            def ffn(self):
                for n in SLOTS:
                    self.n[n] += 6 if n.endswith("0") else 5
                for n in KINDS:
                    self.n[n] += GROUPS

            def each(self, names, times=1):
                for n in names:
                    self.n[n] += times
                    self.n[n[:-1]] += times

        PER_LAYER = {n: 2 * (6 if n.endswith("0") else 5) + 2 for n in SLOTS} | {n: 2 * GROUPS + 4 for n in KINDS}
        for n in SLOTS[:4]:
            PER_LAYER[n] += 1
            PER_LAYER[n[:-1]] += 1

        def act_high(act, uses, sl, more=0, more_kind=0):
            kind = sl[:-1]
            act.wait_ge(loaded[sl], uses.now(sl, more) * 16)
            act.wait_ge(used[kind], uses.now(kind, more_kind))
            act.activation(staged[kind][0][:, :], slot[sl][:, :], ACT.Copy).then_inc(high[sl], 1)

        def dve_low(dve, uses, sl, more=0):
            kind = sl[:-1]
            dve.wait_ge(high[sl], uses.now(sl, more))
            dve.tensor_tensor(staged[kind][1][:, :], slot[sl][:, :], staged[kind][0][:, :].bitcast(F32),
                              ALU.subtract).then_inc(split[sl], 1)

        def tile_ready(pe, uses, sl, more=0):
            pe.wait_ge(split[sl], uses.now(sl, more) + 1)

        def products_done(eng, uses, kind, more=0):
            eng.wait_ge(used[kind], uses.now(kind, more) + 1)

        PASSES = ((0, 0), (0, 1), (1, 0))

        def product(pe, out_, lhs, rhs, first, last, **kw):
            for i, (l_, r_) in enumerate(PASSES):
                mm = pe.matmul(out_, lhs(l_), rhs(r_), start=first and i == 0, stop=last and i == 2, **kw)
            return mm

        def fill(sp, uses, name, src, more=0):
            n = uses.now(name, more)
            sp.wait_ge(split[name], n)
            sp.sem_inc(slot_free, 1)
            width = src.shape[2]
            dst = slot[name][:, :].rearrange("p (c n) -> p c n", n=width)
            sp.dma_start(dst, src).then_inc(loaded[name], 16)

        def columns(w, l, start, width=256):
            return w[bass.ds(l, 1), :, bass.ds(start, width)].rearrange("a (c p) n -> p (a c) n", p=P)

        def krows(w, l, start):
            return w[bass.ds(l, 1), bass.ds(start, 256), :].rearrange("a (c p) n -> p (a c) n", p=P)

        def sp_ffn(sp, uses, l, wg, g0, wu, u0, wd):
            def gu(g, par_, more=0):
                fill(sp, uses, f"gate{par_}", columns(wg, l, g * 256 + g0), more)
                fill(sp, uses, f"up{par_}", columns(wu, l, g * 256 + u0), more)

            def dn(g, par_, more=0):
                fill(sp, uses, f"down{par_}", krows(wd, l, g * 256), more)

            gu(0, 0)
            gu(1, 1)
            dn(0, 0)
            with sp.Fori(0, LOOPS) as it:
                gu(it * 2 + 2, 0, it + 1)
                dn(it * 2 + 1, 1, it)
                gu(it * 2 + 3, 1, it + 1)
                dn(it * 2 + 2, 0, it + 1)
            gu(10, 0, LOOPS + 1)
            dn(9, 1, LOOPS)
            dn(10, 0, LOOPS + 1)
            uses.ffn()

        def sp_proj(sp, uses, l, w, per, starts):
            with sp.Fori(0, 2) as it:
                for j in range(per):
                    fill(sp, uses, SLOTS[j], columns(w, l, starts(it, j) * P), it)
            uses.each(SLOTS[:per], 2)

        def sp_out(sp, uses, l, w):
            for j in range(4):
                fill(sp, uses, SLOTS[j], krows(w, l, (3 - j) * 256))
            uses.each(SLOTS[:4])

        def start1(it, j):
            return it * 12 + 2 * j if j < 5 else it * 11 + 10

        def start2(it, j):
            return it * 10 + 2 * j

        def over_groups(eng, body):
            body(0, 0, 0)
            body(1, 1, 0)
            with eng.Fori(0, LOOPS) as it:
                body(it * 2 + 2, 0, it + 1)
                body(it * 2 + 3, 1, it + 1)
            body(10, 0, LOOPS + 1)

        def later(g):
            return not isinstance(g, int) or g >= 2

        def final(g):
            return isinstance(g, int) and g == GROUPS - 1

        def pe_ffn(pe, uses, f, n_norm):
            b = f * GROUPS

            def gu(g, par_, more=0):
                if later(g):
                    pe.wait_ge(S["ff_ready"], g + (b - 1))
                for name, bank in (("gate", psum[par_]), ("up", psum[2 + par_])):
                    tile_ready(pe, uses, f"{name}{par_}", more)
                    w = [t_[:, :].rearrange("p (c n) -> p c n", n=256) for t_ in staged[name]]
                    for j in range(2):
                        for c in range(KC):
                            if isinstance(g, int) and g == 0 and name == "gate" and j == 0:
                                pe.wait_ge(S["h_low"], KC * n_norm + c + 1)
                            mm = product(pe, bank[:, j * SEQ:(j + 1) * SEQ], lambda p_: w[p_][:, c, j * P:(j + 1) * P],
                                         lambda p_: hT[p_][:, c, :], c == 0, c == KC - 1)
                    mm.then_inc(used[name], 1)

            def down(g, par_, more=0, first=False, last=False):
                pe.wait_ge(S["ff_ready"], g + (b + 1))
                tile_ready(pe, uses, f"down{par_}", more)
                w = [t_[:, :].rearrange("p (c n) -> p c n", n=D) for t_ in staged["down"]]
                for j in range(2):
                    for t in range(NT):
                        for h in range(2):
                            at = slice(j * SEQ + t * P, j * SEQ + (t + 1) * P)
                            mm = product(pe, psum[4 + 2 * t + h][:, :], lambda p_: ffT[p_][:, par_, at],
                                         lambda p_: w[p_][:, j, h * 512:(h + 1) * 512], first and j == 0,
                                         last and j == 1, skip_group_check=True)
                mm.then_inc(used["down"], 1)

            gu(0, 0)
            gu(1, 1)
            down(0, 0, first=True)
            with pe.Fori(0, LOOPS) as it:
                gu(it * 2 + 2, 0, it + 1)
                down(it * 2 + 1, 1, it)
                gu(it * 2 + 3, 1, it + 1)
                down(it * 2 + 2, 0, it + 1)
            gu(10, 0, LOOPS + 1)
            down(9, 1, LOOPS)
            down(10, 0, LOOPS + 1, last=True)
            uses.ffn()

        def act_ahead(act, uses):
            act_high(act, uses, "gate0")
            act_high(act, uses, "up0")

        def dve_ahead(dve, uses):
            dve_low(dve, uses, "gate0")
            dve_low(dve, uses, "up0")

        def act_ffn(act, uses, f):
            b = f * GROUPS

            def group(g, par_, more):
                if not final(g):
                    act_high(act, uses, f"gate{1 - par_}", more + par_, g + 1)
                    act_high(act, uses, f"up{1 - par_}", more + par_, g + 1)
                products_done(act, uses, "up", g)
                if later(g):
                    act.wait_ge(S["ff_ready"], g + (b - 1))
                act.activation(silu[:, par_, :], psum[par_][:, :], ACT.Silu).then_inc(S["silu_done"], 1)
                act_high(act, uses, f"down{par_}", more, g)

            over_groups(act, group)
            uses.ffn()

        def dve_hidden(dve, up, par_, g, b, uses):
            if later(g) or g + b:
                dve.wait_ge(S["ff_ready"], g + b)
            dve.tensor_tensor(prod, silu[:, par_, :], up, ALU.mult).then_inc(S["prod_done"], 1)
            dve.wait_ge(S["prod_done"], g + (b + 1))
            if later(g):
                products_done(dve, uses, "down", g - 2)
            dve.tensor_copy(ffT[0][:, par_, :], prod).then_inc(S["ff_high"], 1)
            dve.wait_ge(S["ff_high"], g + (b + 1))
            dve.tensor_tensor(ffT[1][:, par_, :], prod, ffT[0][:, par_, :].bitcast(F32),
                              ALU.subtract).then_inc(S["ff_ready"], 1)

        def dve_ffn(dve, uses, f):
            b = f * GROUPS

            def group(g, par_, more):
                if not final(g):
                    dve_low(dve, uses, f"gate{1 - par_}", more + par_)
                    dve_low(dve, uses, f"up{1 - par_}", more + par_)
                dve.wait_ge(S["silu_done"], g + (b + 1))
                dve_hidden(dve, psum[2 + par_][:, :], par_, g, b, uses)
                dve_low(dve, uses, f"down{par_}", more)

            over_groups(dve, group)
            uses.ffn()

        def dve_residual(dve, uses, scale, kind):
            products_done(dve, uses, kind, -1)
            for t in range(NT):
                for h in range(2):
                    xs = x[:, t, h * 512:(h + 1) * 512]
                    ins = dve.scalar_tensor_tensor(xs, psum[4 + 2 * t + h][:, :], scale, xs, ALU.mult, ALU.add)
            ins.then_inc(S["x_updated"], 1)

        def act_norm(act, n):
            if n == 0:
                act.wait_ge(x_in, 16)
            else:
                act.wait_ge(S["x_updated"], n)
            for t in range(NT):
                act.activation(hN[:, t, :], x[:, t, :], ACT.Square,
                               accum_out=rstd[:, t:t + 1]).then_inc(S["squares_done"], 1)
            act.wait_ge(S["squares_done"], 2 * n + 2)
            act.activation(rstd[:, 2:4], rstd[:, 0:2], ACT.Sqrt, bias=eps["norm"], scale=1.0 / D)\
               .then_inc(S["rms_root"], 1)

        def dve_norm(dve, n, link):
            dve.wait_ge(S["rms_root"], n + 1)
            link(dve.reciprocal(rstd[:, 4:6], rstd[:, 2:4]))
            for t in range(NT):
                dve.tensor_scalar(hN[:, t, :], x[:, t, :], rstd[:, 4 + t:5 + t], None, ALU.mult)\
                   .then_inc(S["normed"], 1)

        def pe_turn(pe, n, src, ready, count=None):
            for c in range(KC):
                for t in range(NT):
                    if ready is not None and c == 0:
                        pe.wait_ge(ready, NT * (n if count is None else count) + t + 1)
                    at = (c % 2) * SEQ + t * P
                    mm = pe.transpose(psum[4 + c // 2][:, at:at + P], src[:, t, c * P:(c + 1) * P], ident)
                if c % 2 == 1:
                    mm.then_inc(S["turned"], 1)

        def act_turned(act, n, gain):
            for c in range(KC):
                if c % 2 == 0:
                    act.wait_ge(S["turned"], KC // 2 * n + c // 2 + 1)
                src = psum[4 + c // 2][:, (c % 2) * SEQ:(c % 2 + 1) * SEQ]
                act.activation(hT[0][:, c, :], src, ACT.Copy, scale=col(gain, c) if gain else 1.0)\
                   .then_inc(S["h_high"], 1)

        def dve_turned(dve, n, gain):
            for c in range(KC):
                dve.wait_ge(S["h_high"], KC * n + (c // 2) * 2 + 2)
                src = psum[4 + c // 2][:, (c % 2) * SEQ:(c % 2 + 1) * SEQ]
                dve.scalar_tensor_tensor(hT[1][:, c, :], src, col(gain, c) if gain else 1.0,
                                         hT[0][:, c, :].bitcast(F32), ALU.mult, ALU.subtract)\
                   .then_inc(S["h_low"], 1)

        def pe_proj(pe, uses, per, n_norm):
            with pe.Fori(0, 2) as it:
                for j in range(per):
                    if j >= 4:
                        pe.wait_ge(S["proj_ready"], it * per + (j - 3))
                    sl = SLOTS[j]
                    tile_ready(pe, uses, sl, it)
                    w = [t_[:, :].rearrange("p (c n) -> p c n", n=256) for t_ in staged[sl[:-1]]]
                    for i in range(2):
                        for c in range(KC):
                            if j == 0 and i == 0:
                                pe.wait_ge(S["h_low"], KC * n_norm + c + 1)
                            mm = product(pe, psum[j][:, i * SEQ:(i + 1) * SEQ], lambda p_: w[p_][:, c, i * P:(i + 1) * P],
                                         lambda p_: hT[p_][:, c, :], c == 0, c == KC - 1)
                    mm.then_inc(used[sl[:-1]], 1)
                pe.wait_ge(S["proj_ready"], it * per + (per - 1 if per < 6 else 4))
            uses.each(SLOTS[:per], 2)

        def body_kind(per, j):
            kinds = [SLOTS[i][:-1] for i in range(per)]
            return kinds.count(kinds[j]), kinds[:j].count(kinds[j])

        def act_proj(act, uses, per):
            with act.Fori(0, 2) as it:
                for j in range(per):
                    a_round, before = body_kind(per, j)
                    act_high(act, uses, SLOTS[j], it, it * a_round + before)
            uses.each(SLOTS[:per], 2)

        def dve_proj(dve, uses, per, starts):
            with dve.Fori(0, 2) as it:
                def copy(j):
                    a_round, before = body_kind(per, j)
                    products_done(dve, uses, SLOTS[j][:-1], it * a_round + before)
                    if j == 5:
                        dve.wait_ge(S["proj_ready"], it * per + 5)
                    dve.tensor_scalar(proj[:, bass.ds(starts(it, j), 2), 1:SEQ + 1],
                                      psum[j][:, :].rearrange("p (a b) -> p a b", a=2), 1.0, None,
                                      ALU.mult).then_inc(S["proj_ready"], 1)

                for j in range(per):
                    dve_low(dve, uses, SLOTS[j], it)
                    if j:
                        copy(j - 1)
                copy(per - 1)
            uses.each(SLOTS[:per], 2)

        def pe_out(pe, uses, ready):
            for k in range(4):
                ready(k)
                tile_ready(pe, uses, SLOTS[k], 0)
                w = [t_[:, :].rearrange("p (c n) -> p c n", n=D) for t_ in staged[SLOTS[k][:-1]]]
                for j in range(2):
                    c = 2 * (3 - k) + j
                    for t in range(NT):
                        for h in range(2):
                            mm = product(pe, psum[4 + 2 * t + h][:, :], lambda p_: hT[p_][:, c, t * P:(t + 1) * P],
                                         lambda p_: w[p_][:, j, h * 512:(h + 1) * 512], k == 0 and j == 0,
                                         k == 3 and j == 1, skip_group_check=True)
                mm.then_inc(used[SLOTS[k][:-1]], 1)
            uses.each(SLOTS[:4])

        def act_mixed(act, lo, hi):
            act.activation(hT[0][:, lo:hi, :], mix[:, lo:hi, :], ACT.Copy).then_inc(S["mix_high"], 1)

        def dve_mixed(dve, lo, hi):
            dve.tensor_tensor(hT[1][:, lo:hi, :], mix[:, lo:hi, :], hT[0][:, lo:hi, :].bitcast(F32),
                              ALU.subtract).then_inc(S["mix_low"], 1)

        def half(h):
            return slice(64 * (h % 2), 64 * (h % 2) + 64)

        def pe_attention(pe, nh, qc, kc, vtok, logit_, probT_):
            def score(h):
                bank, r = psum[h % 4], half(h)
                if h >= 4:
                    pe.wait_ge(S["biased"], h - 3)
                q, k = proj[r, qc + h // 2, 1:], proj[r, kc + h // 2, 1:]
                pe.matmul(bank[:, 0:P], q[:, 0:P], k[:, 0:P], start=True, stop=True)
                pe.matmul(bank[:, P:3 * P], q[:, P:], k, start=True, stop=True).then_inc(S["score_mm"], 1)

            def turn(h):
                pe.wait_ge(S["p_ready"], h + 1)
                if h >= 2:
                    pe.wait_ge(S["pt_done"], h - 1)
                for i in range(3):
                    mm = pe.transpose(psum[4 + h % 2][:, i * P:(i + 1) * P], logit_[:, h % 2, i * P:(i + 1) * P],
                                      ident)
                mm.then_inc(S["pt_mm"], 1)

            def value(h):
                pe.wait_ge(S["pt_done"], h + 1)
                if h % 2 == 0 and h >= 4:
                    pe.wait_ge(S["mixa_ready"], h // 2 - 1)
                bank = psum[6 + (h // 2) % 2]
                v = [vtok[:, t, h * 64:(h + 1) * 64] for t in range(NT)]
                pt = [probT_[:, h % 2, i * P:(i + 1) * P] for i in range(3)]
                pe.matmul(bank[half(h), 0:P], v[0], pt[0], start=True, stop=True)
                pe.matmul(bank[half(h), P:2 * P], v[0], pt[1], start=True, stop=False)
                pe.matmul(bank[half(h), P:2 * P], v[1], pt[2], start=False, stop=True).then_inc(S["av_mm"], 1)

            score(0)
            score(1)
            for h in range(nh):
                if h + 2 < nh:
                    score(h + 2)
                turn(h)
                if h:
                    value(h - 1)
            value(nh - 1)

        def dve_attention(dve, nh, bias, logit_, link):
            def logits(h):
                dve.wait_ge(S["score_mm"], h + 1)
                if h >= 2:
                    dve.wait_ge(S["pt_mm"], h - 1)
                bank, bh_ = psum[h % 4], bias(h)
                dve.scalar_tensor_tensor(logit_[:, h % 2, 0:P], bank[:, 0:P], 0.125, bh_[:, P:2 * P],
                                         ALU.mult, ALU.add)
                dve.scalar_tensor_tensor(logit_[:, h % 2, P:3 * P], bank[:, P:3 * P], 0.125, bh_,
                                         ALU.mult, ALU.add).then_inc(S["biased"], 1)
                dve.wait_ge(S["biased"], h + 1)
                dve.tensor_reduce(amax[:, h, 0:1], logit_[:, h % 2, 0:P], AX, ALU.max)
                link(dve.tensor_reduce(amax[:, h, 1:2], logit_[:, h % 2, P:3 * P], AX, ALU.max))
                dve.tensor_scalar(anmax[:, h, :], amax[:, h, :], -1.0, None, ALU.mult).then_inc(S["maxed"], 1)

            def normalise(h):
                dve.wait_ge(S["exp_done"], 2 * h + 2)
                link(dve.reciprocal(arec[:, h, :], asum[:, h, :]))
                for t, (lo, hi) in enumerate(((0, P), (P, 3 * P))):
                    ins = dve.tensor_scalar(logit_[:, h % 2, lo:hi], logit_[:, h % 2, lo:hi], arec[:, h, t:t + 1],
                                            None, ALU.mult)
                ins.then_inc(S["p_ready"], 1)

            logits(0)
            for h in range(nh):
                if h + 1 < nh:
                    logits(h + 1)
                normalise(h)

        def act_attention(act, nh, logit_, probT_, to):
            def exps(h):
                act.wait_ge(S["maxed"], h + 1)
                for t, (lo, hi) in enumerate(((0, P), (P, 3 * P))):
                    act.activation(logit_[:, h % 2, lo:hi], logit_[:, h % 2, lo:hi], ACT.Exp, bias=anmax[:, h, t:t + 1],
                                   accum_out=asum[:, h, t:t + 1]).then_inc(S["exp_done"], 1)

            def copy(h):
                act.wait_ge(S["pt_mm"], h + 1)
                if h >= 2:
                    act.wait_ge(S["av_mm"], h - 1)
                act.activation(probT_[:, h % 2, :], psum[4 + h % 2][:, 0:384], ACT.Copy).then_inc(S["pt_done"], 1)

            def out_(pair):
                act.wait_ge(S["av_mm"], 2 * pair + 2)
                act.activation(mix[:, to + pair, :], psum[6 + pair % 2][:, 0:SEQ], ACT.Copy)\
                   .then_inc(S["mixa_ready"], 1)

            exps(0)
            for h in range(nh):
                if h + 1 < nh:
                    exps(h + 1)
                copy(h)
                if h % 2 == 0 and h >= 2:
                    out_(h // 2 - 1)
            out_(nh // 2 - 1)

        def prob(t, h):
            return t * NH1 + h

        def bank_pair(c):
            return c // 2, slice((c % 2) * SEQ, (c % 2 + 1) * SEQ)

        def three(first):
            return [(psum[first][:, :].rearrange("p (a b) -> p a b", a=2), slice(0, 2)),
                    (psum[first + 1][:, 0:SEQ].rearrange("p (a b) -> p a b", a=1), slice(2, 3))]

        def ones_product(pe, first, src, mat=pairs):
            flat = src.rearrange("p a b -> p (a b)")
            pe.matmul(psum[first][:, :], mat, flat[:, 0:512], start=True, stop=True)
            return pe.matmul(psum[first + 1][:, 0:SEQ], mat, flat[:, 512:768], start=True, stop=True)

        TOK = [(w, t) for w in range(5) for t in range(NT)]
        TOK_BANK = [5, 6, 7, 0, 1, 2, 5, 6, 7, 0]

        def pe_mixer(pe, uses):
            pe.wait_ge(S["proj_ready"], 12)
            pe.wait_ge(S["lora_acts"], 2)
            for lo, hi, first, src in ((0, 32, 0, lact), (32, 64, 2, None), (64, 128, 4, lact)):
                for c in range(3):
                    b, cols_ = bank_pair(c)
                    rhs = src[lo:hi, :] if src is not None else sh[lo:hi, LORA, :]
                    mm = pe.matmul(psum[first + b][:, cols_], lora_w[lo:hi, c * P:(c + 1) * P], rhs,
                                   start=True, stop=True)
                mm.then_inc(S["lora_mm"], 1)
            pe.wait_ge(S["kk_sq"], 1)
            ones_product(pe, 6, tmp).then_inc(S["kk_sum"], 1)
            pe.wait_ge(S["qk_sq"], 1)
            pe.wait_ge(S["decay_sig"], 3)
            pe.wait_ge(S["iclr_sig"], 3)
            flat = qsq.rearrange("p a b -> p (a b)")
            for i in range(3):
                mm = pe.matmul(psum[i][:, :], pairs, flat[:, i * 512:(i + 1) * 512], start=True, stop=True)
            mm.then_inc(S["qk_sum"], 1)
            pe.wait_ge(S["bonus_sq"], 1)
            pe.wait_ge(S["gate_copied"], 2)
            ones_product(pe, 3, tmp).then_inc(S["bonus_mm"], 1)
            pe.wait_ge(S["rw_ready"], 1)
            pe.wait_ge(S["qk_root"], 1)
            for n, (w, t) in enumerate(TOK):
                if n >= 6:
                    pe.wait_ge(S["tok_copied_a" if n % 2 == 0 else "tok_copied_d"], (n - 6) // 2 + 1)
                for c in range(3):
                    if w == 0:
                        src = ar[:, c, t, 0, :]
                    elif w == 4:
                        src = proj[:, AV + c, 1 + t * P:1 + (t + 1) * P]
                    else:
                        src = (None, bh[:, c], kh[:, c], sh[:, V + c])[w][:, t * P:(t + 1) * P]
                    mm = pe.transpose(psum[TOK_BANK[n]][:, c * P:(c + 1) * P], src, ident)
                mm.then_inc(S["tok_mm"], 1)
            pe.wait_ge(S["qk_ready"], 1)
            pe.wait_ge(S["tok_copied_a"], 5)
            pe.wait_ge(S["tok_copied_d"], 5)
            pe.wait_ge(S["bonus_ready"], 1)
            pe_attention(pe, NH1, AQ, AK, avtok, logit, probT)
            pe.wait_ge(S["mixa_ready"], 3)
            for t in range(NT):
                for h in range(NH1):
                    p, r, c = prob(t, h), half(h), h // 2
                    if p >= 4:
                        pe.wait_ge(S["mats_ready"], p - 3)
                    rhs = ar[r, c, t].rearrange("p a b -> p (a b)")
                    pe.matmul(psum[p % 4][:, 0:256], bh[r, c, t * P:(t + 1) * P], rhs, start=True, stop=True)
                    pe.matmul(psum[p % 4][:, 256:512], kh[r, c, t * P:(t + 1) * P], rhs, start=True,
                              stop=True).then_inc(S["mats_mm"], 1)
                    if p % 4 == 3:
                        b = p // 4
                        pe.wait_ge(S["mats_ready"], p + 1)
                        for i in range(4):
                            mm = pe.transpose(psum[4 + b][:, i * P:(i + 1) * P], mats[:, 4 * b + i, 0, :], ident)
                        mm.then_inc(S["a_mm"], 1)
            for step, b, kind, n, dst, lhs, rhs, needs, _ in CHAIN:
                if step == 0:
                    pe.wait_ge(S["d_ready"], b + 1)
                    pe.wait_ge(S["dt_ready"], b + 1)
                    pe.wait_ge(S["mats_ready"], 12)
                if step == 1 and kind == "add":
                    pe.wait_ge(S["inv_seed"], 1)
                for k_, m in needs:
                    pe.wait_ge(S["copy_done" if k_ == "copy" else "add_done"], m + 1)
                if n >= 4:
                    pe.wait_ge(S["copy_done" if kind == "copy" else "add_done"], n - 3)
                bank = psum[(0 if kind == "copy" else 4) + n % 4]
                for i in range(4):
                    at, q = slice(i * P, (i + 1) * P), 4 * b + i
                    if rhs is None:
                        src = mats[:, q, 0, :] if lhs == "AT" else chain[lhs][:, q, :]
                        mm = pe.transpose(bank[:, at], src, ident)
                    else:
                        mm = pe.matmul(bank[:, at], chain[lhs][:, q, :], chain[rhs][:, q, :], start=True, stop=True)
                mm.then_inc(S["copy_mm" if kind == "copy" else "add_mm"], 1)
            inv = chain["INV"]
            pe.wait_ge(S["copy_done"], COPIES)
            for t in range(NT):
                for h in range(NH1):
                    mm = pe.matmul(psum[t][:, h * 64:(h + 1) * 64], mats[:, prob(t, h), 2, :],
                                   tok[:, 3, t, h * 64:(h + 1) * 64], start=True, stop=True)
                mm.then_inc(S["pav_mm"], 1)
            pe.wait_ge(S["add_done"], ADDS)
            for t in range(NT):
                for h in range(NH1):
                    mm = pe.matmul(psum[2 + t][half(h), (h // 2) * P:(h // 2 + 1) * P],
                                   tok[:, 0, t, h * 64:(h + 1) * 64], inv[:, prob(t, h), :], start=True, stop=True)
                mm.then_inc(S["mat_mm"], 1)
            pe.wait_ge(S["conv_acc"], 1)
            for c in range(2):
                mm = pe.matmul(psum[7][:, 0:SEQ], ones, mix[:, 6 + c, :], start=(c == 0), stop=(c == 1))
            mm.then_inc(S["cl_mean"], 1)
            pe.wait_ge(S["cl_sq"], 1)
            for c in range(2):
                mm = pe.matmul(psum[7][:, SEQ:2 * SEQ], ones, proj[:, CG + c, 1:], start=(c == 0), stop=(c == 1))
            mm.then_inc(S["cl_var"], 1)
            pe.wait_ge(S["cl_root"], 1)
            for ch in range(4):
                t, rows_ = ch // 2, slice(64 * (ch % 2), 64 * (ch % 2) + 64)
                if ch % 2 == 0:
                    pe.wait_ge(S["pav_done"], t + 1)
                    for h in range(NH1):
                        mm = pe.matmul(psum[4 + t][:, h * 64:(h + 1) * 64], inv[:, prob(t, h), :],
                                       pav[:, t, h * 64:(h + 1) * 64], start=(h == 0), stop=True,
                                       skip_group_check=True)
                if ch > 0:
                    pe.wait_ge(S["mat_done"], t + 1)
                    pe.wait_ge(S["st_done"], ch)
                    for pr in range(3):
                        at = slice(pr * P, (pr + 1) * P)
                        mm = pe.matmul(psum[4 + t][rows_, at], mat_[:, t, pr * P + 64 * (ch % 2):pr * P + 64 * (ch % 2) + 64],
                                       state[:, ch - 1, pr, :], start=False, stop=True, skip_group_check=True)
                mm.then_inc(S["sa_mm"], 1)
                if ch == 3:
                    break
                bank = psum[6 + ch % 2]
                for pr in range(3):
                    at = slice(pr * P, (pr + 1) * P)
                    pe.matmul(bank[:, at], tok[rows_, 2, t, at], tok[rows_, 3, t, at], start=(pr == 0), stop=False,
                              skip_group_check=True)
                pe.wait_ge(S["sa_done"], ch + 1)
                for pr in range(3):
                    at = slice(pr * P, (pr + 1) * P)
                    mm = pe.matmul(bank[:, at], tok[rows_, 1, t, at], satok[rows_, t, at], start=False, stop=True,
                                   skip_group_check=True)
                mm.then_inc(S["st_mm"], 1)
            pe.wait_ge(S["sa_done"], 4)
            for c in range(3):
                for t in range(NT):
                    at = slice(t * P, (t + 1) * P)
                    for h in (2 * c, 2 * c + 1):
                        v = slice(h * 64, (h + 1) * 64)
                        pe.matmul(psum[c][half(h), at], satok[:, t, v], mats[:, prob(t, h), 1, :], start=True,
                                  stop=False, skip_group_check=True)
                        pe.matmul(psum[c][half(h), at], tok[:, 3, t, v], mats[:, prob(t, h), 3, :], start=False,
                                  stop=True, skip_group_check=True)
                    for ch in (2 * t, 2 * t + 1):
                        if ch > 0:
                            k = 64 * (ch % 2)
                            mm = pe.matmul(psum[c][:, t * P + k:t * P + k + 64], state[:, ch - 1, c, :],
                                           ar[:, c, t, 1, k:k + 64], start=False, stop=True, skip_group_check=True)
                mm.then_inc(S["y_mm"], 1)
            pe.wait_ge(S["y_copied"], 3)
            ones_product(pe, 2, ysb).then_inc(S["gn_mean"], 1)
            pe.wait_ge(S["gn_sq"], 1)
            ones_product(pe, 0, ysq).then_inc(S["gn_var"], 1)
            pe_out(pe, uses, lambda k: pe.wait_ge(S["mix_low"], 1 if k < 2 else 2))

        def act_mixer(act, uses, link):
            act.wait_ge(S["proj_ready"], 12)
            act.activation(qsq, proj[:, AQ:AQ + 6, 1:], ACT.Square).then_inc(S["qk_sq"], 1)
            act.activation(proj[:, CG:CG + 2, 1:], proj[:, CG:CG + 2, 1:], ACT.Sigmoid).then_inc(S["conv_sig"], 1)
            act.wait_ge(S["shifted"], 10)
            act.activation(lact[0:32, :], sh[0:32, LORA, :], ACT.Tanh).then_inc(S["lora_acts"], 1)
            act.activation(lact[64:128, :], sh[64:128, LORA, :], ACT.Sigmoid).then_inc(S["lora_acts"], 1)
            act.wait_ge(S["lora_mm"], 2)
            for c in range(3):
                b, cols_ = bank_pair(c)
                act.activation(ld[:, c, :], psum[b][:, cols_], ACT.Sigmoid, bias=col("rwkv_w0", c))\
                   .then_inc(S["decay_sig"], 1)
                act.activation(iclr[:, c, :], psum[2 + b][:, cols_], ACT.Sigmoid, bias=col("rwkv_a0", c))\
                   .then_inc(S["iclr_sig"], 1)
            act.wait_ge(S["lora_mm"], 3)
            for v, at in three(4):
                act.activation(gate[:, at, :], v, ACT.Copy).then_inc(S["gate_copied"], 1)
            act.wait_ge(S["kk_sum"], 1)
            for i, (v, at) in enumerate(three(6)):
                ins = act.activation(tmp[:, at, :], v, ACT.Sqrt, bias=eps["kk"])
            ins.then_inc(S["kk_root"], 1)
            act.wait_ge(S["qk_sum"], 1)
            for i in range(3):
                ins = act.activation(qsq[:, 2 * i:2 * i + 2, :], psum[i][:, :].rearrange("p (a b) -> p a b", a=2),
                                     ACT.Sqrt, bias=eps["norm"], scale=1.0 / 64)
            ins.then_inc(S["qk_root"], 1)
            act.wait_ge(S["cum_ready"], 2)
            act.activation(ec, cum, ACT.Exp).then_inc(S["exps_done"], 1)
            act.activation(en, cum, ACT.Exp, scale=-1.0).then_inc(S["exps_done"], 1)
            act.activation(ecx, ld, ACT.Exp).then_inc(S["exps_done"], 1)
            for n in range(0, 10, 2):
                w, t = TOK[n]
                act.wait_ge(S["tok_mm"], n + 1)
                dst = tok[:, w, t, :] if w < 4 else avtok[:, t, 0:384]
                act.activation(dst, psum[TOK_BANK[n]][:, 0:384], ACT.Copy).then_inc(S["tok_copied_a"], 1)
            act_attention(act, NH1, logit, probT, 3)
            for step, b, kind, n, dst, *_ in CHAIN:
                if kind == "copy":
                    act.wait_ge(S["copy_mm"], n + 1)
                    act.activation(chain[dst][:, 4 * b:4 * b + 4, :],
                                   psum[n % 4][:, :].rearrange("p (a b) -> p a b", a=4), ACT.Copy)\
                       .then_inc(S["copy_done"], 1)
            for t in range(NT):
                act.wait_ge(S["pav_mm"], t + 1)
                act.activation(pav[:, t, :], psum[t][:, 0:384], ACT.Copy).then_inc(S["pav_done"], 1)
            for t in range(NT):
                act.wait_ge(S["mat_mm"], t + 1)
                act.activation(mat_[:, t, :], psum[2 + t][:, 0:384], ACT.Copy).then_inc(S["mat_done"], 1)
            act.wait_ge(S["cl_var"], 1)
            act.activation(proj[:, CG, 1:], psum[7][:, SEQ:], ACT.Sqrt, bias=eps["ln"], scale=1.0 / 256)\
               .then_inc(S["cl_root"], 1)
            for ch in range(4):
                t, rows_ = ch // 2, slice(64 * (ch % 2), 64 * (ch % 2) + 64)
                act.wait_ge(S["sa_mm"], ch + 1)
                act.activation(satok[rows_, t, :], psum[4 + t][rows_, 0:384], ACT.Copy).then_inc(S["sa_done"], 1)
            act.wait_ge(S["cl_ready"], 1)
            for c in range(2):
                act.activation(mix[:, 6 + c, :], mix[:, 6 + c, :], ACT.Silu, bias=col("conv_ln_b", c),
                               scale=col("conv_ln_w", c)).then_inc(S["mixc_ready"], 1)
            for c in range(3):
                act.wait_ge(S["y_mm"], c + 1)
                act.activation(ysb[:, c, :], psum[c][:, 0:SEQ], ACT.Copy).then_inc(S["y_copied"], 1)
            act.wait_ge(S["mixc_ready"], 2)
            act_mixed(act, 3, KC)
            act_high(act, uses, SLOTS[0])
            act.wait_ge(S["gn_var"], 1)
            for v, at in three(0):
                ins = act.activation(yroot[:, at, :], v, ACT.Sqrt, bias=eps["gn"], scale=1.0 / 64)
            ins.then_inc(S["gn_root"], 1)
            act_high(act, uses, SLOTS[1])
            act_high(act, uses, SLOTS[2])
            act.wait_ge(S["mixr_ready"], 1)
            act_mixed(act, 0, 3)
            act_high(act, uses, SLOTS[3], 0, 1)
            uses.each(SLOTS[:4])

        def dve_mixer(dve, uses, link):
            mult, add, sub = ALU.mult, ALU.add, ALU.subtract
            dve.wait_ge(S["proj_ready"], 12)
            link(dve.tensor_tensor(sh, proj[:, 0:10, 0:SEQ], proj[:, 0:10, 1:], sub))
            for c in (9, 3, 4, 5, 0, 1, 2, 6, 7, 8):
                dve.scalar_tensor_tensor(sh[:, c, :], sh[:, c, :], col("shift_mu", c), proj[:, c, 1:], mult, add)\
                   .then_inc(S["shifted"], 1)
            dve.wait_ge(S["shifted"], 10)
            for c in range(3):
                ins = dve.tensor_scalar(kk[:, c, :], sh[:, K + c, :], col("rwkv_k_k", c), None, mult)
            link(ins)
            dve.tensor_tensor(tmp, kk, kk, mult).then_inc(S["kk_sq"], 1)
            dve.wait_ge(S["decay_sig"], 3)
            link(dve.tensor_scalar(ld, ld, -float(np.exp(-0.5)), None, mult))
            for c in range(3):
                ins = dve.tensor_tensor_scan(cum[:, c, :], const("scan"), ld[:, c, :], 0.0, mult, add)
            ins.then_inc(S["cum_ready"], 1)
            dve.wait_ge(S["cum_ready"], 1)
            dve.tensor_tensor(ld, cum, ld, sub).then_inc(S["cum_ready"], 1)
            dve.wait_ge(S["iclr_sig"], 3)
            for c in range(3):
                ins = dve.tensor_scalar(kmod[:, c, :], iclr[:, c, :], 1.0, col("rwkv_k_a", c), sub, mult)
            link(ins)
            link(dve.scalar_tensor_tensor(kmod, kmod, 1.0, sh[:, K:K + 3, :], add, mult))
            dve.wait_ge(S["kk_root"], 1)
            link(dve.reciprocal(tmp, tmp))
            link(dve.tensor_tensor(kk, kk, tmp, mult))
            link(dve.tensor_tensor(iclr, kk, iclr, mult))
            for c in range(3):
                ins = dve.scalar_tensor_tensor(tmp[:, c, :], sh[:, R + c, :], col("rwkv_r_k", c), kmod[:, c, :],
                                               mult, mult)
            ins.then_inc(S["bonus_sq"], 1)
            dve.wait_ge(S["exps_done"], 3)
            v4 = lambda a_: a_.rearrange("p c (t k) -> p c t k", t=NT)
            dve.scalar_tensor_tensor(ar[:, :, :, 0, :], v4(kk), -1.0, v4(ecx), mult, mult)
            dve.tensor_tensor(ar[:, :, :, 1, :], v4(sh[:, R:R + 3, :]), v4(ec), mult)
            dve.tensor_tensor(bh, iclr, en, mult)
            dve.tensor_tensor(kh, kmod, en, mult).then_inc(S["rw_ready"], 1)
            dve.wait_ge(S["qk_root"], 1)
            link(dve.reciprocal(qsq, qsq))
            for c in range(6):
                ins = dve.scalar_tensor_tensor(proj[:, AQ + c, 1:], proj[:, AQ + c, 1:],
                                               col("attn_q_norm" if c < 3 else "attn_k_norm"), qsq[:, c, :],
                                               mult, mult)
            ins.then_inc(S["qk_ready"], 1)
            dve.wait_ge(S["bonus_mm"], 1)
            for v, at in three(3):
                ins = dve.tensor_tensor(bonus[:, at, :], v, sh[:, V + at.start:V + at.stop, :], mult)
            ins.then_inc(S["bonus_ready"], 1)
            for n in range(1, 10, 2):
                w, t = TOK[n]
                dve.wait_ge(S["tok_mm"], n + 1)
                dst = tok[:, w, t, :] if w < 4 else avtok[:, t, 0:384]
                dve.tensor_copy(dst, psum[TOK_BANK[n]][:, 0:384]).then_inc(S["tok_copied_d"], 1)
            bias1 = const("bias1")
            dve_attention(dve, NH1, lambda h: bias1[:, h * 256:(h + 1) * 256], logit, link)
            m4 = const("mask4")
            blk = const("blk16").unsqueeze(1).broadcast_to([P, 4, P])
            for p in range(12):
                dve.wait_ge(S["mats_mm"], p + 1)
                dve.tensor_tensor(mats[:, p].rearrange("p a b -> p (a b)"), psum[p % 4][:, :], m4, mult)\
                   .then_inc(S["mats_ready"], 1)
                if p % 4 == 3:
                    b = p // 4
                    dve.wait_ge(S["a_mm"], b + 1)
                    dve.wait_ge(S["mats_ready"], p + 1)
                    dve.tensor_tensor(chain["D"][:, 4 * b:4 * b + 4, :],
                                      psum[4 + b][:, :].rearrange("p (a b) -> p a b", a=4), blk, mult)\
                       .then_inc(S["d_ready"], 1)
                    dve.tensor_tensor(chain["DT"][:, 4 * b:4 * b + 4, :], mats[:, 4 * b:4 * b + 4, 0, :], blk, mult)\
                       .then_inc(S["dt_ready"], 1)
            dve.wait_ge(S["dt_ready"], 3)
            dve.tensor_tensor(chain["INV"], chain["DT"], ident.unsqueeze(1).broadcast_to([P, 12, P]), add)\
               .then_inc(S["inv_seed"], 1)
            for step, b, kind, n, dst, _, _, _, before in CHAIN:
                if kind == "add":
                    dve.wait_ge(S["add_mm"], n + 1)
                    src = psum[4 + n % 4][:, :].rearrange("p (a b) -> p a b", a=4)
                    to = chain[dst][:, 4 * b:4 * b + 4, :]
                    if dst == "INV":
                        if before is None:
                            dve.wait_ge(S["inv_seed"], 1)
                        else:
                            dve.wait_ge(S["add_done"], before[1] + 1)
                        ins = dve.tensor_tensor(to, src, to, add)
                    else:
                        if before[0] == "copy":
                            dve.wait_ge(S["copy_done"], before[1] + 1)
                        blk = const("blk32" if dst == "D" else "blk64").unsqueeze(1).broadcast_to([P, 4, P])
                        ins = dve.tensor_tensor(to, src, blk, mult)
                    ins.then_inc(S["add_done"], 1)
            dve.wait_ge(S["cl_mean"], 1)
            for c in range(2):
                ins = dve.scalar_tensor_tensor(mix[:, 6 + c, :], psum[7][:, 0:SEQ], -1.0 / 256, mix[:, 6 + c, :],
                                               mult, add)
            link(ins)
            dve.tensor_tensor(proj[:, CG:CG + 2, 1:], mix[:, 6:8, :], mix[:, 6:8, :], mult).then_inc(S["cl_sq"], 1)
            dve.wait_ge(S["cl_root"], 1)
            link(dve.reciprocal(proj[:, CG + 1, 1:], proj[:, CG, 1:]))
            for c in range(2):
                ins = dve.tensor_tensor(mix[:, 6 + c, :], mix[:, 6 + c, :], proj[:, CG + 1, 1:], mult)
            ins.then_inc(S["cl_ready"], 1)
            for ch in range(3):
                dve.wait_ge(S["st_mm"], ch + 1)
                src = psum[6 + ch % 2][:, 0:384].rearrange("p (a b) -> p a b", a=3)
                if ch == 0:
                    dve.wait_ge(S["cend_ready"], 3)
                    dve.tensor_tensor(state[:, 0], src, cend[:, 0], mult).then_inc(S["st_done"], 1)
                else:
                    link(dve.tensor_tensor(state[:, ch], src, state[:, ch - 1], add))
                    dve.tensor_tensor(state[:, ch], state[:, ch], cend[:, ch], mult).then_inc(S["st_done"], 1)
                dve.wait_ge(S["st_done"], ch + 1)
            dve.wait_ge(S["gn_mean"], 1)
            for v, at in three(2):
                ins = dve.scalar_tensor_tensor(ysb[:, at, :], v, -1.0 / 64, ysb[:, at, :], mult, add)
            link(ins)
            dve.tensor_tensor(ysq, ysb, ysb, mult).then_inc(S["gn_sq"], 1)
            dve.wait_ge(S["mix_high"], 1)
            dve_mixed(dve, 3, KC)
            dve_low(dve, uses, SLOTS[0])
            dve.wait_ge(S["gn_root"], 1)
            link(dve.reciprocal(yroot, yroot))
            link(dve.tensor_tensor(ysb, ysb, yroot, mult))
            for c in range(3):
                ins = dve.tensor_scalar(ysb[:, c, :], ysb[:, c, :], col("rwkv_ln_w", c), col("rwkv_ln_b", c),
                                        mult, add)
            link(ins)
            link(dve.tensor_tensor(ysb, ysb, bonus, add))
            dve.tensor_tensor(mix[:, 0:3, :], ysb, gate, mult).then_inc(S["mixr_ready"], 1)
            dve_low(dve, uses, SLOTS[1])
            dve.wait_ge(S["mix_high"], 2)
            dve_mixed(dve, 0, 3)
            dve_low(dve, uses, SLOTS[2])
            dve_low(dve, uses, SLOTS[3])
            uses.each(SLOTS[:4])

        def pool_mixer(pool, link):
            mult, add = ALU.mult, ALU.add
            z = proj[:, CU:CU + 2, 1:]
            pool.wait_ge(S["conv_sig"], 1)
            link(pool.tensor_tensor(z, z, proj[:, CG:CG + 2, 1:], mult))
            for c in range(2):
                ins = pool.tensor_scalar(mix[:, 6 + c, :], z[:, c, :], col("conv_dw_w", 2 * (CONV_W - 1) + c),
                                         col("conv_dw_b", c), mult, add)
            link(ins)
            part = proj[:, CG:CG + 2, 1:]
            for lag in range(1, CONV_W):
                for c in range(2):
                    ins = pool.tensor_scalar(part[:, c, lag:], z[:, c, 0:SEQ - lag],
                                             col("conv_dw_w", 2 * (CONV_W - 1 - lag) + c), None, mult)
                link(ins)
                ins = pool.tensor_tensor(mix[:, 6:8, lag:], mix[:, 6:8, lag:], part[:, :, lag:], add)
                if lag < CONV_W - 1:
                    link(ins)
            ins.then_inc(S["conv_acc"], 1)
            pool.wait_ge(S["add_done"], ADDS)
            pool.wait_ge(S["exps_done"], 1)
            for ch in range(3):
                end = ec[:, :, (ch + 1) * CHUNK - 1:(ch + 1) * CHUNK].broadcast_to([P, 3, P])
                pool.tensor_tensor(cend[:, ch], end, pairs.unsqueeze(1).broadcast_to([P, 3, P]), mult)\
                    .then_inc(S["cend_ready"], 1)

        def dve_pick_rows(dve, l):
            dve.wait_ge(rows_in, 16 * N_ROW_DMAS)
            one = lambda a_: a_.rearrange("p a b -> p (a b)")
            dve.tensor_scalar(row_now[0:NROWS, :], one(rows[0:NROWS, bass.ds(l, 1), :]), 1.0, None, ALU.mult)\
               .then_inc(S["rows_picked"], 1)
            dve.tensor_scalar(lora_w[:, :], one(lora_all[:, bass.ds(l, 1), :]), 1.0, None, ALU.mult)\
               .then_inc(S["rows_picked"], 1)
            dve.wait_ge(S["params_psum"], 1)
            dve.tensor_copy(par[:, 0:NROWS], psum[7][:, 0:NROWS]).then_inc(S["params_ready"], 1)
            dve.wait_ge(S["params_ready"], 1)

        ROW_SOURCES = [(ROWS[n], a[n].rearrange("l (r p) -> r l p", p=P)) for n in
                       ("norm_ffn1", "norm_mix", "norm_ffn2", "shift_mu", "rwkv_w0", "rwkv_a0", "rwkv_k_k",
                        "rwkv_k_a", "rwkv_ln_w", "rwkv_ln_b", "conv_dw_b", "conv_ln_w", "conv_ln_b")]
        ROW_SOURCES += [(ROWS["rwkv_r_k"], a["rwkv_r_k"].rearrange("l (r h) p -> r l (h p)", h=2)),
                        (ROWS["conv_dw_w"], None)]
        LORAS = (("rwkv_w2", 0, 32), ("rwkv_a2", 32, 64), ("rwkv_g2", 64, 128))
        N_ROW_DMAS = len(ROW_SOURCES) - 1 + DEPTH + 4 + len(LORAS)

        def load_rows(eng):
            n = 0
            for at, src in ROW_SOURCES:
                if src is None:
                    for l in range(DEPTH):
                        eng.dma_start(rows[at:at + 2 * CONV_W, l, :],
                                      a["conv_dw_w"][l].rearrange("j (c p) -> (j c) p", p=P)).then_inc(rows_in, 16)
                        n += 1
                else:
                    eng.dma_start(rows[at:at + src.shape[0], :, :], src).then_inc(rows_in, 16)
                    n += 1
            for name in ("attn_q_norm", "attn_k_norm"):
                for half_ in range(2):
                    eng.dma_start(rows[ROWS[name]:ROWS[name] + 1, :, half_ * 64:half_ * 64 + 64],
                                  a[name].rearrange("(o l) k -> o l k", o=1)).then_inc(rows_in, 16)
                    n += 1
            for name, lo, hi in LORAS:
                eng.dma_start(lora_all[lo:hi, :, :], a[name].rearrange("l k n -> k l n")).then_inc(rows_in, 16)
                n += 1
            assert n == N_ROW_DMAS

        def layer_over(eng, l):
            eng.drain().then_inc(arrived, 1)
            eng.wait_ge(cleared, l + 1)
            eng.sem_inc(resumed, 1)

        N_SECOND = 5 + 1 + 4
        SECOND = DEPTH

        def act_second_loads(act):
            w3, b1_, cw, ps = a["ffn_conv_w_2"], a["ffn_conv_b_2"], a["conv_w_2"], a["pool_scale_2"]
            act.wait_ge(S["pool_link"], 2)
            for dst, src in ((rows2[0:88, 0, :], w3[0, 0:2].rearrange("j (c p) -> (j c) p", p=P)),
                             (rows2[0:44, 1, :], w3[0, 2].rearrange("(c p) -> c p", p=P)),
                             (rows2[44:88, 1, :], b1_[0].rearrange("(c p) -> c p", p=P)),
                             (rows2[88:94, 1, :], cw[0].rearrange("j (c p) -> (j c) p", p=P)),
                             (rows2[94:96, 1, :], ps[0].rearrange("(c p) -> c p", p=P)),
                             (tab[0:NH2, 32:64], a["rel_bias_2"])):
                act.dma_start(dst, src).then_inc(second_in, 16)
            for g in range(4):
                lo = 64 * (g % 2)
                act.dma_start(wpool[lo:lo + 64, g // 2, lo:lo + 64], a["w_pool_2"][0, g]).then_inc(second_in, 16)

        def load_ln(eng, g, b):
            for i, n in enumerate((g, b)):
                eng.dma_start(ln_gb[:, i, :], a[n].broadcast_to([P, D])).then_inc(x_in, 16)

        def pe_second(pe, uses):
            pe_turn(pe, 0, x, None)
            pe.wait_ge(second_in, 16 * N_SECOND)
            pe.transpose(psum[0][:, 0:88], rows2[0:88, 0, :], ident[0:88, 0:88])
            pe.transpose(psum[0][:, 128:128 + B_ROWS], rows2[0:B_ROWS, 1, :], ident[0:B_ROWS, 0:B_ROWS])
            pe.transpose(psum[0][0:32, 256:256 + NH2], tab[0:NH2, 32:64], ident[0:NH2, 0:NH2])\
              .then_inc(S["params_psum"], 1)
            pe.wait_ge(S["params_ready"], 1)
            for h in range(NH2):
                if h >= 2:
                    pe.wait_ge(S["spread_ready"], h - 1)
                pe.matmul(psum[1 + h % 2][:, 0:384], tab[0:33, h:h + 1].broadcast_to([33, P]), hot[:, :],
                          start=True, stop=True).then_inc(S["biasrow_mm"], 1)
            pe.wait_ge(S["spread_ready"], NH2)
            pe_proj(pe, uses, 5, 0)
            pe.wait_ge(S["proj_ready"], 10)
            pe.wait_ge(S["spread_ready"], NH2)
            for t in range(NT):
                for c in range(4):
                    mm = pe.transpose(psum[6 + t][:, c * P:(c + 1) * P], proj[:, V2 + c, 1 + t * P:1 + (t + 1) * P],
                                      ident)
                mm.then_inc(S["tok_mm"], 1)
            pe.wait_ge(S["tok_copied_a"], 2)
            pe_attention(pe, NH2, Q2, K2, avtok2, logit2, probT2)
            pe.wait_ge(S["pool_ready"], 1)
            pe.wait_ge(S["mixa_ready"], 4)
            for c in range(2):
                mm = pe.matmul(psum[c][:, 0:SEQ], wpool[:, c, :], pl[:, 0, c, :], start=True, stop=True)
            mm.then_inc(S["pool_mm"], 1)
            pe_out(pe, uses, lambda k: pe.wait_ge(S["mix_low"], 1 if k < 2 else 2))
            pe_turn(pe, 1, x, S["normed"], count=0)
            pe_ffn(pe, uses, 0, 1)

        def act_second(act, uses):
            act_second_loads(act)
            load_ln(act, "ln1_g_2", "ln1_b_2")
            act_turned(act, 0, None)
            for h in range(NH2):
                act.wait_ge(S["biasrow_mm"], h + 1)
                act.activation(spread[:, h, :], psum[1 + h % 2][:, 0:384], ACT.Copy).then_inc(S["spread_ready"], 1)
            act.wait_ge(S["spread_ready"], NH2)
            act.dma_start(scratch.ap(), spread).then_inc(spread_out, 16)
            act.wait_ge(spread_out, 16)
            pitch = NH2 * 384
            act.dma_start(bias2, bass.AP(scratch, P - 1, [[pitch - 1, P], [384, NH2], [1, 2 * P]]))\
               .then_inc(bias_in, 16)
            act_proj(act, uses, 5)
            for t in range(NT):
                act.wait_ge(S["tok_mm"], t + 1)
                act.activation(avtok2[:, t, :], psum[6 + t][:, :], ACT.Copy).then_inc(S["tok_copied_a"], 1)
            act_attention(act, NH2, logit2, probT2, 0)
            act.wait_ge(S["pool_mm"], 1)
            for c in range(2):
                ins = act.activation(mix[:, 6 + c, :], psum[c][:, 0:SEQ], ACT.Copy, scale=par2c[:, 6 + c:7 + c])
            ins.then_inc(S["mixr_ready"], 1)
            act.wait_ge(S["mixr_ready"], 1)
            act.wait_ge(S["mixc_ready"], 1)
            act_mixed(act, 4, KC)
            act_high(act, uses, SLOTS[0])
            act.wait_ge(S["mixa_ready"], 4)
            act_mixed(act, 0, 4)
            act_high(act, uses, SLOTS[1])
            act_high(act, uses, SLOTS[2])
            act_high(act, uses, SLOTS[3], 0, 1)
            uses.each(SLOTS[:4])
            act_ahead(act, uses)
            act_ln(act, 0)
            act.wait_ge(S["normed"], NT)
            load_ln(act, "ln2_g_2", "ln2_b_2")
            act_turned(act, 1, None)

            def group(g, par_, more):
                if not final(g):
                    act_high(act, uses, f"gate{1 - par_}", more + par_, g + 1)
                    act_high(act, uses, f"up{1 - par_}", more + par_, g + 1)
                products_done(act, uses, "up", g)
                act.wait_ge(S["taps_picked"], g + 1)
                if later(g):
                    act.wait_ge(S["ff_ready"], g - 1)
                for q, bank in enumerate((psum[2 + par_], psum[par_])):
                    for j in range(2):
                        at = slice(j * SEQ, (j + 1) * SEQ)
                        ins = act.activation(taps[:, par_, q, at], bank[:, at], ACT.Identity,
                                             bias=tap_now[:, par_, 3, q, j:j + 1],
                                             scale=tap_now[:, par_, 2, q, j:j + 1])
                ins.then_inc(S["taps_act"], 1)
                act.wait_ge(S["taps_done"], g + 1)
                act.activation(silu[:, par_, :], taps[:, par_, 1, :], ACT.Silu).then_inc(S["silu_done"], 1)
                act_high(act, uses, f"down{par_}", more, g)

            over_groups(act, group)
            uses.ffn()
            act_ln(act, 1)
            act.wait_ge(S["normed"], 2 * NT)
            act.dma_start(out[0].rearrange("(t p) n -> p t n", p=P), x[:, :, :]).then_inc(stored, 16)
            act.wait_ge(stored, 16)

        def act_ln(act, n):
            for t in range(NT):
                act.wait_ge(S["stats_ready"], NT * n + t + 1)
                act.activation(rstd[:, t:t + 1], lnvar[:, t, 1:2], ACT.Sqrt, bias=eps["ln"])\
                   .then_inc(S["rms_root"], 1)

        def dve_ln(dve, n, link):
            for t in range(NT):
                for h in range(2):
                    xs = x[:, t, h * 512:(h + 1) * 512]
                    ins = dve.scalar_tensor_tensor(xs, xs, ALPHA, psum[4 + 2 * t + h][:, :], ALU.mult, ALU.add)
                link(ins)
                for h in range(2):
                    ins = dve.bn_stats(lnstat[:, h, :], x[:, t, h * 512:(h + 1) * 512])
                link(ins)
                dve.bn_aggr(lnvar[:, t, :], lnstat).then_inc(S["stats_ready"], 1)
                dve.wait_ge(S["stats_ready"], NT * n + t + 1)
            dve.wait_ge(x_in, 16 * (1 + 2 * n + 2))
            for t in range(NT):
                dve.wait_ge(S["rms_root"], NT * n + t + 1)
                link(dve.reciprocal(rstd[:, 4 + t:5 + t], rstd[:, t:t + 1]))
                link(dve.tensor_scalar(x[:, t, :], x[:, t, :], lnvar[:, t, 0:1], rstd[:, 4 + t:5 + t],
                                       ALU.subtract, ALU.mult))
                link(dve.tensor_tensor(x[:, t, :], x[:, t, :], ln_gb[:, 0, :], ALU.mult))
                dve.tensor_tensor(x[:, t, :], x[:, t, :], ln_gb[:, 1, :], ALU.add).then_inc(S["normed"], 1)

        def dve_second(dve, uses, link):
            dve_turned(dve, 0, None)
            dve.wait_ge(S["params_psum"], 1)
            dve.tensor_copy(par2[:, 0:2, :].rearrange("p a b -> p (a b)"), psum[0][:, 0:88])
            dve.tensor_copy(par2[:, 2:4, :].rearrange("p a b -> p (a b)"), psum[0][:, 128:216])
            dve.tensor_copy(tab[0:32, 0:NH2], psum[0][0:32, 256:256 + NH2])
            dve.tensor_copy(par2c, psum[0][:, 216:224]).then_inc(S["params_ready"], 1)
            dve_proj(dve, uses, 5, start2)
            dve.wait_ge(bias_in, 16)
            dve_attention(dve, NH2, lambda h: bias2[:, h, :], logit2, link)
            dve.wait_ge(S["mix_high"], 1)
            dve_mixed(dve, 4, KC)
            dve_low(dve, uses, SLOTS[0])
            dve.wait_ge(S["mix_high"], 2)
            dve_mixed(dve, 0, 4)
            for k in range(1, 4):
                dve_low(dve, uses, SLOTS[k])
            uses.each(SLOTS[:4])
            products_done(dve, uses, "gate", -1)
            dve_ln(dve, 0, link)
            dve_ahead(dve, uses)
            dve_turned(dve, 1, None)
            view = par2.rearrange("p k (q u) -> p k q u", q=2)

            def group(g, par_, more):
                if not final(g):
                    dve_low(dve, uses, f"gate{1 - par_}", more + par_)
                    dve_low(dve, uses, f"up{1 - par_}", more + par_)
                if later(g):
                    dve.wait_ge(S["taps_act"], g - 1)
                dve.tensor_scalar(tap_now[:, par_], view[:, :, :, bass.ds(g * 2, 2)], 1.0, None,
                                  ALU.mult).then_inc(S["taps_picked"], 1)
                dve.wait_ge(S["taps_picked"], g + 1)
                dve.wait_ge(S["taps_act"], g + 1)
                for lag in (1, 2):
                    for q, bank in enumerate((psum[2 + par_], psum[par_])):
                        for j in range(2):
                            to = taps[:, par_, q, j * SEQ + lag:(j + 1) * SEQ]
                            ins = dve.scalar_tensor_tensor(to, bank[:, j * SEQ:(j + 1) * SEQ - lag],
                                                           tap_now[:, par_, 2 - lag, q, j:j + 1], to,
                                                           ALU.mult, ALU.add)
                    ins.then_inc(S["lag_done" if lag == 1 else "taps_done"], 1)
                    if lag == 1:
                        dve.wait_ge(S["lag_done"], g + 1)
                dve.wait_ge(S["silu_done"], g + 1)
                dve_hidden(dve, taps[:, par_, 0, :], par_, g, 0, uses)
                dve_low(dve, uses, f"down{par_}", more)

            over_groups(dve, group)
            uses.ffn()
            products_done(dve, uses, "down", -1)
            dve_ln(dve, 1, link)

        def pool_second(pool, link):
            mult, add = ALU.mult, ALU.add
            link(pool.memset(wpool, 0.0))
            link(pool.memset(tab[32:33, 0:NH2], 1.0))
            pool.wait_ge(S["proj_ready"], 10)
            pool.wait_ge(S["params_ready"], 1)
            link(pool.tensor_tensor(cz, proj[:, CC2:CC2 + 2, 1:], proj[:, CX2:CX2 + 2, 1:], mult))
            for c in range(2):
                ins = pool.tensor_scalar(mix[:, 4 + c, :], cz[:, c, :], par2c[:, 4 + c:5 + c], None, mult)
            link(ins)
            part = proj[:, CC2:CC2 + 2, 1:]
            for lag in (1, 2):
                for c in range(2):
                    i = 2 * (2 - lag) + c
                    ins = pool.tensor_scalar(part[:, c, lag:], cz[:, c, 0:SEQ - lag], par2c[:, i:i + 1], None, mult)
                link(ins)
                link(pool.tensor_tensor(mix[:, 4:6, lag:], mix[:, 4:6, lag:], part[:, :, lag:], add))
            pool.tensor_tensor(mix[:, 4:6, :], mix[:, 4:6, :], proj[:, CB2:CB2 + 2, 1:], mult)\
                .then_inc(S["mixc_ready"], 1)
            p_ = proj[:, PI2:PI2 + 2, 1:]
            u, v = pl[:, 0], pl[:, 1]
            link(pool.tensor_copy(u, p_))
            link(pool.tensor_tensor(u[:, :, 1:], u[:, :, 1:], p_[:, :, 0:SEQ - 1], add))
            link(pool.tensor_copy(v, u))
            link(pool.tensor_tensor(v[64:P, 0, 2:], v[64:P, 0, 2:], u[64:P, 0, 0:SEQ - 2], add))
            link(pool.tensor_tensor(v[:, 1, 2:], v[:, 1, 2:], u[:, 1, 0:SEQ - 2], add))
            link(pool.tensor_copy(u, v))
            link(pool.tensor_tensor(u[:, 1, 4:], u[:, 1, 4:], v[:, 1, 0:SEQ - 4], add))
            link(pool.tensor_copy(v, u))
            link(pool.tensor_tensor(v[64:P, 1, 8:], v[64:P, 1, 8:], u[64:P, 1, 0:SEQ - 8], add))
            link(pool.tensor_tensor(v, v, const("poolw").rearrange("p (a b) -> p a b", a=2), mult))
            pool.tensor_tensor(u, v, p_, ALU.subtract).then_inc(S["pool_ready"], 1)

        @block.sync
        def _(sp):
            with sp.Fori(0, DEPTH) as l:
                uses = Uses(l, PER_LAYER)
                sp_ffn(sp, uses, l, a["ffn1_w_gate"], 0, a["ffn1_w_up"], 0, a["ffn1_w_down"])
                sp_proj(sp, uses, l, a["w_in"], 6, start1)
                sp_out(sp, uses, l, a["w_out"])
                sp_ffn(sp, uses, l, a["ffn2_w_gate"], 0, a["ffn2_w_up"], 0, a["ffn2_w_down"])
            uses = Uses(SECOND, PER_LAYER)
            sp_proj(sp, uses, 0, a["w_in_2"], 5, start2)
            sp_out(sp, uses, 0, a["w_out_2"])
            sp_ffn(sp, uses, 0, a["w_up_2"], DFF, a["w_up_2"], 0, a["w_down_2"])

        @block.gpsimd
        def _(pool):
            for n, v in (("norm", NORM_EPS), ("gn", GN_EPS), ("ln", LN_EPS), ("kk", 1e-12)):
                pool.memset(eps[n], v)
            pool.memset(proj[:, :, 0:1], 0.0).then_inc(setup_done, 1)
            with pool.Fori(0, DEPTH) as l:
                pool.wait_ge(S["params_ready"], 1)
                pool_mixer(pool, Chain(pool, S["pool_link"]))
                pool.drain()
                pool.wait_ge(arrived, l * 3 + 3)
                pool.sem_inc(over, 1)
                pool.sem_clear(layer_sems)
                pool.sem_inc(cleared, 1)
            pool_second(pool, Chain(pool, S["pool_link"]))

        @block.scalar
        def _(act):
            act.dma_start(x[:, :, :], a["x"][0].rearrange("(t p) n -> p t n", p=P)).then_inc(x_in, 16)
            act.dma_start(cst[:, :], a["consts"]).then_inc(consts_in, 16)
            act.dma_start(hot[:, :], a["hot"]).then_inc(consts_in, 16)
            load_rows(act)
            act.wait_ge(setup_done, 1)
            with act.Fori(0, DEPTH) as l:
                uses = Uses(l, PER_LAYER)
                act_ahead(act, uses)
                act_norm(act, 0)
                act.wait_ge(S["params_ready"], 1)
                act_turned(act, 0, "norm_ffn1")
                act_ffn(act, uses, 0)
                act_norm(act, 1)
                act_turned(act, 1, "norm_mix")
                act_proj(act, uses, 6)
                act_mixer(act, uses, Chain(act, S["act_link"]))
                act_ahead(act, uses)
                act_norm(act, 2)
                act_turned(act, 2, "norm_ffn2")
                act_ffn(act, uses, 1)
                layer_over(act, l)
            act_second(act, Uses(SECOND, PER_LAYER))

        @block.vector
        def _(dve):
            for n in SLOTS:
                dve.sem_inc(split[n], 1)
            dve.wait_ge(consts_in, 32)
            dve.wait_ge(setup_done, 1)
            with dve.Fori(0, DEPTH) as l:
                uses = Uses(l, PER_LAYER)
                link = Chain(dve, S["dve_link"])
                dve_pick_rows(dve, l)
                dve_norm(dve, 0, link)
                dve_ahead(dve, uses)
                dve_turned(dve, 0, "norm_ffn1")
                dve_ffn(dve, uses, 0)
                dve_residual(dve, uses, 0.5, "down")
                dve_norm(dve, 1, link)
                dve_turned(dve, 1, "norm_mix")
                dve_proj(dve, uses, 6, start1)
                dve_mixer(dve, uses, link)
                dve_residual(dve, uses, 1.0, "gate")
                dve_norm(dve, 2, link)
                dve_ahead(dve, uses)
                dve_turned(dve, 2, "norm_ffn2")
                dve_ffn(dve, uses, 1)
                dve_residual(dve, uses, 0.5, "down")
                layer_over(dve, l)
            dve_second(dve, Uses(SECOND, PER_LAYER), Chain(dve, S["dve_link"]))

        @block.tensor
        def _(pe):
            for n in KINDS:
                pe.sem_inc(used[n], 1)
            pe.wait_ge(consts_in, 32)
            with pe.Fori(0, DEPTH) as l:
                uses = Uses(l, PER_LAYER)
                pe.wait_ge(S["rows_picked"], 1)
                pe.transpose(psum[7][:, 0:NROWS], row_now[0:NROWS, :], ident[0:NROWS, 0:NROWS])\
                  .then_inc(S["params_psum"], 1)
                pe_turn(pe, 0, hN, S["normed"])
                pe_ffn(pe, uses, 0, 0)
                pe_turn(pe, 1, hN, S["normed"])
                pe_proj(pe, uses, 6, 1)
                pe_mixer(pe, uses)
                pe_turn(pe, 2, hN, S["normed"])
                pe_ffn(pe, uses, 1, 2)
                layer_over(pe, l)
            pe_second(pe, Uses(SECOND, PER_LAYER))


INS = ["x", "norm_ffn1", "ffn1_w_gate", "ffn1_w_up", "ffn1_w_down", "norm_mix", "w_in", "shift_mu", "rwkv_w0",
       "rwkv_w2", "rwkv_a0", "rwkv_a2", "rwkv_g2", "rwkv_k_k", "rwkv_k_a", "rwkv_r_k", "rwkv_ln_w", "rwkv_ln_b",
       "attn_q_norm", "attn_k_norm", "conv_dw_w", "conv_dw_b", "conv_ln_w", "conv_ln_b", "w_out", "norm_ffn2",
       "ffn2_w_gate", "ffn2_w_up", "ffn2_w_down", "w_in_2", "conv_w_2", "w_pool_2", "pool_scale_2", "w_out_2",
       "ln1_g_2", "ln1_b_2", "w_up_2", "ffn_conv_w_2", "ffn_conv_b_2", "w_down_2", "ln2_g_2", "ln2_b_2",
       "rel_bias_2"]


def kernel(**inputs):
    import concourse.bacc as bacc
    from concourse.bass_utils import run_bass_kernel_spmd

    nc = bacc.Bacc("TRN2", target_bir_lowering=False, num_devices=1)
    packed, _, hot = constants()
    arrays = {f"in_{n}_dram": np.ascontiguousarray(inputs[n]) for n in INS}
    arrays["in_consts_dram"] = packed
    arrays["in_hot_dram"] = hot
    args = {n: nc.dram_tensor(f"in_{n}_dram", arrays[f"in_{n}_dram"].shape, F32, kind="ExternalInput").ap()
            for n in INS + ["consts", "hot"]}
    out = nc.dram_tensor("out_0_dram", (1, SEQ, D), F32, kind="ExternalOutput").ap()
    build(nc, args, out)
    r = run_bass_kernel_spmd(nc, [arrays], core_ids=[0])
    return r.results[0]["out_0_dram"]
```

```python
from contextlib import ExitStack

import numpy as np

import concourse.bass as bass
from concourse import mybir

F32 = mybir.dt.float32
F32R = mybir.dt.float32r
ALU = mybir.AluOpType
ACT = mybir.ActivationFunctionType
AX = mybir.AxisListType.X

P = 128
SEQ, D, DEPTH = 256, 1024, 2
NT = SEQ // P
KC = D // P
DFF = 2816
DIN = 2944
NCH = DIN // P
DIN2 = 2560
CONV_W = 31
CHUNK = 64
NH1, NH2 = 6, 8
NORM_EPS, GN_EPS, LN_EPS = 1e-6, 64e-5, 1e-5
ALPHA = 2.0 ** 0.25
NEG = -1e30
WORK = 20992
GROUPS = DFF // 256
LOOPS = (GROUPS - 3) // 2
SLOTS = ["gate0", "up0", "down0", "gate1", "up1", "down1"]
PROJ_SLOTS = ["up0", "down0", "gate0", "up1", "down1", "gate1"]
OUT_SLOTS = ["gate0", "down0", "up0", "down1"]
OUT_PAIRS = (3, 2, 1, 0)
OUT2_SLOTS = ["gate0", "down0", "gate1", "up0"]
OUT2_PAIRS = (2, 0, 1, 3)
KINDS = ["gate", "up", "down"]
assert GROUPS == 11 and NCH == 23 and DEPTH == 2

R, K, V, LORA, AQ, AK, AV, CU, CG = 0, 3, 6, 9, 10, 13, 16, 19, 21
Q2, K2, V2, CB2, CC2, CX2, PI2 = 0, 4, 8, 12, 14, 16, 18


def param_rows():
    rows, at = {}, 0
    for name, n in (("norm_ffn1", 8), ("norm_mix", 8), ("norm_ffn2", 8), ("shift_mu", 10), ("rwkv_w0", 3),
                    ("rwkv_a0", 3), ("rwkv_k_k", 3), ("rwkv_k_a", 3), ("rwkv_r_k", 3), ("rwkv_ln_w", 3),
                    ("rwkv_ln_b", 3), ("conv_dw_w", 2 * CONV_W), ("conv_dw_b", 2), ("conv_ln_w", 2),
                    ("conv_ln_b", 2), ("attn_q_norm", 1), ("attn_k_norm", 1)):
        rows[name] = at
        at += n
    return rows, at


ROWS, NROWS = param_rows()
B_TAP2, B_BIAS, B_CONV, B_POOL, B_ROWS = 0, 44, 88, 94, 96


def constants():
    s = np.arange(P)[:, None]
    t = np.arange(P)[None, :]
    same = lambda n: (s // n == t // n)
    f = lambda m: m.astype(np.float32)
    strict, incl = f((s < t) & same(CHUNK)), f((s <= t) & same(CHUNK))
    parts = {
        "ident": np.eye(P, dtype=np.float32),
        "pair": f(same(64)),
        "mask4": np.concatenate([strict, incl, strict, incl], 1),
        "blk16": f(same(16)),
        "blk32": f(same(32) & ~same(16)),
        "blk64": f(same(64) & ~same(32)),
        "ones": np.ones((P, P), np.float32),
        "pick": f(s // 64 == np.arange(22)[None, :] - 10),
        "scan": np.broadcast_to(f(np.arange(SEQ) % CHUNK != 0), (P, SEQ)),
    }
    dist = (P + s) - np.arange(2 * P)[None, :]
    count = sum(((dist >= 0) & (dist % dil == 0) & (dist <= win)).astype(int)
                for win, dil in ((128, 1), (512, 4), (2048, 16)))
    logc = np.where(count > 0, np.log(np.maximum(count, 1)), NEG)
    slopes = [2.0 ** (-2.0 * (i + 1)) for i in range(4)] + [2.0 ** (-1.0 * (i + 1)) for i in range(8)][0::2][:2]
    parts["bias1"] = np.concatenate([np.where(count > 0, -m * dist + logc, NEG) for m in slopes], 1)
    pos = np.arange(1, SEQ + 1)
    parts["poolw"] = np.concatenate(
        [np.concatenate([np.broadcast_to(1.0 / np.minimum(pos, w), (64, SEQ)) for w in pair], 0)
         for pair in ((2, 4), (8, 16))], 1)
    at, cols = 0, {}
    for name, a in parts.items():
        cols[name] = (at, at + a.shape[1])
        at += a.shape[1]
    packed = np.ascontiguousarray(np.concatenate([np.asarray(a, np.float32) for a in parts.values()], 1))
    d = 255 - np.arange(384)
    n = np.maximum(d, 0)
    nf = np.maximum(n, 1).astype(np.float32)
    large = 16 + (np.log(nf / np.float32(16)) / np.float32(np.log(1024 / 16)) * np.float32(16)).astype(np.int32)
    bucket = np.where(n < 16, n, np.minimum(large, 31))
    hot = np.zeros((33, 384), np.float32)
    hot[bucket, np.arange(384)] = (d >= 0)
    hot[32] = np.where(d < 0, NEG, 0.0)
    heads = f(np.arange(12 * 64)[None, :] // 64 == np.arange(12)[:, None])
    return packed, cols, hot, heads


def chain_plan():
    steps = [
        [("copy", "D2", "DT", "D"), ("copy", "D2T", "D", "DT")],
        [("add", "INV", "D2", "INV"), ("copy", "D", "D2T", "D2"), ("copy", "DT", "D2", "D2T")],
        [("add", "INV", "D", "INV"), ("copy", "D2", "DT", "D")],
        [("add", "INV", "D2", "INV"), ("add", "D", "AT", None)],
        [("copy", "D2T", "INV", None), ("copy", "DT", "D", "INV")],
        [("add", "INV", "D2T", "DT"), ("add", "D2", "AT", None)],
        [("copy", "D2T", "INV", None), ("copy", "DT", "D2", "INV")],
        [("add", "INV", "D2T", "DT")],
    ]
    plan, n = [], {"copy": 0, "add": 0}
    last = {}
    for step, products in enumerate(steps):
        for b in range(3):
            written = []
            for kind, dst, lhs, rhs in products:
                needs = [last.get((x, b)) for x in (lhs, rhs) if x]
                plan.append((step, b, kind, n[kind], dst, lhs, rhs, [x for x in needs if x], last.get((dst, b))))
                written.append(((dst, b), (kind, n[kind])))
                n[kind] += 1
            last.update(written)
    return plan


CHAIN = chain_plan()
COPIES, ADDS = (sum(c[2] == k for c in CHAIN) for k in ("copy", "add"))


def build(nc, a, out):
    packed_cols = constants()[1]
    ctx = ExitStack()
    with ctx:
        def sb(name, shape):
            return ctx.enter_context(nc.sbuf_tensor(name, shape, F32))

        loaded = {n: ctx.enter_context(nc.semaphore(f"loaded_{n}")) for n in SLOTS}
        high = {n: ctx.enter_context(nc.semaphore(f"high_{n}")) for n in SLOTS}
        split = {n: ctx.enter_context(nc.semaphore(f"split_{n}")) for n in SLOTS}
        used = {n: ctx.enter_context(nc.semaphore(f"used_{n}")) for n in KINDS}
        arrived = ctx.enter_context(nc.semaphore("arrived"))
        cleared = ctx.enter_context(nc.semaphore("cleared"))
        ident_in = ctx.enter_context(nc.semaphore("ident_in"))
        consts_in = ctx.enter_context(nc.semaphore("consts_in"))
        x_in = ctx.enter_context(nc.semaphore("x_in"))
        rows_in = ctx.enter_context(nc.semaphore("rows_in"))
        loads_seen = ctx.enter_context(nc.semaphore("loads_seen"))
        wpool_in = ctx.enter_context(nc.semaphore("wpool_in"))
        second_in = ctx.enter_context(nc.semaphore("second_in"))
        gain_in = ctx.enter_context(nc.semaphore("gain_in"))
        setup_done = ctx.enter_context(nc.semaphore("setup_done"))
        spread_out = ctx.enter_context(nc.semaphore("spread_out"))
        bias_in = ctx.enter_context(nc.semaphore("bias_in"))
        over = ctx.enter_context(nc.semaphore("over"))
        resumed = ctx.enter_context(nc.semaphore("resumed"))
        lora_in = ctx.enter_context(nc.semaphore("lora_in"))
        slot_free = ctx.enter_context(nc.semaphore("slot_free"))
        stored = ctx.enter_context(nc.semaphore("stored"))

        names = """gain_picked gain_psum gain_ready rows_picked params_psum params_ready squares_done rms_root normed turned
            h_high h_low prod_done ff_high mix_high mix_low silu_done ff_ready x_updated  proj_ready dve_link
            act_link pool_link shifted lora_acts lora_mm decay_sig iclr_sig gate_copied cum_ready exps_done
            kk_sq kk_sum kk_root kk_inv kk_spread rw_ready bonus_sq bonus_mm bonus_ready tok_mm tok_copied_a tok_copied_d
            mats_mm mats_ready a_mm d_ready dt_ready inv_seed copy_mm add_mm copy_done add_done
            pav_mm pav_done mat_mm mat_done sa_mm sa_done st_mm st_done cend_ready y_mm y_copied
            gn_mean gn_sq gn_var gn_root gn_inv gn_spread mixr_ready ln_factors ln_scaled
            qk_sq qk_sum qk_root qk_inv qk_spread qk_ready score_mm biased maxed exp_done p_ready pt_mm pt_done av_mm mixa_ready
            conv_sig conv_z conv_acc cl_mean cl_sq cl_var cl_root cl_ready mixc_ready
            biasrow_mm spread_ready pool_ready pool_mm taps_act taps_picked lag_done taps_done stats_ready""".split()
        S = {n: ctx.enter_context(nc.semaphore(n)) for n in names}
        layer_sems = range(S[names[0]].num, S[names[-1]].num + 1)
        assert [S[n].num for n in names] == list(layer_sems)

        slot = {n: sb(f"w_{n}", [P, 2048]) for n in SLOTS}
        x = sb("x", [P, NT, D])
        proj = sb("proj", [P, NCH, SEQ + 1])
        mix = sb("mix", [P, KC, SEQ])
        cst = sb("cst", [P, list(packed_cols.values())[-1][1]])
        rows = sb("rows", [P, DEPTH, P])
        row_now = sb("row_now", [P, P])
        par = sb("par", [P, P])
        lora_w = sb("lora_w", [P, 384])
        small = sb("small", [P, 96])
        hot = sb("hot", [33, 384])
        heads = sb("heads", [12, 12 * 64])
        work_at = (nc.sbuf_base + 31) // 32 * 32
        work = sb("work", [P, WORK])
        pair_at = (nc.sbuf_base + 31) // 32 * 32
        hT = [ctx.enter_context(nc.sbuf_tensor(f"hT_{n}", [P, KC, SEQ], F32R)) for n in ("hi", "lo")]
        spare = nc.alloc_sbuf_tensor_at("spare", [P, 2 * KC * SEQ], F32, offset=pair_at)

        def over_work(name, at, *shape):
            return nc.alloc_sbuf_tensor_at(name, [P, *shape], F32R, offset=work_at + 4 * at)

        staged = {n: [over_work(f"{n}_{part}", 4096 * i + 2048 * j, 2048) for j, part in enumerate(("hi", "lo"))]
                  for i, n in enumerate(KINDS)}
        ffT = [over_work(f"ff_{part}", 12288 + 1024 * j, 2, 512) for j, part in enumerate(("hi", "lo"))]
        psum = [ctx.enter_context(nc.psum_tensor(f"bank{i}", [P, 512], F32)) for i in range(8)]

        def area(at, *shape):
            n = int(np.prod(shape))
            v = work[:, at:at + n]
            if len(shape) == 2:
                v = v.rearrange("p (a b) -> p a b", a=shape[0])
            if len(shape) == 3:
                v = v.rearrange("p (a b c) -> p a b c", a=shape[0], b=shape[1])
            if len(shape) == 4:
                v = v.rearrange("p (a b c d) -> p a b c d", a=shape[0], b=shape[1], c=shape[2])
            return v, at + n

        def const(name, parts=slice(0, P)):
            lo, hi = packed_cols[name]
            return cst[parts, lo:hi]

        ident, pairs, ones = const("ident"), const("pair"), const("ones")
        o_ffn = 14336
        silu, o = area(o_ffn, 2, 512)
        prod, o = area(o, 512)
        taps, o = area(o, 2, 2, 512)
        hN, _ = area(o_ffn, NT, D)
        sh, o = area(0, 10, SEQ)
        ar, o = area(o, 3, NT, 2, P)
        bh, o = area(o, 3, SEQ)
        kh, o = area(o, 3, SEQ)
        ec, o = area(o, 3, SEQ)
        tok, o = area(o, 4, NT, 384)
        avtok, o = area(o, NT, 384)
        o_mats = o
        mats, o = area(o, 12, 4, P)
        o_chain = o
        chain = {}
        for n in ("D2", "D2T"):
            chain[n], o = area(o, 12, P)
        gate, o = area(o, 3, SEQ)
        bonus, o = area(o, 3, SEQ)
        assert o <= WORK, o
        blocks = lambda at: spare[:, at:at + 12 * P].rearrange("p (a b) -> p a b", a=12)
        chain |= {"D": blocks(0), "DT": blocks(12 * P), "INV": area(0, 12, P)[0]}
        o = o_mats
        ld, o = area(o, 3, SEQ)
        cum, o = area(o, 3, SEQ)
        ecx, o = area(o, 3, SEQ)
        en, o = area(o, 3, SEQ)
        iclr, o = area(o, 3, SEQ)
        kk, o = area(o, 3, SEQ)
        kmod, o = area(o, 3, SEQ)
        tmp, o = area(o, 3, SEQ)
        lact, o = area(o, SEQ)
        assert o <= o_chain + 2 * 12 * P, o
        qsq = mix[:, 0:6, :]
        qkinv = mix[0:12, 0, :]
        kkinv = tmp[0:6, 0, :]
        logit = spare[:, 24 * P:24 * P + 768].rearrange("p (a b) -> p a b", a=2)
        probT, _ = area(6 * SEQ, 2, 384)
        o = o_chain
        pav, o = area(o, NT, 384)
        mat_, o = area(o, NT, 384)
        satok, o = area(o, NT, 384)
        ysb, o = area(o, 3, SEQ)
        assert o <= o_chain + 2 * 12 * P
        nine = lambda at: spare[:, at:at + 9 * P].rearrange("p (a b c) -> p a b c", a=3, b=3)
        state = nine(0)
        cend = nine(9 * P)
        ysq, o = area(12288, 3, SEQ)
        gninv = area(o, SEQ)[0][0:6, :]
        par2, o = area(o_ffn + 3584, 4, 44)
        par2c, o = area(o, 8)
        tap_now, o = area(o, 2, 4, 2, 2)
        ln_gb, o = area(o, 2, D)
        assert o <= WORK, o
        bias2, o = area(12288, NH2, 2 * P)
        spread = area(o_ffn, 384)[0][0:NH2, :]
        rows2, o = area(o_ffn + 3072, 2, P)
        tab, o = area(o, 64)
        assert o <= o_ffn + 3584
        wpool, o = area(20184, 2, P)
        assert o <= WORK
        avtok2, o = area(4096, NT, 512)
        logit2, o = area(o, 2, 384)
        probT2, o = area(o, 2, 384)
        cz, o = area(o, 2, SEQ)
        pl, o = area(o, 2, 2, SEQ)
        assert o <= 8192
        rstd = small[:, 0:8]
        eps = {n: small[:, 8 + i:9 + i] for i, n in enumerate(("norm", "gn", "ln", "kk"))}
        amax, anmax, asum, arec = (small[:, 12 + 16 * i:28 + 16 * i].rearrange("p (h t) -> p h t", t=NT)
                                   for i in range(4))
        unused = small[:, 92:93]
        lnbias = small[:, 93:95]
        lnstat = small[:, 76:88].rearrange("p (a b) -> p a b", a=2)
        lnvar = small[:, 88:92].rearrange("p (a b) -> p a b", a=2)

        block = ctx.enter_context(nc.Block())
        scratch = nc.dram_tensor("bias_scratch", [P, NH2, 384], F32)

        def col(name, i=0):
            c = ROWS[name] + i
            return par[:, c:c + 1]

        class Chain:

            def __init__(self, eng, sem):
                self.eng, self.sem, self.n = eng, sem, 0

            def __call__(self, ins):
                self.n += 1
                ins.then_inc(self.sem, 1)
                self.eng.wait_ge(self.sem, self.n)

        class Uses:

            def __init__(self, layer, per_layer):
                self.base = lambda n: layer * per_layer[n]
                self.n = dict.fromkeys(SLOTS + KINDS, 0)

            def now(self, name, more=0):
                return self.base(name) + (more + self.n[name] + 1)

            def ffn(self):
                for n in SLOTS:
                    self.n[n] += 6 if n.endswith("0") else 5
                for n in KINDS:
                    self.n[n] += FFN_FILLS[n]

            def each(self, names, times=1):
                for n in names:
                    self.n[n] += times
                    self.n[n[:-1]] += times

        FFN_FILLS = {"gate": GROUPS + 1, "up": GROUPS, "down": GROUPS - 1}
        PER_LAYER = {n: 2 * (6 if n.endswith("0") else 5) + 2 for n in SLOTS} | {n: 2 * FFN_FILLS[n] + 4 for n in KINDS}
        for n in OUT_SLOTS:
            PER_LAYER[n] += 1
            PER_LAYER[n[:-1]] += 1

        def act_high(act, uses, sl, more=0, more_kind=0, kind=None):
            kind = kind or sl[:-1]
            act.wait_ge(loaded[sl], uses.now(sl, more) * 16)
            act.wait_ge(used[kind], uses.now(kind, more_kind))
            act.activation(staged[kind][0][:, :], slot[sl][:, :], ACT.Copy).then_inc(high[sl], 1)

        def dve_low(dve, uses, sl, more=0, kind=None):
            kind = kind or sl[:-1]
            dve.wait_ge(high[sl], uses.now(sl, more))
            dve.tensor_tensor(staged[kind][1][:, :], slot[sl][:, :], staged[kind][0][:, :].bitcast(F32),
                              ALU.subtract).then_inc(split[sl], 1)

        def tile_ready(pe, uses, sl, more=0):
            pe.wait_ge(split[sl], uses.now(sl, more) + 1)

        def products_done(eng, uses, kind, more=0):
            eng.wait_ge(used[kind], uses.now(kind, more) + 1)

        PASSES = ((0, 0), (0, 1), (1, 0))

        def product(pe, out_, lhs, rhs, first, last, **kw):
            for i, (l_, r_) in enumerate(PASSES):
                mm = pe.matmul(out_, lhs(l_), rhs(r_), start=first and i == 0, stop=last and i == 2, **kw)
            return mm

        def fill(sp, uses, name, src, more=0):
            n = uses.now(name, more)
            sp.wait_ge(split[name], n)
            sp.sem_inc(slot_free, 1)
            width = src.shape[2]
            dst = slot[name][:, :].rearrange("p (c n) -> p c n", n=width)
            sp.dma_start(dst, src).then_inc(loaded[name], 16)

        def columns(w, l, start, width=256):
            return w[bass.ds(l, 1), :, bass.ds(start, width)].rearrange("a (c p) n -> p (a c) n", p=P)

        def krows(w, l, start):
            return w[bass.ds(l, 1), bass.ds(start, 256), :].rearrange("a (c p) n -> p (a c) n", p=P)

        def sp_ffn(sp, uses, l, wg, g0, wu, u0, wd):
            def gu(g, par_, more=0):
                fill(sp, uses, f"gate{par_}", columns(wg, l, g * 256 + g0), more)
                fill(sp, uses, f"up{par_}", columns(wu, l, g * 256 + u0), more)

            def dn(g, par_, more=0):
                fill(sp, uses, f"down{par_}", krows(wd, l, g * 256), more)

            gu(0, 0)
            gu(1, 1)
            dn(0, 0)
            with sp.Fori(0, LOOPS) as it:
                gu(it * 2 + 2, 0, it + 1)
                dn(it * 2 + 1, 1, it)
                gu(it * 2 + 3, 1, it + 1)
                dn(it * 2 + 2, 0, it + 1)
            gu(10, 0, LOOPS + 1)
            dn(9, 1, LOOPS)
            dn(10, 0, LOOPS + 1)
            uses.ffn()

        def sp_proj(sp, uses, l, w, per, starts):
            with sp.Fori(0, 2) as it:
                for j in range(per):
                    fill(sp, uses, PROJ_SLOTS[j], columns(w, l, starts(it, j) * P), it)
            uses.each(PROJ_SLOTS[:per], 2)

        def sp_out(sp, uses, l, w, slots, pairs_):
            for sl, pair in zip(slots, pairs_):
                fill(sp, uses, sl, krows(w, l, pair * 256))
            uses.each(slots)

        def start1(it, j):
            return it * 12 + 2 * j if j < 5 else it * 11 + 10

        def start2(it, j):
            return it * 10 + 2 * j

        def over_groups(eng, body):
            body(0, 0, 0)
            body(1, 1, 0)
            with eng.Fori(0, LOOPS) as it:
                body(it * 2 + 2, 0, it + 1)
                body(it * 2 + 3, 1, it + 1)
            body(10, 0, LOOPS + 1)

        def later(g):
            return not isinstance(g, int) or g >= 2

        def final(g):
            return isinstance(g, int) and g == GROUPS - 1

        def pe_ffn(pe, uses, f, n_norm):
            b = f * GROUPS

            def gu(g, par_, more=0):
                if later(g):
                    pe.wait_ge(S["ff_ready"], g + (b - 1))
                for name, bank in (("gate", psum[par_]), ("up", psum[2 + par_])):
                    tile_ready(pe, uses, f"{name}{par_}", more)
                    w = [t_[:, :].rearrange("p (c n) -> p c n", n=256) for t_ in staged[name]]
                    for j in range(2):
                        for c in range(KC):
                            if isinstance(g, int) and g == 0 and name == "gate" and j == 0:
                                pe.wait_ge(S["h_low"], KC * n_norm + c + 1)
                            mm = product(pe, bank[:, j * SEQ:(j + 1) * SEQ], lambda p_: w[p_][:, c, j * P:(j + 1) * P],
                                         lambda p_: hT[p_][:, c, :], c == 0, c == KC - 1)
                    mm.then_inc(used[name], 1)

            def down(g, par_, more=0, first=False, last=False):
                pe.wait_ge(S["ff_ready"], g + (b + 1))
                tile_ready(pe, uses, f"down{par_}", more)
                kind = "gate" if last else "down"
                w = [t_[:, :].rearrange("p (c n) -> p c n", n=D) for t_ in staged[kind]]
                for j in range(2):
                    for t in range(NT):
                        for h in range(2):
                            at = slice(j * SEQ + t * P, j * SEQ + (t + 1) * P)
                            mm = product(pe, psum[4 + 2 * t + h][:, :], lambda p_: ffT[p_][:, par_, at],
                                         lambda p_: w[p_][:, j, h * 512:(h + 1) * 512], first and j == 0,
                                         last and j == 1, skip_group_check=True)
                mm.then_inc(used[kind], 1)

            gu(0, 0)
            gu(1, 1)
            down(0, 0, first=True)
            with pe.Fori(0, LOOPS) as it:
                gu(it * 2 + 2, 0, it + 1)
                down(it * 2 + 1, 1, it)
                gu(it * 2 + 3, 1, it + 1)
                down(it * 2 + 2, 0, it + 1)
            gu(10, 0, LOOPS + 1)
            down(9, 1, LOOPS)
            down(10, 0, LOOPS + 1, last=True)
            uses.ffn()

        def act_ahead(act, uses, slots=("gate0", "up0")):
            for sl in slots:
                act_high(act, uses, sl)

        def dve_ahead(dve, uses, slots=("gate0", "up0")):
            for sl in slots:
                dve_low(dve, uses, sl)

        def act_ffn(act, uses, f):
            b = f * GROUPS

            def group(g, par_, more):
                if not final(g):
                    act_high(act, uses, f"gate{1 - par_}", more + par_, g + 1)
                    act_high(act, uses, f"up{1 - par_}", more + par_, g + 1)
                products_done(act, uses, "up", g)
                if later(g):
                    act.wait_ge(S["ff_ready"], g + (b - 1))
                act.activation(silu[:, par_, :], psum[par_][:, :], ACT.Silu).then_inc(S["silu_done"], 1)
                if final(g):
                    act_high(act, uses, f"down{par_}", more, g + 1, "gate")
                else:
                    act_high(act, uses, f"down{par_}", more, g)

            over_groups(act, group)
            uses.ffn()

        def dve_hidden(dve, up, par_, g, b, uses):
            if later(g) or g + b:
                dve.wait_ge(S["ff_ready"], g + b)
            dve.tensor_tensor(prod, silu[:, par_, :], up, ALU.mult).then_inc(S["prod_done"], 1)
            dve.wait_ge(S["prod_done"], g + (b + 1))
            if later(g):
                products_done(dve, uses, "down", g - 2)
            dve.tensor_copy(ffT[0][:, par_, :], prod).then_inc(S["ff_high"], 1)
            dve.wait_ge(S["ff_high"], g + (b + 1))
            dve.tensor_tensor(ffT[1][:, par_, :], prod, ffT[0][:, par_, :].bitcast(F32),
                              ALU.subtract).then_inc(S["ff_ready"], 1)

        def dve_ffn(dve, uses, f):
            b = f * GROUPS

            def group(g, par_, more):
                if not final(g):
                    dve_low(dve, uses, f"gate{1 - par_}", more + par_)
                    dve_low(dve, uses, f"up{1 - par_}", more + par_)
                dve.wait_ge(S["silu_done"], g + (b + 1))
                dve_hidden(dve, psum[2 + par_][:, :], par_, g, b, uses)
                dve_low(dve, uses, f"down{par_}", more, "gate" if final(g) else "down")

            over_groups(dve, group)
            uses.ffn()

        def dve_residual(dve, uses, scale, kind):
            products_done(dve, uses, kind, -1)
            for t in range(NT):
                for h in range(2):
                    xs = x[:, t, h * 512:(h + 1) * 512]
                    ins = dve.scalar_tensor_tensor(xs, psum[4 + 2 * t + h][:, :], scale, xs, ALU.mult, ALU.add)
                ins.then_inc(S["x_updated"], 1)

        def act_norm(act, n):
            act.activation(unused, eps["norm"], ACT.Sqrt)
            if n == 0:
                act.wait_ge(x_in, 16)
            for t in range(NT):
                if n:
                    act.wait_ge(S["x_updated"], NT * (n - 1) + t + 1)
                act.activation(hN[:, t, :], x[:, t, :], ACT.Square,
                               accum_out=rstd[:, t:t + 1]).then_inc(S["squares_done"], 1)
            act.wait_ge(S["squares_done"], 2 * n + 2)
            act.activation(rstd[:, 2:4], rstd[:, 0:2], ACT.Sqrt, bias=eps["norm"], scale=1.0 / D)\
               .then_inc(S["rms_root"], 1)

        def dve_norm(dve, n, link):
            dve.wait_ge(S["rms_root"], n + 1)
            link(dve.reciprocal(rstd[:, 4:6], rstd[:, 2:4]))
            for t in range(NT):
                dve.tensor_scalar(hN[:, t, :], x[:, t, :], rstd[:, 4 + t:5 + t], None, ALU.mult)\
                   .then_inc(S["normed"], 1)

        def pe_turn(pe, n, src, ready, count=None):
            for c in range(KC):
                for t in range(NT):
                    if ready is not None and c == 0:
                        pe.wait_ge(ready, NT * (n if count is None else count) + t + 1)
                    at = (c % 2) * SEQ + t * P
                    mm = pe.transpose(psum[4 + c // 2][:, at:at + P], src[:, t, c * P:(c + 1) * P], ident)
                if c % 2 == 1:
                    mm.then_inc(S["turned"], 1)

        def act_turned(act, n, gain):
            for c in range(KC):
                if c % 2 == 0:
                    act.wait_ge(S["turned"], KC // 2 * n + c // 2 + 1)
                src = psum[4 + c // 2][:, (c % 2) * SEQ:(c % 2 + 1) * SEQ]
                act.activation(hT[0][:, c, :], src, ACT.Copy, scale=col(gain, c) if gain else 1.0)\
                   .then_inc(S["h_high"], 1)

        def dve_turned(dve, n, gain):
            for c in range(KC):
                dve.wait_ge(S["h_high"], KC * n + (c // 2) * 2 + 2)
                src = psum[4 + c // 2][:, (c % 2) * SEQ:(c % 2 + 1) * SEQ]
                dve.scalar_tensor_tensor(hT[1][:, c, :], src, col(gain, c) if gain else 1.0,
                                         hT[0][:, c, :].bitcast(F32), ALU.mult, ALU.subtract)\
                   .then_inc(S["h_low"], 1)

        def pe_proj(pe, uses, per, n_norm):
            with pe.Fori(0, 2) as it:
                for j in range(per):
                    if j >= 4:
                        pe.wait_ge(S["proj_ready"], it * per + (j - 3))
                    sl = PROJ_SLOTS[j]
                    tile_ready(pe, uses, sl, it)
                    w = [t_[:, :].rearrange("p (c n) -> p c n", n=256) for t_ in staged[sl[:-1]]]
                    for i in range(2):
                        for c in range(KC):
                            if j == 0 and i == 0:
                                pe.wait_ge(S["h_low"], KC * n_norm + c + 1)
                            mm = product(pe, psum[j][:, i * SEQ:(i + 1) * SEQ], lambda p_: w[p_][:, c, i * P:(i + 1) * P],
                                         lambda p_: hT[p_][:, c, :], c == 0, c == KC - 1)
                    mm.then_inc(used[sl[:-1]], 1)
                pe.wait_ge(S["proj_ready"], it * per + (per - 1 if per < 6 else 4))
            uses.each(PROJ_SLOTS[:per], 2)

        def proj_tiles(per):
            kinds = [sl[:-1] for sl in PROJ_SLOTS[:per] * 2]
            return [(n, n // per, n % per, PROJ_SLOTS[n % per], kinds[:n].count(kinds[n])) for n in range(2 * per)]

        def act_proj(act, uses, per):
            for n, it, _, sl, before in proj_tiles(per):
                if n >= 2:
                    act_high(act, uses, sl, it, before)
            uses.each(PROJ_SLOTS[:per], 2)

        def dve_proj(dve, uses, per, starts):
            tiles = proj_tiles(per)
            for n, it, j, sl, before in tiles:
                if n + 2 < len(tiles):
                    dve_low(dve, uses, tiles[n + 2][3], tiles[n + 2][1])
                products_done(dve, uses, sl[:-1], before)
                if j == 5:
                    dve.wait_ge(S["proj_ready"], n)
                dve.tensor_scalar(proj[:, starts(it, j):starts(it, j) + 2, 1:SEQ + 1],
                                  psum[j][:, :].rearrange("p (a b) -> p a b", a=2), 1.0, None,
                                  ALU.mult).then_inc(S["proj_ready"], 1)
            uses.each(PROJ_SLOTS[:per], 2)

        def pe_out(pe, uses, k, ready, slots, pairs_, steps=range(2)):
            if 0 in steps:
                ready(k)
                tile_ready(pe, uses, slots[k], 0)
            w = [t_[:, :].rearrange("p (c n) -> p c n", n=D) for t_ in staged[slots[k][:-1]]]
            for j in steps:
                c = 2 * pairs_[k] + j
                for t in range(NT):
                    for h in range(2):
                        mm = product(pe, psum[4 + 2 * t + h][:, :], lambda p_: hT[p_][:, c, t * P:(t + 1) * P],
                                     lambda p_: w[p_][:, j, h * 512:(h + 1) * 512], k == 0 and j == 0,
                                     k == 3 and j == 1, skip_group_check=True)
            if 1 in steps:
                mm.then_inc(used[slots[k][:-1]], 1)

        def act_mixed(act, lo, hi):
            act.activation(hT[0][:, lo:hi, :], mix[:, lo:hi, :], ACT.Copy).then_inc(S["mix_high"], 1)

        def dve_mixed(dve, lo, hi):
            dve.tensor_tensor(hT[1][:, lo:hi, :], mix[:, lo:hi, :], hT[0][:, lo:hi, :].bitcast(F32),
                              ALU.subtract).then_inc(S["mix_low"], 1)

        def half(h):
            return slice(64 * (h % 2), 64 * (h % 2) + 64)

        class PeAttention:

            def __init__(self, pe, qc, kc, vtok, logit_, probT_, banks):
                self.pe, self.qc, self.kc = pe, qc, kc
                self.vtok, self.logit, self.probT, (self.b_score, self.b_turn, self.b_value) = vtok, logit_, probT_, banks

            def score(self, h):
                pe, n, r = self.pe, len(self.b_score), half(h)
                bank = psum[self.b_score[h % n]]
                if h >= n:
                    pe.wait_ge(S["biased"], h - n + 1)
                q, k = proj[r, self.qc + h // 2, 1:], proj[r, self.kc + h // 2, 1:]
                pe.matmul(bank[:, 0:P], q[:, 0:P], k[:, 0:P], start=True, stop=True)
                pe.matmul(bank[:, P:3 * P], q[:, P:], k, start=True, stop=True).then_inc(S["score_mm"], 1)

            def turn(self, h):
                pe, n = self.pe, len(self.b_turn)
                pe.wait_ge(S["p_ready"], h + 1)
                if h >= n:
                    pe.wait_ge(S["pt_done"], h - n + 1)
                for i in range(3):
                    mm = pe.transpose(psum[self.b_turn[h % n]][:, i * P:(i + 1) * P],
                                      self.logit[:, h % 2, i * P:(i + 1) * P], ident)
                mm.then_inc(S["pt_mm"], 1)

            def value(self, h):
                pe, n, pair = self.pe, len(self.b_value), h // 2
                pe.wait_ge(S["pt_done"], h + 1)
                if h % 2 == 0 and pair >= n:
                    pe.wait_ge(S["mixa_ready"], pair - n + 1)
                bank = psum[self.b_value[pair % n]]
                v = [self.vtok[:, t, h * 64:(h + 1) * 64] for t in range(NT)]
                pt = [self.probT[:, h % 2, i * P:(i + 1) * P] for i in range(3)]
                pe.matmul(bank[half(h), 0:P], v[0], pt[0], start=True, stop=True)
                pe.matmul(bank[half(h), P:2 * P], v[0], pt[1], start=True, stop=False)
                pe.matmul(bank[half(h), P:2 * P], v[1], pt[2], start=False, stop=True).then_inc(S["av_mm"], 1)

        class DveAttention:
            def __init__(self, dve, bias, logit_, banks, link):
                self.dve, self.bias, self.logit, self.b_score, self.link = dve, bias, logit_, banks[0], link

            def logits(self, h):
                dve, logit_, n = self.dve, self.logit, len(self.b_score)
                dve.wait_ge(S["score_mm"], h + 1)
                if h >= 2:
                    dve.wait_ge(S["pt_mm"], h - 1)
                bank, bh_ = psum[self.b_score[h % n]], self.bias(h)
                dve.scalar_tensor_tensor(logit_[:, h % 2, 0:P], bank[:, 0:P], 0.125, bh_[:, P:2 * P],
                                         ALU.mult, ALU.add)
                dve.scalar_tensor_tensor(logit_[:, h % 2, P:3 * P], bank[:, P:3 * P], 0.125, bh_,
                                         ALU.mult, ALU.add).then_inc(S["biased"], 1)
                dve.wait_ge(S["biased"], h + 1)
                dve.tensor_reduce(amax[:, h, 0:1], logit_[:, h % 2, 0:P], AX, ALU.max)
                self.link(dve.tensor_reduce(amax[:, h, 1:2], logit_[:, h % 2, P:3 * P], AX, ALU.max))
                dve.tensor_scalar(anmax[:, h, :], amax[:, h, :], -1.0, None, ALU.mult).then_inc(S["maxed"], 1)

            def normalise(self, h):
                dve, logit_ = self.dve, self.logit
                dve.wait_ge(S["exp_done"], 2 * h + 2)
                self.link(dve.reciprocal(arec[:, h, :], asum[:, h, :]))
                for t, (lo, hi) in enumerate(((0, P), (P, 3 * P))):
                    ins = dve.tensor_scalar(logit_[:, h % 2, lo:hi], logit_[:, h % 2, lo:hi], arec[:, h, t:t + 1],
                                            None, ALU.mult)
                ins.then_inc(S["p_ready"], 1)

        def act_attention(act, nh, logit_, probT_, banks, to, beside=lambda h: None):
            _, b_turn, b_value = banks

            def exps(h):
                act.wait_ge(S["maxed"], h + 1)
                for t, (lo, hi) in enumerate(((0, P), (P, 3 * P))):
                    act.activation(logit_[:, h % 2, lo:hi], logit_[:, h % 2, lo:hi], ACT.Exp, bias=anmax[:, h, t:t + 1],
                                   accum_out=asum[:, h, t:t + 1]).then_inc(S["exp_done"], 1)

            def copy(h):
                act.wait_ge(S["pt_mm"], h + 1)
                if h >= 2:
                    act.wait_ge(S["av_mm"], h - 1)
                act.activation(probT_[:, h % 2, :], psum[b_turn[h % len(b_turn)]][:, 0:384], ACT.Copy)\
                   .then_inc(S["pt_done"], 1)

            def out_(pair):
                act.wait_ge(S["av_mm"], 2 * pair + 2)
                act.activation(mix[:, to + pair, :], psum[b_value[pair % len(b_value)]][:, 0:SEQ], ACT.Copy)\
                   .then_inc(S["mixa_ready"], 1)

            exps(0)
            for h in range(nh):
                if h + 1 < nh:
                    exps(h + 1)
                copy(h)
                if h % 2 == 0 and h >= 2:
                    out_(h // 2 - 1)
                beside(h)
            out_(nh // 2 - 1)

        def prob(t, h):
            return t * NH1 + h

        def bank_pair(c):
            return c // 2, slice((c % 2) * SEQ, (c % 2 + 1) * SEQ)

        def three(first):
            return [(psum[first][:, :].rearrange("p (a b) -> p a b", a=2), slice(0, 2)),
                    (psum[first + 1][:, 0:SEQ].rearrange("p (a b) -> p a b", a=1), slice(2, 3))]

        def ones_product(pe, first, src, mat=pairs):
            flat = src.rearrange("p a b -> p (a b)")
            pe.matmul(psum[first][:, :], mat, flat[:, 0:512], start=True, stop=True)
            return pe.matmul(psum[first + 1][:, 0:SEQ], mat, flat[:, 512:768], start=True, stop=True)

        TOK = [(w, t) for w in range(5) for t in range(NT)]
        TOK_BANK = [6, 2, 3, 7, 0, 1, 6, 2, 3, 7]
        BANKS1 = ((4, 5), (6,), (7,))
        BANKS2 = ((0, 1), (2,), (3,))

        def spread_heads(pe, n, banks, src):
            for c in range(n // 2):
                mm = pe.matmul(psum[banks[c // 2]][:, (c % 2) * SEQ:(c % 2 + 1) * SEQ],
                               heads[0:n, c * P:(c + 1) * P], src,
                               start=True, stop=True)
            return mm

        def sum_heads(pe, n, bank, src):
            for c in range(n // 2):
                mm = pe.matmul(psum[bank][0:n, 0:SEQ], const("pick")[:, 10 - 2 * c:10 - 2 * c + n], src[:, c, :],
                               start=(c == 0), stop=(c == n // 2 - 1))
            return mm

        def pe_mixer(pe, uses):
            pe.wait_ge(consts_in, 48)
            pe.wait_ge(S["proj_ready"], 12)
            pe.wait_ge(S["lora_acts"], 2)
            for lo, hi, first, src in ((0, 32, 0, lact), (32, 64, 2, None), (64, 128, 4, lact)):
                if first == 4:
                    pe.wait_ge(S["kk_sq"], 1)
                    sum_heads(pe, 6, 6, tmp).then_inc(S["kk_sum"], 1)
                    pe.wait_ge(S["qk_sq"], 1)
                    sum_heads(pe, 12, 7, qsq).then_inc(S["qk_sum"], 1)
                for c in range(3):
                    b, cols_ = bank_pair(c)
                    rhs = src[lo:hi, :] if src is not None else sh[lo:hi, LORA, :]
                    mm = pe.matmul(psum[first + b][:, cols_], lora_w[lo:hi, c * P:(c + 1) * P], rhs,
                                   start=True, stop=True)
                mm.then_inc(S["lora_mm"], 1)
            pe.wait_ge(S["kk_inv"], 1)
            pe.wait_ge(S["iclr_sig"], 3)
            spread_heads(pe, 6, (2, 3), kkinv).then_inc(S["kk_spread"], 1)
            pe.wait_ge(S["qk_inv"], 1)
            pe.wait_ge(S["decay_sig"], 3)
            spread_heads(pe, 12, (7, 0, 1), qkinv).then_inc(S["qk_spread"], 1)
            pe.wait_ge(S["rw_ready"], 1)
            for n, (w, t) in enumerate(TOK):
                if n == 3:
                    pe.wait_ge(S["bonus_sq"], 1)
                    pe.wait_ge(S["gate_copied"], 2)
                    ones_product(pe, 4, tmp).then_inc(S["bonus_mm"], 1)
                    pe.wait_ge(S["qk_ready"], 1)
                if n >= 6:
                    pe.wait_ge(S["tok_copied_a" if n % 2 == 0 else "tok_copied_d"], (n - 6) // 2 + 1)
                for c in range(3):
                    if w == 0:
                        src = ar[:, c, t, 0, :]
                    elif w == 4:
                        src = proj[:, AV + c, 1 + t * P:1 + (t + 1) * P]
                    else:
                        src = (None, bh[:, c], kh[:, c], sh[:, V + c])[w][:, t * P:(t + 1) * P]
                    mm = pe.transpose(psum[TOK_BANK[n]][:, c * P:(c + 1) * P], src, ident)
                mm.then_inc(S["tok_mm"], 1)
            pe.wait_ge(S["tok_copied_a"], 5)
            pe.wait_ge(S["tok_copied_d"], 5)
            pe.wait_ge(S["bonus_ready"], 1)
            attention = PeAttention(pe, AQ, AK, avtok, logit, probT, BANKS1)
            attention.score(0)
            attention.score(1)
            for p in range(12):
                t, h = divmod(p, NH1)
                r, c = half(h), h // 2
                if p >= 3:
                    pe.wait_ge(S["mats_ready"], p - 2)
                rhs = ar[r, c, t].rearrange("p a b -> p (a b)")
                pe.matmul(psum[p % 3][:, 0:256], bh[r, c, t * P:(t + 1) * P], rhs, start=True, stop=True)
                pe.matmul(psum[p % 3][:, 256:512], kh[r, c, t * P:(t + 1) * P], rhs, start=True,
                          stop=True).then_inc(S["mats_mm"], 1)
                if p % 2 == 1:
                    step = p // 2
                    attention.turn(step)
                    if step:
                        attention.value(step - 1)
                    if step + 2 < NH1:
                        attention.score(step + 2)
                if p % 4 == 3:
                    b = p // 4
                    pe.wait_ge(S["mats_ready"], p + 1)
                    if b:
                        pe.wait_ge(S["d_ready"], b)
                    for i in range(4):
                        mm = pe.transpose(psum[3][:, i * P:(i + 1) * P], mats[:, 4 * b + i, 0, :], ident)
                    mm.then_inc(S["a_mm"], 1)
            attention.value(NH1 - 1)
            for step, b, kind, n, dst, lhs, rhs, needs, _ in CHAIN:
                if step == 0:
                    pe.wait_ge(S["d_ready"], b + 1)
                    pe.wait_ge(S["dt_ready"], b + 1)
                    pe.wait_ge(S["mats_ready"], 12)
                if step == 0 and n == 3:
                    pe.wait_ge(S["d_ready"], 3)
                if step == 1 and kind == "add":
                    pe.wait_ge(S["inv_seed"], 1)
                    pe.wait_ge(S["mixa_ready"], 3)
                for k_, m in needs:
                    pe.wait_ge(S["copy_done" if k_ == "copy" else "add_done"], m + 1)
                if n >= 4:
                    pe.wait_ge(S["copy_done" if kind == "copy" else "add_done"], n - 3)
                bank = psum[(0 if kind == "copy" else 4) + n % 4]
                for i in range(4):
                    at, q = slice(i * P, (i + 1) * P), 4 * b + i
                    if rhs is None:
                        src = mats[:, q, 0, :] if lhs == "AT" else chain[lhs][:, q, :]
                        mm = pe.transpose(bank[:, at], src, ident)
                    else:
                        mm = pe.matmul(bank[:, at], chain[lhs][:, q, :], chain[rhs][:, q, :], start=True, stop=True)
                mm.then_inc(S["copy_mm" if kind == "copy" else "add_mm"], 1)
            inv = chain["INV"]
            pe.wait_ge(S["copy_done"], COPIES)
            for t in range(NT):
                for h in range(NH1):
                    mm = pe.matmul(psum[t][:, h * 64:(h + 1) * 64], mats[:, prob(t, h), 2, :],
                                   tok[:, 3, t, h * 64:(h + 1) * 64], start=True, stop=True)
                mm.then_inc(S["pav_mm"], 1)
            pe.wait_ge(S["add_done"], ADDS)
            for t in range(NT):
                for h in range(NH1):
                    mm = pe.matmul(psum[2 + t][half(h), (h // 2) * P:(h // 2 + 1) * P],
                                   tok[:, 0, t, h * 64:(h + 1) * 64], inv[:, prob(t, h), :], start=True, stop=True)
                mm.then_inc(S["mat_mm"], 1)
            def values_of(t):
                for c in range(3):
                    for h in (2 * c, 2 * c + 1):
                        pe.matmul(psum[c][half(h), t * P:(t + 1) * P], tok[:, 3, t, h * 64:(h + 1) * 64],
                                  mats[:, prob(t, h), 3, :], start=True, stop=False, skip_group_check=True)

            def y_of(t, c):
                at = slice(t * P, (t + 1) * P)
                for h in (2 * c, 2 * c + 1):
                    mm = pe.matmul(psum[c][half(h), at], satok[:, t, h * 64:(h + 1) * 64],
                                   mats[:, prob(t, h), 1, :], start=False, stop=True, skip_group_check=True)
                for ch in (2 * t, 2 * t + 1):
                    if ch > 0:
                        k = 64 * (ch % 2)
                        mm = pe.matmul(psum[c][:, t * P + k:t * P + k + 64], state[:, ch - 1, c, :],
                                       ar[:, c, t, 1, k:k + 64], start=False, stop=True, skip_group_check=True)
                return mm

            for ch in range(4):
                t, rows_ = ch // 2, slice(64 * (ch % 2), 64 * (ch % 2) + 64)
                if ch % 2 == 0:
                    pe.wait_ge(S["pav_done"], t + 1)
                    for h in range(NH1):
                        mm = pe.matmul(psum[4 + t][:, h * 64:(h + 1) * 64], inv[:, prob(t, h), :],
                                       pav[:, t, h * 64:(h + 1) * 64], start=(h == 0), stop=True,
                                       skip_group_check=True)
                if ch > 0:
                    pe.wait_ge(S["mat_done"], t + 1)
                    pe.wait_ge(S["st_done"], ch)
                    for pr in range(3):
                        at = slice(pr * P, (pr + 1) * P)
                        mm = pe.matmul(psum[4 + t][rows_, at], mat_[:, t, pr * P + 64 * (ch % 2):pr * P + 64 * (ch % 2) + 64],
                                       state[:, ch - 1, pr, :], start=False, stop=True, skip_group_check=True)
                mm.then_inc(S["sa_mm"], 1)
                if ch < 3:
                    bank = psum[6 + ch % 2]
                    for pr in range(3):
                        at = slice(pr * P, (pr + 1) * P)
                        pe.matmul(bank[:, at], tok[rows_, 2, t, at], tok[rows_, 3, t, at], start=(pr == 0), stop=False,
                                  skip_group_check=True)
                    pe.wait_ge(S["sa_done"], ch + 1)
                    for pr in range(3):
                        at = slice(pr * P, (pr + 1) * P)
                        mm = pe.matmul(bank[:, at], tok[rows_, 1, t, at], satok[rows_, t, at], start=False, stop=True,
                                       skip_group_check=True)
                    mm.then_inc(S["st_mm"], 1)
                if ch == 1:
                    values_of(0)
                    pe.wait_ge(S["conv_acc"], 1)
                    pe.wait_ge(S["mat_done"], 2)
                    for c in range(2):
                        mm = pe.matmul(psum[3][:, 0:SEQ], ones, mix[:, 6 + c, :], start=(c == 0), stop=(c == 1))
                    mm.then_inc(S["cl_mean"], 1)
                if ch == 2:
                    for c in range(3):
                        y_of(0, c)
                    pe.wait_ge(S["cl_sq"], 1)
                    for c in range(2):
                        mm = pe.matmul(psum[3][:, SEQ:2 * SEQ], ones, proj[:, CG + c, 1:], start=(c == 0), stop=(c == 1))
                    mm.then_inc(S["cl_var"], 1)
                    values_of(1)
            pe.wait_ge(S["sa_done"], 4)
            for c in range(3):
                y_of(1, c).then_inc(S["y_mm"], 1)
            pe.wait_ge(S["cl_root"], 1)
            for c in range(3):
                pe.wait_ge(S["y_copied"], c + 1)
                pe.matmul(psum[3 + c][:, 0:SEQ], pairs, ysb[:, c, :], start=True, stop=True).then_inc(S["gn_mean"], 1)
            pe.wait_ge(S["gn_sq"], 3)
            sum_heads(pe, 6, 0, ysq).then_inc(S["gn_var"], 1)

            def ready(k):
                if k == 1:
                    pe.wait_ge(S["gn_inv"], 1)
                    spread_heads(pe, 6, (1, 2), gninv).then_inc(S["gn_spread"], 1)
                pe.wait_ge(S["mix_low"], (1, 1, 2, 4)[k])

            for k in range(4):
                pe_out(pe, uses, k, ready, OUT_SLOTS, OUT_PAIRS)
            uses.each(OUT_SLOTS)

        def act_mixer(act, uses, link):
            act.wait_ge(S["proj_ready"], 12)
            act.activation(proj[:, CG:CG + 2, 1:], proj[:, CG:CG + 2, 1:], ACT.Sigmoid).then_inc(S["conv_sig"], 1)
            act.wait_ge(S["shifted"], 1)
            act.activation(lact[64:128, :], sh[64:128, LORA, :], ACT.Sigmoid).then_inc(S["lora_acts"], 1)
            act.activation(lact[0:32, :], sh[0:32, LORA, :], ACT.Tanh).then_inc(S["lora_acts"], 1)
            act.wait_ge(S["shifted"], 4)
            for c in range(3):
                ins = act.activation(tmp[:, c, :], sh[:, K + c, :], ACT.Square, scale=col("rwkv_k_k", c))
            ins.then_inc(S["kk_sq"], 1)
            act.activation(qsq, proj[:, AQ:AQ + 6, 1:], ACT.Square).then_inc(S["qk_sq"], 1)
            act.wait_ge(S["lora_mm"], 2)
            for c in range(3):
                b, cols_ = bank_pair(c)
                act.activation(ld[:, c, :], psum[b][:, cols_], ACT.Sigmoid, bias=col("rwkv_w0", c))\
                   .then_inc(S["decay_sig"], 1)
                act.activation(iclr[:, c, :], psum[2 + b][:, cols_], ACT.Sigmoid, bias=col("rwkv_a0", c))\
                   .then_inc(S["iclr_sig"], 1)
            act.wait_ge(S["kk_sum"], 1)
            act.activation(kkinv, psum[6][0:6, 0:SEQ], ACT.Sqrt, bias=eps["kk"][0:6, :]).then_inc(S["kk_root"], 1)
            act.wait_ge(S["qk_sum"], 1)
            act.activation(qkinv, psum[7][0:12, 0:SEQ], ACT.Sqrt, bias=eps["norm"][0:12, :], scale=1.0 / 64)\
               .then_inc(S["qk_root"], 1)
            act.wait_ge(S["lora_mm"], 3)
            for v, at in three(4):
                act.activation(gate[:, at, :], v, ACT.Copy).then_inc(S["gate_copied"], 1)
            act.wait_ge(S["cum_ready"], 2)
            rate = float(np.exp(-0.5))
            act.activation(ec, cum, ACT.Exp, scale=-rate).then_inc(S["exps_done"], 1)
            act.activation(en, cum, ACT.Exp, scale=rate).then_inc(S["exps_done"], 1)
            act.activation(ecx, ld, ACT.Exp, scale=-rate).then_inc(S["exps_done"], 1)
            for n in range(0, 10, 2):
                w, t = TOK[n]
                act.wait_ge(S["tok_mm"], n + 1)
                dst = tok[:, w, t, :] if w < 4 else avtok[:, t, 0:384]
                act.activation(dst, psum[TOK_BANK[n]][:, 0:384], ACT.Copy).then_inc(S["tok_copied_a"], 1)
            act_attention(act, NH1, logit, probT, BANKS1, 3)
            for step, b, kind, n, dst, *_ in CHAIN:
                if kind == "copy":
                    act.wait_ge(S["copy_mm"], n + 1)
                    act.activation(chain[dst][:, 4 * b:4 * b + 4, :],
                                   psum[n % 4][:, :].rearrange("p (a b) -> p a b", a=4), ACT.Copy)\
                       .then_inc(S["copy_done"], 1)
            for t in range(NT):
                act.wait_ge(S["pav_mm"], t + 1)
                act.activation(pav[:, t, :], psum[t][:, 0:384], ACT.Copy).then_inc(S["pav_done"], 1)
            for t in range(NT):
                act.wait_ge(S["mat_mm"], t + 1)
                act.activation(mat_[:, t, :], psum[2 + t][:, 0:384], ACT.Copy).then_inc(S["mat_done"], 1)
            for ch in range(4):
                t, rows_ = ch // 2, slice(64 * (ch % 2), 64 * (ch % 2) + 64)
                act.wait_ge(S["sa_mm"], ch + 1)
                act.activation(satok[rows_, t, :], psum[4 + t][rows_, 0:384], ACT.Copy).then_inc(S["sa_done"], 1)
                if ch == 3:
                    act.wait_ge(S["cl_var"], 1)
                    act.activation(proj[:, CG, 1:], psum[3][:, SEQ:], ACT.Sqrt, bias=eps["ln"], scale=1.0 / 256)\
                       .then_inc(S["cl_root"], 1)
            for c in range(3):
                act.wait_ge(S["y_mm"], c + 1)
                act.activation(ysb[:, c, :], psum[c][:, 0:SEQ], ACT.Copy).then_inc(S["y_copied"], 1)
            act.wait_ge(S["cl_ready"], 1)
            for c in range(2):
                act.activation(mix[:, 6 + c, :], mix[:, 6 + c, :], ACT.Silu, bias=col("conv_ln_b", c),
                               scale=col("conv_ln_w", c)).then_inc(S["mixc_ready"], 1)
            act.wait_ge(S["mixc_ready"], 2)
            act_mixed(act, 3, KC)
            act_high(act, uses, OUT_SLOTS[0])
            act.wait_ge(S["gn_var"], 1)
            act.activation(gninv, psum[0][0:6, 0:SEQ], ACT.Sqrt, bias=eps["gn"][0:6, :], scale=1.0 / 64)\
               .then_inc(S["gn_root"], 1)
            act_high(act, uses, OUT_SLOTS[1])
            for i, c in enumerate((2, 1, 0)):
                act.wait_ge(S["mixr_ready"], i + 1)
                act_mixed(act, c, c + 1)
            act_high(act, uses, OUT_SLOTS[2])
            act_high(act, uses, OUT_SLOTS[3], 0, 1)
            uses.each(OUT_SLOTS)

        def dve_mixer(dve, uses, link):
            mult, add, sub = ALU.mult, ALU.add, ALU.subtract
            dve.wait_ge(consts_in, 48)
            dve.wait_ge(S["proj_ready"], 12)
            for lo, hi in ((LORA, LORA + 1), (K, K + 3), (R, R + 3), (V, V + 3)):
                link(dve.tensor_tensor(sh[:, lo:hi, :], proj[:, lo:hi, 0:SEQ], proj[:, lo:hi, 1:], sub))
                for c in range(lo, hi):
                    dve.scalar_tensor_tensor(sh[:, c, :], sh[:, c, :], col("shift_mu", c), proj[:, c, 1:], mult, add)\
                       .then_inc(S["shifted"], 1)
            dve.wait_ge(S["shifted"], 10)
            for c in range(3):
                ins = dve.tensor_scalar(kk[:, c, :], sh[:, K + c, :], col("rwkv_k_k", c), None, mult)
            dve.wait_ge(S["decay_sig"], 3)
            for c in range(3):
                ins = dve.tensor_tensor_scan(cum[:, c, :], const("scan"), ld[:, c, :], 0.0, mult, add)
            ins.then_inc(S["cum_ready"], 1)
            dve.wait_ge(S["cum_ready"], 1)
            dve.tensor_tensor(ld, cum, ld, sub).then_inc(S["cum_ready"], 1)
            dve.wait_ge(S["kk_root"], 1)
            dve.reciprocal(kkinv, kkinv).then_inc(S["kk_inv"], 1)
            dve.wait_ge(S["iclr_sig"], 3)
            for c in range(3):
                ins = dve.tensor_scalar(kmod[:, c, :], iclr[:, c, :], 1.0, col("rwkv_k_a", c), sub, mult)
            link(ins)
            link(dve.scalar_tensor_tensor(kmod, kmod, 1.0, sh[:, K:K + 3, :], add, mult))
            dve.wait_ge(S["qk_root"], 1)
            dve.reciprocal(qkinv, qkinv).then_inc(S["qk_inv"], 1)
            dve.wait_ge(S["kk_spread"], 1)
            for v, at in three(2):
                ins = dve.tensor_tensor(kk[:, at, :], kk[:, at, :], v, mult)
            link(ins)
            link(dve.tensor_tensor(iclr, kk, iclr, mult))
            dve.wait_ge(S["exps_done"], 3)
            v4 = lambda a_: a_.rearrange("p c (t k) -> p c t k", t=NT)
            dve.scalar_tensor_tensor(ar[:, :, :, 0, :], v4(kk), -1.0, v4(ecx), mult, mult)
            dve.tensor_tensor(ar[:, :, :, 1, :], v4(sh[:, R:R + 3, :]), v4(ec), mult)
            dve.tensor_tensor(bh, iclr, en, mult)
            dve.tensor_tensor(kh, kmod, en, mult).then_inc(S["rw_ready"], 1)
            for c in range(3):
                ins = dve.scalar_tensor_tensor(tmp[:, c, :], sh[:, R + c, :], col("rwkv_r_k", c), kmod[:, c, :],
                                               mult, mult)
            ins.then_inc(S["bonus_sq"], 1)
            dve.wait_ge(S["qk_spread"], 1)
            for c in range(6):
                ins = dve.scalar_tensor_tensor(proj[:, AQ + c, 1:], proj[:, AQ + c, 1:],
                                               col("attn_q_norm" if c < 3 else "attn_k_norm"),
                                               psum[(7, 0, 1)[c // 2]][:, (c % 2) * SEQ:(c % 2 + 1) * SEQ],
                                               mult, mult)
            ins.then_inc(S["qk_ready"], 1)
            for n in range(1, 10, 2):
                w, t = TOK[n]
                dve.wait_ge(S["tok_mm"], n + 1)
                dst = tok[:, w, t, :] if w < 4 else avtok[:, t, 0:384]
                dve.tensor_copy(dst, psum[TOK_BANK[n]][:, 0:384]).then_inc(S["tok_copied_d"], 1)
            dve.wait_ge(S["bonus_mm"], 1)
            for v, at in three(4):
                ins = dve.tensor_tensor(bonus[:, at, :], v, sh[:, V + at.start:V + at.stop, :], mult)
            ins.then_inc(S["bonus_ready"], 1)
            bias1, m4 = const("bias1"), const("mask4")
            blk = const("blk16").unsqueeze(1).broadcast_to([P, 4, P])
            attention = DveAttention(dve, lambda h: bias1[:, h * 256:(h + 1) * 256], logit, BANKS1, link)

            def mats_of(p):
                dve.wait_ge(S["mats_mm"], p + 1)
                dve.tensor_tensor(mats[:, p].rearrange("p a b -> p (a b)"), psum[p % 3][:, :], m4, mult)\
                   .then_inc(S["mats_ready"], 1)

            def within_blocks(b):
                dve.wait_ge(S["a_mm"], b + 1)
                dve.wait_ge(S["mats_ready"], 4 * b + 4)
                dve.tensor_tensor(chain["D"][:, 4 * b:4 * b + 4, :],
                                  psum[3][:, :].rearrange("p (a b) -> p a b", a=4), blk, mult)\
                   .then_inc(S["d_ready"], 1)
                dve.tensor_tensor(chain["DT"][:, 4 * b:4 * b + 4, :], mats[:, 4 * b:4 * b + 4, 0, :], blk, mult)\
                   .then_inc(S["dt_ready"], 1)

            attention.logits(0)
            for h in range(NH1):
                if h + 1 < NH1:
                    attention.logits(h + 1)
                mats_of(2 * h)
                attention.normalise(h)
                mats_of(2 * h + 1)
                if h % 2 == 0 and h:
                    within_blocks(h // 2 - 1)
            within_blocks(2)
            dve.wait_ge(S["dt_ready"], 3)
            dve.tensor_tensor(chain["INV"], chain["DT"], ident.unsqueeze(1).broadcast_to([P, 12, P]), add)\
               .then_inc(S["inv_seed"], 1)
            for step, b, kind, n, dst, _, _, _, before in CHAIN:
                if kind == "add":
                    dve.wait_ge(S["add_mm"], n + 1)
                    src = psum[4 + n % 4][:, :].rearrange("p (a b) -> p a b", a=4)
                    to = chain[dst][:, 4 * b:4 * b + 4, :]
                    if dst == "INV":
                        if before is None:
                            dve.wait_ge(S["inv_seed"], 1)
                        else:
                            dve.wait_ge(S["add_done"], before[1] + 1)
                        ins = dve.tensor_tensor(to, src, to, add)
                    else:
                        if before[0] == "copy":
                            dve.wait_ge(S["copy_done"], before[1] + 1)
                        blk = const("blk32" if dst == "D" else "blk64").unsqueeze(1).broadcast_to([P, 4, P])
                        ins = dve.tensor_tensor(to, src, blk, mult)
                    ins.then_inc(S["add_done"], 1)
            for c in range(3):
                ins = dve.scalar_tensor_tensor(bonus[:, c, :], bonus[:, c, :], col("rwkv_ln_b", c), gate[:, c, :],
                                               add, mult)
            link(ins)
            for c in range(3):
                ins = dve.tensor_scalar(gate[:, c, :], gate[:, c, :], col("rwkv_ln_w", c), None, mult)
            link(ins)
            for c in range(3):
                dve.wait_ge(S["add_done"], ADDS)
                end = ec[:, :, (c + 1) * CHUNK - 1:(c + 1) * CHUNK].broadcast_to([P, 3, P])
                dve.tensor_tensor(cend[:, c], end, pairs.unsqueeze(1).broadcast_to([P, 3, P]), mult)\
                   .then_inc(S["cend_ready"], 1)
            for ch in range(3):
                dve.wait_ge(S["st_mm"], ch + 1)
                src = psum[6 + ch % 2][:, 0:384].rearrange("p (a b) -> p a b", a=3)
                if ch == 0:
                    dve.wait_ge(S["cend_ready"], 3)
                    dve.tensor_tensor(state[:, 0], src, cend[:, 0], mult).then_inc(S["st_done"], 1)
                else:
                    link(dve.tensor_tensor(state[:, ch], src, state[:, ch - 1], add))
                    dve.tensor_tensor(state[:, ch], state[:, ch], cend[:, ch], mult).then_inc(S["st_done"], 1)
                dve.wait_ge(S["st_done"], ch + 1)
                if ch == 1:
                    dve.wait_ge(S["cl_mean"], 1)
                    for c in range(2):
                        ins = dve.scalar_tensor_tensor(mix[:, 6 + c, :], psum[3][:, 0:SEQ], -1.0 / 256,
                                                       mix[:, 6 + c, :], mult, add)
                    link(ins)
                    dve.tensor_tensor(proj[:, CG:CG + 2, 1:], mix[:, 6:8, :], mix[:, 6:8, :], mult)\
                       .then_inc(S["cl_sq"], 1)
            dve.wait_ge(S["cl_root"], 1)
            link(dve.reciprocal(proj[:, CG + 1, 1:], proj[:, CG, 1:]))
            for c in range(2):
                ins = dve.tensor_tensor(mix[:, 6 + c, :], mix[:, 6 + c, :], proj[:, CG + 1, 1:], mult)
            ins.then_inc(S["cl_ready"], 1)
            for c in range(3):
                dve.wait_ge(S["gn_mean"], c + 1)
                link(dve.scalar_tensor_tensor(ysb[:, c, :], psum[3 + c][:, 0:SEQ], -1.0 / 64, ysb[:, c, :], mult, add))
                dve.tensor_tensor(ysq[:, c, :], ysb[:, c, :], ysb[:, c, :], mult).then_inc(S["gn_sq"], 1)
            dve.wait_ge(S["mix_high"], 1)
            dve_mixed(dve, 3, KC)
            dve_low(dve, uses, OUT_SLOTS[0])
            dve.wait_ge(S["gn_sq"], 3)
            link(dve.tensor_tensor(ysb, ysb, gate, mult))
            dve.wait_ge(S["gn_root"], 1)
            dve.reciprocal(gninv, gninv).then_inc(S["gn_inv"], 1)
            dve_low(dve, uses, OUT_SLOTS[1])
            dve.wait_ge(S["gn_spread"], 1)
            for c in (2, 1, 0):
                b, cols_ = bank_pair(c)
                link(dve.tensor_tensor(ysb[:, c, :], ysb[:, c, :], psum[1 + b][:, cols_], mult))
                dve.tensor_tensor(mix[:, c, :], ysb[:, c, :], bonus[:, c, :], add).then_inc(S["mixr_ready"], 1)
            for i, c in enumerate((2, 1, 0)):
                dve.wait_ge(S["mix_high"], i + 2)
                dve_mixed(dve, c, c + 1)
            dve_low(dve, uses, OUT_SLOTS[2])
            dve_low(dve, uses, OUT_SLOTS[3])
            uses.each(OUT_SLOTS)

        def pool_mixer(pool, link):
            mult, add = ALU.mult, ALU.add
            z = proj[:, CU:CU + 2, 1:]
            pool.wait_ge(S["conv_sig"], 1)
            link(pool.tensor_tensor(z, z, proj[:, CG:CG + 2, 1:], mult))
            for c in range(2):
                ins = pool.tensor_scalar(mix[:, 6 + c, :], z[:, c, :], col("conv_dw_w", 2 * (CONV_W - 1) + c),
                                         col("conv_dw_b", c), mult, add)
            link(ins)
            part = proj[:, CG:CG + 2, 1:]
            for lag in range(1, CONV_W):
                for c in range(2):
                    ins = pool.tensor_scalar(part[:, c, lag:], z[:, c, 0:SEQ - lag],
                                             col("conv_dw_w", 2 * (CONV_W - 1 - lag) + c), None, mult)
                link(ins)
                ins = pool.tensor_tensor(mix[:, 6:8, lag:], mix[:, 6:8, lag:], part[:, :, lag:], add)
                if lag < CONV_W - 1:
                    link(ins)
            ins.then_inc(S["conv_acc"], 1)

        def dve_pick_gain(dve, l):
            dve.tensor_scalar(row_now[0:8, :], rows[0:8, bass.ds(l, 1), :].rearrange("p a b -> p (a b)"), 1.0, None,
                              ALU.mult).then_inc(S["gain_picked"], 1)
            dve.wait_ge(S["gain_psum"], 1)
            dve.tensor_copy(par[:, 0:8], psum[3][:, 0:8]).then_inc(S["gain_ready"], 1)
            dve.wait_ge(S["gain_ready"], 1)

        def dve_pick_rows(dve, l):
            dve.wait_ge(rows_in, 16 * N_ROW_DMAS)
            one = lambda a_: a_.rearrange("p a b -> p (a b)")
            dve.tensor_scalar(row_now[0:NROWS, :], one(rows[0:NROWS, bass.ds(l, 1), :]), 1.0, None, ALU.mult)\
               .then_inc(S["rows_picked"], 1)

        def dve_rows_turned(dve):
            dve.wait_ge(S["params_psum"], 1)
            dve.tensor_copy(par[:, 0:NROWS], psum[3][:, 0:NROWS]).then_inc(S["params_ready"], 1)
            dve.wait_ge(S["params_ready"], 1)

        ROW_SOURCES = [(ROWS[n], a[n].rearrange("l (r p) -> r l p", p=P)) for n in
                       ("norm_mix", "norm_ffn2", "shift_mu", "rwkv_w0", "rwkv_a0", "rwkv_k_k",
                        "rwkv_k_a", "rwkv_ln_w", "rwkv_ln_b", "conv_dw_b", "conv_ln_w", "conv_ln_b")]
        ROW_SOURCES += [(ROWS["rwkv_r_k"], a["rwkv_r_k"].rearrange("l (r h) p -> r l (h p)", h=2)),
                        (ROWS["conv_dw_w"], None)]
        LORAS = (("rwkv_w2", 0, 32), ("rwkv_a2", 32, 64), ("rwkv_g2", 64, 128))
        assert ROWS["norm_ffn1"] == 0
        N_ROW_DMAS = len(ROW_SOURCES) - 1 + DEPTH + 4

        def load_rows(eng):
            n = 0
            for at, src in ROW_SOURCES:
                if src is None:
                    for l in range(DEPTH):
                        eng.dma_start(rows[at:at + 2 * CONV_W, l, :],
                                      a["conv_dw_w"][l].rearrange("j (c p) -> (j c) p", p=P)).then_inc(rows_in, 16)
                        n += 1
                else:
                    eng.dma_start(rows[at:at + src.shape[0], :, :], src).then_inc(rows_in, 16)
                    n += 1
            for name in ("attn_q_norm", "attn_k_norm"):
                for half_ in range(2):
                    eng.dma_start(rows[ROWS[name]:ROWS[name] + 1, :, half_ * 64:half_ * 64 + 64],
                                  a[name].rearrange("(o l) k -> o l k", o=1)).then_inc(rows_in, 16)
                    n += 1
            assert n == N_ROW_DMAS

        def load_loras(eng, l):
            for name, lo, hi in LORAS:
                eng.dma_start(lora_w[lo:hi, :], a[name][bass.ds(l, 1)].rearrange("a k n -> (a k) n"))\
                   .then_inc(lora_in, 16)

        def layer_over(eng, l):
            eng.drain().then_inc(arrived, 1)
            eng.wait_ge(cleared, l + 1)
            eng.sem_inc(resumed, 1)

        N_SECOND = 6
        SECOND = DEPTH

        def act_second_loads(act):
            w3, b1_, cw, ps = a["ffn_conv_w_2"], a["ffn_conv_b_2"], a["conv_w_2"], a["pool_scale_2"]
            for dst, src in ((rows2[0:88, 0, :], w3[0, 0:2].rearrange("j (c p) -> (j c) p", p=P)),
                             (rows2[0:44, 1, :], w3[0, 2].rearrange("(c p) -> c p", p=P)),
                             (rows2[44:88, 1, :], b1_[0].rearrange("(c p) -> c p", p=P)),
                             (rows2[88:94, 1, :], cw[0].rearrange("j (c p) -> (j c) p", p=P)),
                             (rows2[94:96, 1, :], ps[0].rearrange("(c p) -> c p", p=P)),
                             (tab[0:NH2, 32:64], a["rel_bias_2"])):
                act.dma_start(dst, src).then_inc(second_in, 16)

        def act_wpool_load(act):
            act.wait_ge(S["pool_link"], 1)
            for g in range(4):
                lo = 64 * (g % 2)
                act.dma_start(wpool[lo:lo + 64, g // 2, lo:lo + 64], a["w_pool_2"][0, g]).then_inc(wpool_in, 16)

        def load_ln(eng, g, b):
            for i, n in enumerate((g, b)):
                eng.dma_start(ln_gb[:, i, :], a[n].broadcast_to([P, D])).then_inc(x_in, 16)

        def pe_second(pe, uses):
            pe.wait_ge(second_in, 16 * N_SECOND * DEPTH)
            pe.transpose(psum[0][:, 0:88], rows2[0:88, 0, :], ident[0:88, 0:88])
            pe.transpose(psum[0][:, 128:128 + B_ROWS], rows2[0:B_ROWS, 1, :], ident[0:B_ROWS, 0:B_ROWS])
            pe.transpose(psum[0][0:32, 256:256 + NH2], tab[0:NH2, 32:64], ident[0:NH2, 0:NH2])\
              .then_inc(S["params_psum"], 1)
            pe_turn(pe, 0, x, None)
            pe.wait_ge(S["params_ready"], 1)
            pe.wait_ge(S["pool_link"], 2)
            pe.matmul(psum[1][0:NH2, 0:384], tab[0:33, 0:NH2], hot[:, :], start=True, stop=True)\
              .then_inc(S["biasrow_mm"], 1)
            pe.wait_ge(S["spread_ready"], 1)
            pe_proj(pe, uses, 5, 0)
            pe.wait_ge(S["proj_ready"], 10)
            for t in range(NT):
                for c in range(4):
                    mm = pe.transpose(psum[6 + t][:, c * P:(c + 1) * P], proj[:, V2 + c, 1 + t * P:1 + (t + 1) * P],
                                      ident)
                mm.then_inc(S["tok_mm"], 1)
            pe.wait_ge(S["tok_copied_a"], 2)
            attention = PeAttention(pe, Q2, K2, avtok2, logit2, probT2, BANKS2)
            attention.score(0)
            attention.score(1)
            def ready(k):
                pe.wait_ge(S["mix_low"], k + 1)

            beside = {4: (0, 0), 5: (0, 1), 6: (1, 0), 7: (1, 1)}
            for h in range(NH2):
                if h + 2 < NH2:
                    attention.score(h + 2)
                attention.turn(h)
                if h:
                    attention.value(h - 1)
                if h in beside:
                    k, j = beside[h]
                    pe_out(pe, uses, k, ready, OUT2_SLOTS, OUT2_PAIRS, (j,))
            attention.value(NH2 - 1)
            pe.wait_ge(S["pool_ready"], 1)
            pe.wait_ge(wpool_in, 16 * 4)
            for c in range(2):
                mm = pe.matmul(psum[c][:, 0:SEQ], wpool[:, c, :], pl[:, 0, c, :], start=True, stop=True)
            mm.then_inc(S["pool_mm"], 1)
            for k in (2, 3):
                pe_out(pe, uses, k, ready, OUT2_SLOTS, OUT2_PAIRS)
            uses.each(OUT2_SLOTS)
            pe_turn(pe, 1, x, S["normed"], count=0)
            pe_ffn(pe, uses, 0, 1)

        def act_second(act, uses):
            act_ahead(act, uses, PROJ_SLOTS[:1])
            act_turned(act, 0, None)
            act.wait_ge(S["biasrow_mm"], 1)
            act.activation(spread, psum[1][0:NH2, 0:384], ACT.Copy).then_inc(S["spread_ready"], 1)
            act.wait_ge(S["spread_ready"], 1)
            act.dma_start(scratch.ap().rearrange("p h x -> h p x"), spread.unsqueeze(1).broadcast_to([NH2, P, 384]))\
               .then_inc(spread_out, 16)
            act_ahead(act, uses, PROJ_SLOTS[1:2])
            act_wpool_load(act)
            load_ln(act, "ln1_g_2", "ln1_b_2")
            act_proj(act, uses, 5)
            act_high(act, uses, OUT2_SLOTS[0])
            for t in range(NT):
                act.wait_ge(S["tok_mm"], t + 1)
                act.activation(avtok2[:, t, :], psum[6 + t][:, :], ACT.Copy).then_inc(S["tok_copied_a"], 1)
            act_high(act, uses, OUT2_SLOTS[1])

            def beside(h):
                if h == 3:
                    act.wait_ge(S["mixc_ready"], 1)
                    act_mixed(act, 4, 6)
                if h == 4:
                    act.wait_ge(S["mixa_ready"], 2)
                    act_mixed(act, 0, 2)
                if h == 6:
                    act_high(act, uses, OUT2_SLOTS[2], 0, 1)

            act_attention(act, NH2, logit2, probT2, BANKS2, 0, beside)
            act.wait_ge(S["mixa_ready"], 4)
            act_mixed(act, 2, 4)
            act.wait_ge(S["pool_mm"], 1)
            for c in range(2):
                ins = act.activation(mix[:, 6 + c, :], psum[c][:, 0:SEQ], ACT.Copy, scale=par2c[:, 6 + c:7 + c])
            ins.then_inc(S["mixr_ready"], 1)
            act.wait_ge(S["mixr_ready"], 1)
            act_mixed(act, 6, KC)
            act_high(act, uses, OUT2_SLOTS[3])
            uses.each(OUT2_SLOTS)
            act_ahead(act, uses)
            act_ln(act, 0)
            act.wait_ge(S["normed"], NT)
            load_ln(act, "ln2_g_2", "ln2_b_2")
            act_turned(act, 1, None)

            def group(g, par_, more):
                if not final(g):
                    act_high(act, uses, f"gate{1 - par_}", more + par_, g + 1)
                    act_high(act, uses, f"up{1 - par_}", more + par_, g + 1)
                products_done(act, uses, "up", g)
                act.wait_ge(S["taps_picked"], g + 1)
                if later(g):
                    act.wait_ge(S["ff_ready"], g - 1)
                for q, bank in enumerate((psum[2 + par_], psum[par_])):
                    for j in range(2):
                        at = slice(j * SEQ, (j + 1) * SEQ)
                        ins = act.activation(taps[:, par_, q, at], bank[:, at], ACT.Identity,
                                             bias=tap_now[:, par_, 3, q, j:j + 1],
                                             scale=tap_now[:, par_, 2, q, j:j + 1])
                ins.then_inc(S["taps_act"], 1)
                act.wait_ge(S["taps_done"], g + 1)
                act.activation(silu[:, par_, :], taps[:, par_, 1, :], ACT.Silu).then_inc(S["silu_done"], 1)
                if final(g):
                    act_high(act, uses, f"down{par_}", more, g + 1, "gate")
                else:
                    act_high(act, uses, f"down{par_}", more, g)

            over_groups(act, group)
            uses.ffn()
            act_ln(act, 1)
            for t in range(NT):
                act.wait_ge(S["normed"], NT + t + 1)
                act.dma_start(out[0, t * P:(t + 1) * P, :], x[:, t, :]).then_inc(stored, 16)
            act.wait_ge(stored, 16 * NT)

        def act_ln(act, n):
            act.activation(unused, eps["ln"], ACT.Sqrt)
            for t in range(NT):
                act.wait_ge(S["stats_ready"], NT * n + t + 1)
                act.activation(rstd[:, t:t + 1], lnvar[:, t, 1:2], ACT.Sqrt, bias=eps["ln"])\
                   .then_inc(S["rms_root"], 1)
                act.wait_ge(S["ln_factors"], NT * n + t + 1)
                act.activation(x[:, t, :], x[:, t, :], ACT.Identity, bias=lnbias[:, t:t + 1],
                               scale=rstd[:, 4 + t:5 + t]).then_inc(S["ln_scaled"], 1)

        def dve_ln(dve, n, link):
            def residual(t):
                for h in range(2):
                    xs = x[:, t, h * 512:(h + 1) * 512]
                    ins = dve.scalar_tensor_tensor(xs, xs, ALPHA, psum[4 + 2 * t + h][:, :], ALU.mult, ALU.add)
                link(ins)

            def stats(t):
                for h in range(2):
                    ins = dve.bn_stats(lnstat[:, h, :], x[:, t, h * 512:(h + 1) * 512])
                link(ins)
                dve.bn_aggr(lnvar[:, t, :], lnstat).then_inc(S["stats_ready"], 1)
                dve.wait_ge(S["stats_ready"], NT * n + t + 1)

            def factors(t):
                dve.wait_ge(S["rms_root"], NT * n + t + 1)
                link(dve.reciprocal(rstd[:, 4 + t:5 + t], rstd[:, t:t + 1]))
                dve.scalar_tensor_tensor(lnbias[:, t:t + 1], lnvar[:, t, 0:1], -1.0, rstd[:, 4 + t:5 + t],
                                         ALU.mult, ALU.mult).then_inc(S["ln_factors"], 1)

            residual(0)
            stats(0)
            residual(1)
            factors(0)
            stats(1)
            factors(1)
            dve.wait_ge(x_in, 16 * (1 + 2 * n + 2))
            for t in range(NT):
                dve.wait_ge(S["ln_scaled"], NT * n + t + 1)
                link(dve.tensor_tensor(x[:, t, :], x[:, t, :], ln_gb[:, 0, :], ALU.mult))
                dve.tensor_tensor(x[:, t, :], x[:, t, :], ln_gb[:, 1, :], ALU.add).then_inc(S["normed"], 1)

        def dve_second(dve, uses, link):
            dve.wait_ge(S["params_psum"], 1)
            dve.tensor_copy(par2[:, 0:2, :].rearrange("p a b -> p (a b)"), psum[0][:, 0:88])
            dve.tensor_copy(par2[:, 2:4, :].rearrange("p a b -> p (a b)"), psum[0][:, 128:216])
            dve.tensor_copy(tab[0:32, 0:NH2], psum[0][0:32, 256:256 + NH2])
            dve.tensor_copy(par2c, psum[0][:, 216:224]).then_inc(S["params_ready"], 1)
            dve_ahead(dve, uses, PROJ_SLOTS[:1])
            dve_turned(dve, 0, None)
            dve_ahead(dve, uses, PROJ_SLOTS[1:2])
            dve_proj(dve, uses, 5, start2)
            dve.wait_ge(bias_in, 16)
            attention = DveAttention(dve, lambda h: bias2[:, h, :], logit2, BANKS2, link)
            dve_low(dve, uses, OUT2_SLOTS[0])
            attention.logits(0)
            for h in range(NH2):
                if h + 1 < NH2:
                    attention.logits(h + 1)
                attention.normalise(h)
                if h == 1:
                    dve_low(dve, uses, OUT2_SLOTS[1])
                if h == 3:
                    dve.wait_ge(S["mix_high"], 1)
                    dve_mixed(dve, 4, 6)
                if h == 5:
                    dve.wait_ge(S["mix_high"], 2)
                    dve_mixed(dve, 0, 2)
            dve_low(dve, uses, OUT2_SLOTS[2])
            dve.wait_ge(S["mix_high"], 3)
            dve_mixed(dve, 2, 4)
            dve.wait_ge(S["mix_high"], 4)
            dve_mixed(dve, 6, KC)
            dve_low(dve, uses, OUT2_SLOTS[3])
            uses.each(OUT2_SLOTS)
            dve_ahead(dve, uses, ("gate0",))
            products_done(dve, uses, "up", -1)
            dve_ln(dve, 0, link)
            dve_turned(dve, 1, None)
            dve_ahead(dve, uses, ("up0",))
            view = par2.rearrange("p k (q u) -> p k q u", q=2)

            def group(g, par_, more):
                if not final(g):
                    dve_low(dve, uses, f"gate{1 - par_}", more + par_)
                    dve_low(dve, uses, f"up{1 - par_}", more + par_)
                if later(g):
                    dve.wait_ge(S["taps_act"], g - 1)
                dve.tensor_scalar(tap_now[:, par_], view[:, :, :, bass.ds(g * 2, 2)], 1.0, None,
                                  ALU.mult).then_inc(S["taps_picked"], 1)
                dve.wait_ge(S["taps_picked"], g + 1)
                dve.wait_ge(S["taps_act"], g + 1)
                for lag in (1, 2):
                    for q, bank in enumerate((psum[2 + par_], psum[par_])):
                        for j in range(2):
                            to = taps[:, par_, q, j * SEQ + lag:(j + 1) * SEQ]
                            ins = dve.scalar_tensor_tensor(to, bank[:, j * SEQ:(j + 1) * SEQ - lag],
                                                           tap_now[:, par_, 2 - lag, q, j:j + 1], to,
                                                           ALU.mult, ALU.add)
                    ins.then_inc(S["lag_done" if lag == 1 else "taps_done"], 1)
                    if lag == 1:
                        dve.wait_ge(S["lag_done"], g + 1)
                dve.wait_ge(S["silu_done"], g + 1)
                dve_hidden(dve, taps[:, par_, 0, :], par_, g, 0, uses)
                dve_low(dve, uses, f"down{par_}", more, "gate" if final(g) else "down")

            over_groups(dve, group)
            uses.ffn()
            products_done(dve, uses, "gate", -1)
            dve_ln(dve, 1, link)

        def pool_second(pool, link):
            mult, add = ALU.mult, ALU.add
            link(pool.memset(wpool, 0.0))
            link(pool.memset(tab[32:33, 0:NH2], 1.0))
            pool.wait_ge(S["proj_ready"], 10)
            pool.wait_ge(S["params_ready"], 1)
            link(pool.tensor_tensor(cz, proj[:, CC2:CC2 + 2, 1:], proj[:, CX2:CX2 + 2, 1:], mult))
            for c in range(2):
                ins = pool.tensor_scalar(mix[:, 4 + c, :], cz[:, c, :], par2c[:, 4 + c:5 + c], None, mult)
            link(ins)
            part = proj[:, CC2:CC2 + 2, 1:]
            for lag in (1, 2):
                for c in range(2):
                    i = 2 * (2 - lag) + c
                    ins = pool.tensor_scalar(part[:, c, lag:], cz[:, c, 0:SEQ - lag], par2c[:, i:i + 1], None, mult)
                link(ins)
                link(pool.tensor_tensor(mix[:, 4:6, lag:], mix[:, 4:6, lag:], part[:, :, lag:], add))
            pool.tensor_tensor(mix[:, 4:6, :], mix[:, 4:6, :], proj[:, CB2:CB2 + 2, 1:], mult)\
                .then_inc(S["mixc_ready"], 1)
            p_ = proj[:, PI2:PI2 + 2, 1:]
            u, v = pl[:, 0], pl[:, 1]
            link(pool.tensor_copy(u, p_))
            link(pool.tensor_tensor(u[:, :, 1:], u[:, :, 1:], p_[:, :, 0:SEQ - 1], add))
            link(pool.tensor_copy(v, u))
            link(pool.tensor_tensor(v[64:P, 0, 2:], v[64:P, 0, 2:], u[64:P, 0, 0:SEQ - 2], add))
            link(pool.tensor_tensor(v[:, 1, 2:], v[:, 1, 2:], u[:, 1, 0:SEQ - 2], add))
            link(pool.tensor_copy(u, v))
            link(pool.tensor_tensor(u[:, 1, 4:], u[:, 1, 4:], v[:, 1, 0:SEQ - 4], add))
            link(pool.tensor_copy(v, u))
            link(pool.tensor_tensor(v[64:P, 1, 8:], v[64:P, 1, 8:], u[64:P, 1, 0:SEQ - 8], add))
            link(pool.tensor_tensor(v, v, const("poolw").rearrange("p (a b) -> p a b", a=2), mult))
            pool.tensor_tensor(u, v, p_, ALU.subtract).then_inc(S["pool_ready"], 1)

        @block.sync
        def _(sp):
            sp.dma_start(x[:, :, :], a["x"][0].rearrange("(t p) n -> p t n", p=P)).then_inc(x_in, 16)
            with sp.Fori(0, DEPTH) as l:
                uses = Uses(l, PER_LAYER)
                sp_ffn(sp, uses, l, a["ffn1_w_gate"], 0, a["ffn1_w_up"], 0, a["ffn1_w_down"])
                load_loras(sp, l)
                sp_proj(sp, uses, l, a["w_in"], 6, start1)
                sp_out(sp, uses, l, a["w_out"], OUT_SLOTS, OUT_PAIRS)
                sp_ffn(sp, uses, l, a["ffn2_w_gate"], 0, a["ffn2_w_up"], 0, a["ffn2_w_down"])
            uses = Uses(SECOND, PER_LAYER)
            sp_proj(sp, uses, 0, a["w_in_2"], 5, start2)
            sp.wait_ge(spread_out, 16)
            pitch = NH2 * 384
            sp.dma_start(bias2, bass.AP(scratch, P - 1, [[pitch - 1, P], [384, NH2], [1, 2 * P]])).then_inc(bias_in, 16)
            sp_out(sp, uses, 0, a["w_out_2"], OUT2_SLOTS, OUT2_PAIRS)
            sp_ffn(sp, uses, 0, a["w_up_2"], DFF, a["w_up_2"], 0, a["w_down_2"])

        @block.gpsimd
        def _(pool):
            for n, v in (("norm", NORM_EPS), ("gn", GN_EPS), ("ln", LN_EPS), ("kk", 1e-12)):
                pool.memset(eps[n], v)
            pool.memset(proj[:, :, 0:1], 0.0).then_inc(setup_done, 1)
            load_rows(pool)
            with pool.Fori(0, DEPTH) as l:
                pool.wait_ge(S["params_ready"], 1)
                pool_mixer(pool, Chain(pool, S["pool_link"]))
                pool.drain()
                pool.wait_ge(arrived, l * 3 + 3)
                pool.sem_inc(over, 1)
                pool.sem_clear(layer_sems)
                pool.sem_inc(cleared, 1)
            pool_second(pool, Chain(pool, S["pool_link"]))

        @block.scalar
        def _(act):
            act.dma_start(cst[:, 0:P], a["consts"][:, 0:P]).then_inc(ident_in, 16)
            act.dma_start(rows[0:8, :, :], a["norm_ffn1"].rearrange("l (r p) -> r l p", p=P)).then_inc(gain_in, 16)
            act.dma_start(cst[:, P:], a["consts"][:, P:]).then_inc(consts_in, 16)
            act.dma_start(hot[:, :], a["hot"]).then_inc(consts_in, 16)
            act.dma_start(heads[:, :], a["heads"]).then_inc(consts_in, 16)
            act.wait_ge(setup_done, 1)
            with act.Fori(0, DEPTH) as l:
                uses = Uses(l, PER_LAYER)
                act_norm(act, 0)
                act_ahead(act, uses, ("gate0",))
                act.wait_ge(S["gain_ready"], 1)
                act_turned(act, 0, "norm_ffn1")
                act_ahead(act, uses, ("up0",))
                act_ffn(act, uses, 0)
                act_ahead(act, uses, PROJ_SLOTS[:2])
                act_norm(act, 1)
                act.wait_ge(S["params_ready"], 1)
                act_turned(act, 1, "norm_mix")
                act_proj(act, uses, 6)
                act_mixer(act, uses, Chain(act, S["act_link"]))
                act_second_loads(act)
                act_ahead(act, uses)
                act_norm(act, 2)
                act_turned(act, 2, "norm_ffn2")
                act_ffn(act, uses, 1)
                act.wait_ge(second_in, l * (16 * N_SECOND) + 16 * N_SECOND)
                act.sem_inc(loads_seen, 1)
                layer_over(act, l)
            act_second(act, Uses(SECOND, PER_LAYER))

        @block.vector
        def _(dve):
            for n in SLOTS:
                dve.sem_inc(split[n], 1)
            dve.wait_ge(setup_done, 1)
            dve.wait_ge(gain_in, 16)
            with dve.Fori(0, DEPTH) as l:
                uses = Uses(l, PER_LAYER)
                link = Chain(dve, S["dve_link"])
                dve_norm(dve, 0, link)
                dve_pick_gain(dve, l)
                dve_ahead(dve, uses, ("gate0",))
                dve_turned(dve, 0, "norm_ffn1")
                dve_ahead(dve, uses, ("up0",))
                dve_ffn(dve, uses, 0)
                dve_pick_rows(dve, l)
                dve_ahead(dve, uses, PROJ_SLOTS[:1])
                dve_residual(dve, uses, 0.5, "gate")
                dve_rows_turned(dve)
                dve_ahead(dve, uses, PROJ_SLOTS[1:2])
                dve_norm(dve, 1, link)
                dve_turned(dve, 1, "norm_mix")
                dve_proj(dve, uses, 6, start1)
                dve.wait_ge(lora_in, l * 48 + 48)
                dve_mixer(dve, uses, link)
                dve_ahead(dve, uses, ("gate0",))
                dve_residual(dve, uses, 1.0, "down")
                dve_ahead(dve, uses, ("up0",))
                dve_norm(dve, 2, link)
                dve_turned(dve, 2, "norm_ffn2")
                dve_ffn(dve, uses, 1)
                dve_residual(dve, uses, 0.5, "gate")
                layer_over(dve, l)
            dve_second(dve, Uses(SECOND, PER_LAYER), Chain(dve, S["dve_link"]))

        @block.tensor
        def _(pe):
            for n in KINDS:
                pe.sem_inc(used[n], 1)
            pe.wait_ge(ident_in, 16)
            with pe.Fori(0, DEPTH) as l:
                uses = Uses(l, PER_LAYER)
                pe.wait_ge(S["gain_picked"], 1)
                pe.transpose(psum[3][:, 0:8], row_now[0:8, :], ident[0:8, 0:8]).then_inc(S["gain_psum"], 1)
                pe_turn(pe, 0, hN, S["normed"])
                pe_ffn(pe, uses, 0, 0)
                pe.wait_ge(S["rows_picked"], 1)
                pe.transpose(psum[3][:, 0:NROWS], row_now[0:NROWS, :], ident[0:NROWS, 0:NROWS])\
                  .then_inc(S["params_psum"], 1)
                pe_turn(pe, 1, hN, S["normed"])
                pe_proj(pe, uses, 6, 1)
                pe_mixer(pe, uses)
                pe_turn(pe, 2, hN, S["normed"])
                pe_ffn(pe, uses, 1, 2)
                layer_over(pe, l)
            pe_second(pe, Uses(SECOND, PER_LAYER))


INS = ["x", "norm_ffn1", "ffn1_w_gate", "ffn1_w_up", "ffn1_w_down", "norm_mix", "w_in", "shift_mu", "rwkv_w0",
       "rwkv_w2", "rwkv_a0", "rwkv_a2", "rwkv_g2", "rwkv_k_k", "rwkv_k_a", "rwkv_r_k", "rwkv_ln_w", "rwkv_ln_b",
       "attn_q_norm", "attn_k_norm", "conv_dw_w", "conv_dw_b", "conv_ln_w", "conv_ln_b", "w_out", "norm_ffn2",
       "ffn2_w_gate", "ffn2_w_up", "ffn2_w_down", "w_in_2", "conv_w_2", "w_pool_2", "pool_scale_2", "w_out_2",
       "ln1_g_2", "ln1_b_2", "w_up_2", "ffn_conv_w_2", "ffn_conv_b_2", "w_down_2", "ln2_g_2", "ln2_b_2",
       "rel_bias_2"]


def kernel(**inputs):
    import concourse.bacc as bacc
    from concourse.bass_utils import run_bass_kernel_spmd

    nc = bacc.Bacc("TRN2", target_bir_lowering=False, num_devices=1)
    packed, _, hot, heads = constants()
    arrays = {f"in_{n}_dram": np.ascontiguousarray(inputs[n]) for n in INS}
    arrays["in_consts_dram"] = packed
    arrays["in_hot_dram"] = hot
    arrays["in_heads_dram"] = heads
    args = {n: nc.dram_tensor(f"in_{n}_dram", arrays[f"in_{n}_dram"].shape, F32, kind="ExternalInput").ap()
            for n in INS + ["consts", "hot", "heads"]}
    out = nc.dram_tensor("out_0_dram", (1, SEQ, D), F32, kind="ExternalOutput").ap()
    build(nc, args, out)
    r = run_bass_kernel_spmd(nc, [arrays], core_ids=[0])
    return r.results[0]["out_0_dram"]
```
